# Optimizing a Trainium2 kernel written in Bass

```python
import math
import jax, jax.numpy as jnp
from jax import lax
import numpy as np

D_MODEL = 1024
BATCH = 1
SEQ = 512
DEPTH = 2

N_A = DEPTH // 2
N_B = DEPTH - N_A
RET_HEADS = 4
RET_QK_DIM = D_MODEL // RET_HEADS
RET_V_DIM = 2 * RET_QK_DIM
RET_V_TOTAL = RET_HEADS * RET_V_DIM
RET_CHUNK = 128
A_IN_WIDTH = 2 * D_MODEL + 2 * RET_V_TOTAL
SWA_HEAD_DIM = 64
SWA_Q_HEADS = D_MODEL // SWA_HEAD_DIM
SWA_KV_HEADS = SWA_Q_HEADS // 8
SWA_GROUP = SWA_Q_HEADS // SWA_KV_HEADS
SWA_Q_WIDTH = SWA_Q_HEADS * SWA_HEAD_DIM
KV_WIDTH = SWA_KV_HEADS * SWA_HEAD_DIM
WINDOW = 128
BLOCK = 128
REL_BUCKETS = 32
REL_MAX_DIST = 128
EPS = 1e-6


def rms(x):
    xf = x.astype(jnp.float32)
    return (xf * lax.rsqrt(jnp.mean(xf * xf, axis=-1, keepdims=True) + EPS)).astype(x.dtype)

def rmsnorm(x, g):
    return (rms(x) * g).astype(x.dtype)

def xpos_tables(seq, dim):
    angle = 1.0 / (10000.0 ** jnp.linspace(0.0, 1.0, dim // 2, dtype=jnp.float32))
    angle = jnp.repeat(angle, 2)
    pos = jnp.arange(seq, dtype=jnp.float32)[:, None]
    return jnp.sin(pos * angle), jnp.cos(pos * angle)

def theta_shift(x, sin, cos):
    x1 = x[..., ::2]
    x2 = x[..., 1::2]
    rot = jnp.stack([-x2, x1], axis=-1).reshape(x.shape)
    return x * cos[:, None, :].astype(x.dtype) + rot * sin[:, None, :].astype(x.dtype)

def retention(q, k, v):
    b, s, h, dk = q.shape
    dv = v.shape[-1]
    c = RET_CHUNK
    n = s // c
    dt = q.dtype
    log_gamma = jnp.log(1.0 - 2.0 ** (-5.0 - jnp.arange(h, dtype=jnp.float32)))
    idx = jnp.arange(c, dtype=jnp.float32)
    diff = idx[:, None] - idx[None, :]
    intra_decay = jnp.where(diff[None] >= 0,
                            jnp.exp(jnp.maximum(diff, 0.0)[None] * log_gamma[:, None, None]),
                            0.0).astype(dt)
    q_decay = jnp.exp((idx + 1.0)[:, None] * log_gamma[None, :]).astype(dt)
    k_decay = jnp.exp((c - 1.0 - idx)[:, None] * log_gamma[None, :]).astype(dt)
    chunk_decay = jnp.exp(c * log_gamma).astype(dt)
    k = k * jnp.asarray(dk ** -0.5, dt)

    def to_chunks(t):
        return t.reshape(b, n, c, h, t.shape[-1]).transpose(1, 0, 2, 3, 4)

    def step(state, inp):
        qc, kc, vc = inp
        scores = jnp.einsum('bihd,bjhd->bhij', qc, kc) * intra_decay[None]
        intra = jnp.einsum('bhij,bjhe->bihe', scores, vc)
        inter = jnp.einsum('bihd,bhde->bihe', qc, state) * q_decay[None, :, :, None]
        new_state = (state * chunk_decay[None, :, None, None]
                     + jnp.einsum('bjhd,bjhe->bhde', kc * k_decay[None, :, :, None], vc))
        return new_state, intra + inter

    state0 = jnp.zeros((b, h, dk, dv), dt)
    _, out = lax.scan(step, state0, (to_chunks(q), to_chunks(k), to_chunks(v)))
    return out.transpose(1, 0, 2, 3, 4).reshape(b, s, h, dv)

def retention_layer(x, g_norm, w_in, w_out, sin, cos):
    b, s, _ = x.shape
    proj = rmsnorm(x, g_norm) @ w_in
    q, k, v, gate = jnp.split(proj, [D_MODEL, 2 * D_MODEL, 2 * D_MODEL + RET_V_TOTAL], axis=-1)
    q = theta_shift(q.reshape(b, s, RET_HEADS, RET_QK_DIM), sin, cos)
    k = theta_shift(k.reshape(b, s, RET_HEADS, RET_QK_DIM), sin, cos)
    v = v.reshape(b, s, RET_HEADS, RET_V_DIM)
    o = rms(retention(q, k, v))
    o = o.reshape(b, s, RET_V_TOTAL) * jax.nn.silu(gate)
    return x + o @ w_out

def shared_kv(x, g_norm, w_kv, g_k):
    b, s, _ = x.shape
    nb = s // BLOCK
    kv = rmsnorm(x, g_norm) @ w_kv
    k, v = jnp.split(kv, [KV_WIDTH], axis=-1)
    k = rmsnorm(k.reshape(b, s, SWA_KV_HEADS, SWA_HEAD_DIM), g_k)
    v = v.reshape(b, s, SWA_KV_HEADS, SWA_HEAD_DIM)

    def band(t):
        tb = t.reshape(b, nb, BLOCK, SWA_KV_HEADS, SWA_HEAD_DIM)
        prev = jnp.concatenate([jnp.zeros_like(tb[:, :1]), tb[:, :-1]], axis=1)
        return jnp.concatenate([prev, tb], axis=2)

    return band(k), band(v)

def t5_causal_bucket(dist):
    max_exact = REL_BUCKETS // 2
    dist_f = jnp.maximum(dist, 1).astype(jnp.float32)
    large = max_exact + (jnp.log(dist_f / max_exact) / math.log(REL_MAX_DIST / max_exact)
                         * (REL_BUCKETS - max_exact)).astype(jnp.int32)
    large = jnp.minimum(large, REL_BUCKETS - 1)
    return jnp.where(dist < max_exact, dist, large)

def band_bias_and_mask(rel_bias, nb):
    i = jnp.arange(BLOCK)[:, None]
    j = jnp.arange(2 * BLOCK)[None, :]
    dist = i + BLOCK - j
    bucket = t5_causal_bucket(jnp.maximum(dist, 0))
    bias = rel_bias.astype(jnp.float32)[bucket]
    bias = bias.transpose(2, 0, 1).reshape(SWA_KV_HEADS, SWA_GROUP, BLOCK, 2 * BLOCK)
    in_window = (dist >= 0) & (dist < WINDOW)
    key_pos = jnp.arange(nb)[:, None, None] * BLOCK - BLOCK + j[None]
    mask = in_window[None] & (key_pos >= 0)
    return bias, mask

def swa_layer(x, g_norm, w_in, g_q, sinks, w_out, k_band, v_band, bias, mask):
    b, s, _ = x.shape
    nb = s // BLOCK
    proj = rmsnorm(x, g_norm) @ w_in
    q, gate = jnp.split(proj, [SWA_Q_WIDTH], axis=-1)
    q = rmsnorm(q.reshape(b, nb, BLOCK, SWA_KV_HEADS, SWA_GROUP, SWA_HEAD_DIM), g_q)
    scores = jnp.einsum('bnqkgd,bnjkd->bnkgqj', q, k_band).astype(jnp.float32)
    scores = scores * (SWA_HEAD_DIM ** -0.5) + bias[None, None]
    scores = jnp.where(mask[None, :, None, None], scores, -jnp.inf)
    sink = sinks.astype(jnp.float32).reshape(1, 1, SWA_KV_HEADS, SWA_GROUP, 1, 1)
    m = jnp.maximum(jnp.max(scores, axis=-1, keepdims=True), sink)
    p = jnp.exp(scores - m)
    p = p / (jnp.sum(p, axis=-1, keepdims=True) + jnp.exp(sink - m))
    o = jnp.einsum('bnkgqj,bnjkd->bnqkgd', p.astype(v_band.dtype), v_band)
    o = o.reshape(b, s, SWA_Q_WIDTH) * jax.nn.silu(gate)
    return x + o @ w_out

def first_inputs(seed: int = 0) -> dict:
    key = jax.random.key(seed)
    ks = jax.random.split(key, 13)

    def nrm(k, shape, scale):
        return jax.random.normal(k, shape, jnp.float32) * scale

    return {
        "x": nrm(ks[0], (BATCH, SEQ, D_MODEL), 1.0),
        "a_norm_g": 1.0 + nrm(ks[1], (N_A, D_MODEL), 0.02),
        "a_w_in": nrm(ks[2], (N_A, D_MODEL, A_IN_WIDTH), D_MODEL ** -0.5),
        "a_w_out": nrm(ks[3], (N_A, RET_V_TOTAL, D_MODEL), RET_V_TOTAL ** -0.5),
        "kv_norm_g": 1.0 + nrm(ks[4], (D_MODEL,), 0.02),
        "w_kv": nrm(ks[5], (D_MODEL, 2 * KV_WIDTH), D_MODEL ** -0.5),
        "k_norm_g": 1.0 + nrm(ks[6], (SWA_HEAD_DIM,), 0.02),
        "rel_bias": nrm(ks[7], (REL_BUCKETS, SWA_Q_HEADS), 0.5),
        "b_norm_g": 1.0 + nrm(ks[8], (N_B, D_MODEL), 0.02),
        "b_w_in": nrm(ks[9], (N_B, D_MODEL, 2 * SWA_Q_WIDTH), D_MODEL ** -0.5),
        "b_q_norm_g": 1.0 + nrm(ks[10], (N_B, SWA_HEAD_DIM), 0.02),
        "b_sinks": nrm(ks[11], (N_B, SWA_Q_HEADS), 1.0),
        "b_w_out": nrm(ks[12], (N_B, SWA_Q_WIDTH, D_MODEL), SWA_Q_WIDTH ** -0.5),
    }

def first_block(x, a_norm_g, a_w_in, a_w_out, kv_norm_g, w_kv, k_norm_g, rel_bias,
              b_norm_g, b_w_in, b_q_norm_g, b_sinks, b_w_out):
    s = x.shape[1]
    sin, cos = xpos_tables(s, RET_QK_DIM)
    bias, mask = band_bias_and_mask(rel_bias, s // BLOCK)
    k_band = None
    v_band = None
    for layer in range(DEPTH):
        if layer < N_A:
            x = retention_layer(x, a_norm_g[layer], a_w_in[layer], a_w_out[layer], sin, cos)
        else:
            j = layer - N_A
            if j == 0:
                k_band, v_band = shared_kv(x, kv_norm_g, w_kv, k_norm_g)
            x = swa_layer(x, b_norm_g[j], b_w_in[j], b_q_norm_g[j], b_sinks[j], b_w_out[j],
                          k_band, v_band, bias, mask)
    return x


DEPTH_2 = 1

D_MIX = D_MODEL
MLA_HEADS = 4
MLA_NOPE = 128
MLA_ROPE = 64
MLA_QK = MLA_NOPE + MLA_ROPE
MLA_V = 128
MLA_Q_LORA = 384
MLA_KV_LORA = 256
DIFF_HEADS = 4
DIFF_DQK = 64
DIFF_DV = 2 * DIFF_DQK
IN_MLA = MLA_Q_LORA + MLA_KV_LORA + MLA_ROPE
IN_DIFF_Q = DIFF_HEADS * 2 * DIFF_DQK
IN_DIFF_V = DIFF_HEADS * DIFF_DV
IN_COLS = IN_MLA + 2 * IN_DIFF_Q + IN_DIFF_V
ROPE_THETA = 10000.0
Q_BLOCK = 128
RMS_EPS = 1e-6
PEER_HEADS = 8
PEER_NKEYS = 128
PEER_EXPERTS = PEER_NKEYS * PEER_NKEYS
PEER_DK_HALF = 128
PEER_TOPK = 16
PEER_CHUNK = 128
ADA_INIT = 0.2


def rms_norm(x, g):
    xf = x.astype(jnp.float32)
    y = xf * lax.rsqrt(jnp.mean(xf * xf, axis=-1, keepdims=True) + RMS_EPS)
    return (y * g.astype(jnp.float32)).astype(x.dtype)

def rope_tables(seq, dim):
    half = dim // 2
    inv = 1.0 / (ROPE_THETA ** (jnp.arange(half, dtype=jnp.float32) / half))
    ang = jnp.arange(seq, dtype=jnp.float32)[:, None] * inv[None, :]
    return jnp.cos(ang), jnp.sin(ang)

def apply_rope(x, cos, sin):
    half = x.shape[-1] // 2
    xf = x.astype(jnp.float32)
    x1, x2 = xf[..., :half], xf[..., half:]
    return jnp.concatenate([x1 * cos - x2 * sin, x2 * cos + x1 * sin], axis=-1).astype(x.dtype)

def causal_attention(qs, ks, coeffs, v, scale):
    B, H, S, dv = v.shape
    nb = S // Q_BLOCK
    qbs = tuple(q.reshape(B, H, nb, Q_BLOCK, q.shape[-1]).transpose(2, 0, 1, 3, 4) for q in qs)
    kpos = jnp.arange(S)

    def one_block(args):
        i, qb = args
        qpos = i * Q_BLOCK + jnp.arange(Q_BLOCK)
        mask = kpos[None, :] <= qpos[:, None]
        w = None
        for qi, ki, ci in zip(qb, ks, coeffs):
            s = jnp.einsum('bhqd,bhkd->bhqk', qi, ki).astype(jnp.float32) * scale
            p = jax.nn.softmax(jnp.where(mask, s, -jnp.inf), axis=-1)
            w = ci * p if w is None else w + ci * p
        return jnp.einsum('bhqk,bhkd->bhqd', w.astype(v.dtype), v)

    out = lax.map(one_block, (jnp.arange(nb), qbs))
    return out.transpose(1, 2, 0, 3, 4).reshape(B, H, S, dv)

def peer_ffn(h, w_q, sub_keys, u_tab, v_tab):
    T, D = h.shape
    hc = h.reshape(T // PEER_CHUNK, PEER_CHUNK, D)

    def one_chunk(hb):
        C = hb.shape[0]
        q = (hb @ w_q).reshape(C, PEER_HEADS, 2, PEER_DK_HALF)
        s = jnp.einsum('thpd,hpnd->thpn', q, sub_keys).astype(jnp.float32)
        sv, si = lax.top_k(s, PEER_TOPK)
        cand = sv[:, :, 0, :, None] + sv[:, :, 1, None, :]
        cidx = si[:, :, 0, :, None] * PEER_NKEYS + si[:, :, 1, None, :]
        cand = cand.reshape(C, PEER_HEADS, PEER_TOPK * PEER_TOPK)
        cidx = cidx.reshape(C, PEER_HEADS, PEER_TOPK * PEER_TOPK)
        fv, fpos = lax.top_k(cand, PEER_TOPK)
        eidx = jnp.take_along_axis(cidx, fpos, axis=-1).reshape(C, PEER_HEADS * PEER_TOPK)
        g = jax.nn.softmax(fv, axis=-1).reshape(C, PEER_HEADS * PEER_TOPK)
        u = u_tab[eidx]
        a = jax.nn.gelu(jnp.einsum('ted,td->te', u, hb).astype(jnp.float32), approximate=False)
        coef = (g * a).astype(hb.dtype)
        vv = v_tab[eidx]
        return jnp.einsum('te,ted->td', coef, vv)

    return lax.map(one_chunk, hc).reshape(T, D)

def second_inputs(seed: int = 0) -> dict:
    key = jax.random.key(seed)
    keys = iter(jax.random.split(key, 40))

    def nrm(shape, scale):
        return jax.random.normal(next(keys), shape, jnp.float32) * scale

    def gain(shape):
        return 1.0 + nrm(shape, 0.02)

    L = DEPTH_2
    return {
        'x': nrm((BATCH, SEQ, D_MODEL), 1.0),
        'c': nrm((BATCH, D_MODEL), 1.0),
        'ada_w': nrm((L, D_MODEL, 6 * D_MODEL), ADA_INIT * D_MODEL ** -0.5),
        'ada_b': nrm((L, 6 * D_MODEL), 0.02),
        'norm1_g': gain((L, D_MODEL)),
        'w_in': nrm((L, D_MODEL, IN_COLS), D_MODEL ** -0.5),
        'mla_q_lat_g': gain((L, MLA_Q_LORA)),
        'mla_w_q_up': nrm((L, MLA_Q_LORA, MLA_HEADS * MLA_QK), MLA_Q_LORA ** -0.5),
        'mla_kv_lat_g': gain((L, MLA_KV_LORA)),
        'mla_w_kv_up': nrm((L, MLA_KV_LORA, MLA_HEADS * (MLA_NOPE + MLA_V)), MLA_KV_LORA ** -0.5),
        'mla_q_g': gain((L, MLA_QK)),
        'mla_k_g': gain((L, MLA_QK)),
        'diff_q_g': gain((L, DIFF_DQK)),
        'diff_k_g': gain((L, DIFF_DQK)),
        'diff_lq1': nrm((L, DIFF_DQK), 0.1),
        'diff_lk1': nrm((L, DIFF_DQK), 0.1),
        'diff_lq2': nrm((L, DIFF_DQK), 0.1),
        'diff_lk2': nrm((L, DIFF_DQK), 0.1),
        'diff_subln_g': gain((L, DIFF_DV)),
        'w_out': nrm((L, D_MIX, D_MODEL), D_MIX ** -0.5),
        'norm2_g': gain((L, D_MODEL)),
        'peer_w_q': nrm((L, D_MODEL, PEER_HEADS * 2 * PEER_DK_HALF), D_MODEL ** -0.5),
        'peer_sub_keys': nrm((L, PEER_HEADS, 2, PEER_NKEYS, PEER_DK_HALF), PEER_DK_HALF ** -0.5),
        'peer_u': nrm((L, PEER_EXPERTS, D_MODEL), D_MODEL ** -0.5),
        'peer_v': nrm((L, PEER_EXPERTS, D_MODEL), PEER_HEADS ** -0.5),
    }

def second_block(x, c, ada_w, ada_b, norm1_g, w_in, mla_q_lat_g, mla_w_q_up, mla_kv_lat_g,
              mla_w_kv_up, mla_q_g, mla_k_g, diff_q_g, diff_k_g, diff_lq1, diff_lk1, diff_lq2,
              diff_lk2, diff_subln_g, w_out, norm2_g, peer_w_q, peer_sub_keys, peer_u, peer_v):
    B, S, D = x.shape
    cos_m, sin_m = rope_tables(S, MLA_ROPE)
    cos_d, sin_d = rope_tables(S, DIFF_DQK)

    for l in range(DEPTH_2):
        mod = jax.nn.silu(c) @ ada_w[l] + ada_b[l]
        sh1, sc1, g1, sh2, sc2, g2 = [m[:, None, :] for m in jnp.split(mod, 6, axis=-1)]

        h = rms_norm(x, norm1_g[l]) * (1.0 + sc1) + sh1
        proj = h @ w_in[l]
        o0 = MLA_Q_LORA
        o1 = o0 + MLA_KV_LORA
        o2 = o1 + MLA_ROPE
        o3 = o2 + IN_DIFF_Q
        o4 = o3 + IN_DIFF_Q
        q_lat, kv_lat, kpe_raw = proj[..., :o0], proj[..., o0:o1], proj[..., o1:o2]
        dq, dk, dv = proj[..., o2:o3], proj[..., o3:o4], proj[..., o4:]

        q = (rms_norm(q_lat, mla_q_lat_g[l]) @ mla_w_q_up[l]).reshape(B, S, MLA_HEADS, MLA_QK)
        q = q.transpose(0, 2, 1, 3)
        q_nope = rms_norm(q[..., :MLA_NOPE], mla_q_g[l, :MLA_NOPE])
        q_pe = apply_rope(rms_norm(q[..., MLA_NOPE:], mla_q_g[l, MLA_NOPE:]), cos_m, sin_m)
        kv = (rms_norm(kv_lat, mla_kv_lat_g[l]) @ mla_w_kv_up[l]).reshape(B, S, MLA_HEADS, MLA_NOPE + MLA_V)
        kv = kv.transpose(0, 2, 1, 3)
        k_nope = rms_norm(kv[..., :MLA_NOPE], mla_k_g[l, :MLA_NOPE])
        v_m = kv[..., MLA_NOPE:]
        k_pe = apply_rope(rms_norm(kpe_raw, mla_k_g[l, MLA_NOPE:])[:, None], cos_m, sin_m)
        k_m = jnp.concatenate([k_nope, jnp.broadcast_to(k_pe, (B, MLA_HEADS, S, MLA_ROPE))], axis=-1)
        q_m = jnp.concatenate([q_nope, q_pe], axis=-1)
        out_m = causal_attention((q_m,), (k_m,), (1.0,), v_m, MLA_QK ** -0.5)

        qd = dq.reshape(B, S, DIFF_HEADS, 2, DIFF_DQK).transpose(0, 2, 3, 1, 4)
        kd = dk.reshape(B, S, DIFF_HEADS, 2, DIFF_DQK).transpose(0, 2, 3, 1, 4)
        qd = apply_rope(rms_norm(qd, diff_q_g[l]), cos_d, sin_d)
        kd = apply_rope(rms_norm(kd, diff_k_g[l]), cos_d, sin_d)
        vd = dv.reshape(B, S, DIFF_HEADS, DIFF_DV).transpose(0, 2, 1, 3)
        lambda_init = 0.8 - 0.6 * math.exp(-0.3 * l)
        lam = (jnp.exp(jnp.sum(diff_lq1[l].astype(jnp.float32) * diff_lk1[l].astype(jnp.float32)))
               - jnp.exp(jnp.sum(diff_lq2[l].astype(jnp.float32) * diff_lk2[l].astype(jnp.float32)))
               + lambda_init)
        out_d = causal_attention((qd[:, :, 0], qd[:, :, 1]), (kd[:, :, 0], kd[:, :, 1]),
                                 (1.0, -lam), vd, DIFF_DQK ** -0.5)
        out_d = rms_norm(out_d, diff_subln_g[l]) * (1.0 - lambda_init)

        mixed = jnp.concatenate([out_m.transpose(0, 2, 1, 3).reshape(B, S, MLA_HEADS * MLA_V),
                                 out_d.transpose(0, 2, 1, 3).reshape(B, S, DIFF_HEADS * DIFF_DV)], axis=-1)
        x = x + g1 * (mixed @ w_out[l])

        h2 = rms_norm(x, norm2_g[l]) * (1.0 + sc2) + sh2
        y = peer_ffn(h2.reshape(B * S, D), peer_w_q[l], peer_sub_keys[l], peer_u[l], peer_v[l])
        x = x + g2 * y.reshape(B, S, D)
    return x


def setup_inputs(seed=0):
    out = dict(first_inputs(seed))
    for name, value in second_inputs(seed + 1).items():
        if name != "x":
            out[name + "_2"] = value
    return out


def reference(
    x, a_norm_g, a_w_in, a_w_out, kv_norm_g, w_kv, k_norm_g, rel_bias, b_norm_g, b_w_in,
    b_q_norm_g, b_sinks, b_w_out, c_2, ada_w_2, ada_b_2, norm1_g_2, w_in_2, mla_q_lat_g_2,
    mla_w_q_up_2, mla_kv_lat_g_2, mla_w_kv_up_2, mla_q_g_2, mla_k_g_2, diff_q_g_2, diff_k_g_2,
    diff_lq1_2, diff_lk1_2, diff_lq2_2, diff_lk2_2, diff_subln_g_2, w_out_2, norm2_g_2,
    peer_w_q_2, peer_sub_keys_2, peer_u_2, peer_v_2,
):
    x = first_block(
        x, a_norm_g, a_w_in, a_w_out, kv_norm_g, w_kv, k_norm_g, rel_bias, b_norm_g, b_w_in,
        b_q_norm_g, b_sinks, b_w_out,
    )
    return second_block(
        x, c_2, ada_w_2, ada_b_2, norm1_g_2, w_in_2, mla_q_lat_g_2, mla_w_q_up_2,
        mla_kv_lat_g_2, mla_w_kv_up_2, mla_q_g_2, mla_k_g_2, diff_q_g_2, diff_k_g_2, diff_lq1_2,
        diff_lk1_2, diff_lq2_2, diff_lk2_2, diff_subln_g_2, w_out_2, norm2_g_2, peer_w_q_2,
        peer_sub_keys_2, peer_u_2, peer_v_2,
    )


_drawn_inputs = setup_inputs


def setup_inputs(seed=0):
    import zlib

    import numpy as np

    out = dict(_drawn_inputs(seed))
    spreads = {}
    factors = {'kv_norm_g': 8.0,
     'k_norm_g': 8.0,
     'b_norm_g': 8.0,
     'b_q_norm_g': 8.0,
     'b_sinks': 6.701,
     'ada_b_2': 4.533,
     'norm1_g_2': 8.0,
     'mla_q_lat_g_2': 22.472,
     'mla_w_q_up_2': 5.953,
     'mla_kv_lat_g_2': 24.598,
     'mla_w_kv_up_2': 3.583,
     'mla_q_g_2': 25.12,
     'mla_k_g_2': 8.0,
     'diff_q_g_2': 64.0,
     'diff_k_g_2': 64.0,
     'diff_lq1_2': 64.0,
     'diff_lk1_2': 64.0,
     'diff_lq2_2': 200.0,
     'diff_lk2_2': 8.0,
     'diff_subln_g_2': 200.0,
     'norm2_g_2': 8.0,
     'peer_w_q_2': 3.006,
     'peer_sub_keys_2': 3.026,
     'peer_u_2': 3.343,
     'peer_v_2': 3.0}
    for name, (base, spread) in spreads.items():
        noise = np.random.default_rng([zlib.crc32(name.encode()), seed]).standard_normal(out[name].shape)
        drawn = base * np.exp(spread * noise) if base else spread * noise
        out[name] = __import__('jax').numpy.asarray(drawn.astype(out[name].dtype))
    for name, factor in factors.items():
        out[name] = (out[name] * factor).astype(out[name].dtype)
    return out
```

```python
from contextlib import ExitStack

import numpy as np

import concourse.bass as bass
from concourse import mybir

F32 = mybir.dt.float32
U32 = mybir.dt.uint32
ALU = mybir.AluOpType
ACT = mybir.ActivationFunctionType
AX = mybir.AxisListType

P = 128
T = 512
NT = T // P
D = 1024
KD = D // P
NB = 8
BANK = 512
RET_H = 4
RET_K = KD * 2
SWA_H, SWA_D, SWA_KV = 16, 64, 2
SWA_W = 2 * P
MLA_H, NOPE, ROPE = 4, 128, 64
Q_LAT, KV_LAT = 384, 256
DIFF_H = 4
HALF = ROPE // 2
PEER_H, NKEYS, TOPK = 8, 128, 16
SLOTS = PEER_H * TOPK
EPS = 1e-6
LAMBDA_INIT = 0.8 - 0.6
NEG = -1.0e30
LOWEST = -3.0e38
SQ_SCALE = 2.0 ** -32
SUM_MAX = float(np.finfo(np.float32).max) * 2.0 ** -64
BIG = 1.9e19
SLOT = 4096
NSLOT = 3
GATHER = 4

COLS = {}
for _name, _n in (("a_g", KD), ("kv_g", KD), ("b_g", KD), ("n1_g", KD), ("n2_g", KD), ("c", KD),
                  ("ada_b", 48), ("k_g", 1), ("q_g", 1), ("qlat_g", 3), ("kvlat_g", 2),
                  ("mq_g", 1), ("mk_g", 1), ("sub_g", 1)):
    _at = sum(n for _, n in COLS.values())
    COLS[_name] = (_at, _n)
NCOLS = sum(n for _, n in COLS.values())

ROWS = {}
for _name, _n in (("sinks", SWA_H), ("mq_g", ROPE), ("mk_g", ROPE), ("dq_g", ROPE), ("dk_g", ROPE),
                  ("lq1", ROPE), ("lk1", ROPE), ("lq2", ROPE), ("lk2", ROPE), ("iota", TOPK)):
    _at = sum(n for _, n in ROWS.values())
    ROWS[_name] = (_at, _n)
NROWS = sum(n for _, n in ROWS.values())

ADA_ORDER = [0, 1, 2, 3, 6, 7, 8, 9, 4, 5, 10, 11]
ADA_IN_A = 8


class Jobs:

    def __init__(self):
        self.number = {}

    def add(self, *key):
        self.number[key] = len(self.number)

    def __call__(self, *key):
        j = self.number[key]
        return j % NB, j // NB


def plan_jobs():
    jobs = Jobs()
    for k in range(KD):
        jobs.add("xT_a", k)
    jobs.add("bias", 0)
    for n in range(12):
        for i in range(4):
            jobs.add("a_in", n, i)
        if 1 <= n <= ADA_IN_A:
            jobs.add("ada", n - 1)
    for h in range(RET_H + 1):
        if h < RET_H:
            for j in range(NT):
                jobs.add("ret_s", h, j)
        if h >= 1:
            for i in range(NT):
                jobs.add("ret_o", h - 1, i)
    for f in range(RET_K):
        jobs.add("zT_a", f)
    for half in range(2):
        for t in range(NT):
            jobs.add("a_out", half, t)
    for k in range(KD):
        jobs.add("xT_b", k)
    for t in range(NT):
        jobs.add("kv", t)
    for n in range(4):
        for t in range(NT):
            jobs.add("b_in", n, t)
        jobs.add("ada", ADA_IN_A + n)
    for g in range(SWA_KV):
        jobs.add("kT", g)
    for i in range(KD):
        jobs.add("qT", i)
    for n in range(NT + 1):
        if n < NT:
            for i in range(8):
                jobs.add("swa_s", n, i)
        if n >= 1:
            for i in range(8):
                jobs.add("swa_pT", n - 1, i)
            for g in range(SWA_KV):
                jobs.add("swa_o", n - 1, g)
    for k in range(KD):
        jobs.add("zT_b", k)
    for half in range(2):
        for t in range(NT):
            jobs.add("b_out", half, t)
    for k in range(KD):
        jobs.add("xT_c", k)
    for n in range(6):
        for t in range(NT):
            jobs.add("c_in", n, t)
    for i in range(3):
        jobs.add("qlT", i)
    for i in range(2):
        jobs.add("kvlT", i)
    for t in range(NT):
        jobs.add("q_nope", t)
        jobs.add("q_rope", t)
    for t in range(NT):
        jobs.add("k_nope", t)
        jobs.add("v_up", t)
    for h in range(DIFF_H):
        jobs.add("qdT", h)
        jobs.add("kdT", h)
    jobs.add("kpeT", 0)
    for h in range(MLA_H):
        jobs.add("qnT", h)
        jobs.add("knT", h)
    for i in range(2):
        jobs.add("qrT", i)
    units = [("m", h, i) for h in range(MLA_H) for i in range(NT)] + \
            [("d", h, i) for h in range(DIFF_H) for i in range(NT)]
    for n in range(len(units) + 2):
        if n < len(units):
            jobs.add("att_s", n, 0)
            if units[n][0] == "d":
                jobs.add("att_s", n, 1)
        if n >= 2:
            jobs.add("att_pT", n - 2)
            jobs.add("att_o", n - 2)
    for k in range(KD):
        jobs.add("mT", k)
    for half in range(2):
        for t in range(NT):
            jobs.add("c_out", half, t)
    for k in range(KD):
        jobs.add("xT_d", k)
    for i in range(NT * 2):
        jobs.add("h2", i)
    for i in range(2 * PEER_H):
        jobs.add("pqT", i)
    for t in range(NT):
        for i in range(4):
            jobs.add("peer_s", t, i)
    return jobs, units


def plan_headnorms():
    units = []
    for n in range(2):
        units += [(("b_in", n, t), 8, SWA_D) for t in range(NT)]
    swa = len(units)
    for n, (heads, width) in enumerate(((1, Q_LAT), (1, KV_LAT), (1, ROPE), (8, ROPE), (8, ROPE))):
        units += [(("c_in", n, t), heads, width) for t in range(NT)]
    proj = len(units)
    for t in range(NT):
        units += [(("q_nope", t), MLA_H, NOPE), (("q_rope", t), MLA_H, ROPE)]
    units += [(("k_nope", t), MLA_H, NOPE) for t in range(NT)]
    return units, swa, proj


def network(nc, ins, out, upto=99):
    jobs, att_units = plan_jobs()
    hn_units, HN_SWA, HN_PROJ = plan_headnorms()
    HN_ALL = len(hn_units)

    stream = []
    for n in range(12):
        stream.append((("a_in", n), ins["a_w_in"][n], ("job", "a_in", n, 3)))
        if n < ADA_IN_A:
            stream.append((("ada", n), ins["ada_w"][n], ("ada", n)))
    for n in range(4):
        stream.append((("a_out", n), ins["a_w_out"][n], ("job", "a_out", n // 2, NT - 1)))
    stream.append((("kv", 0), ins["w_kv"], ("job", "kv", NT - 1)))
    for n in range(4):
        stream.append((("b_in", n), ins["b_w_in"][n], ("job", "b_in", n, NT - 1)))
        stream.append((("ada", ADA_IN_A + n), ins["ada_w"][ADA_IN_A + n], ("ada", ADA_IN_A + n)))
    for n in range(2):
        stream.append((("b_out", n), ins["b_w_out"][n], ("job", "b_out", n, NT - 1)))
    stream.append((("c_in", 0), ins["c_in0"], ("job", "c_in", 0, NT - 1)))
    stream.append((("c_in", 1), ins["c_in1"], ("job", "c_in", 2, NT - 1)))
    for n in range(3):
        stream.append((("c_in", 2 + n), ins["c_in2"][n], ("job", "c_in", 3 + n, NT - 1)))
    stream.append((("q_up", 0), ins["w_q_up"], ("job", "q_rope", NT - 1)))
    stream.append((("kv_up", 0), ins["w_kv_up"], ("job", "v_up", NT - 1)))
    for n in range(2):
        stream.append((("c_out", n), ins["c_w_out"][n], ("job", "c_out", n, NT - 1)))
    for n in range(4):
        stream.append((("pq", n), ins["peer_w_q"][n], ("job", "pqT", 4 * n + 3)))
    stream.append((("keys", 0), ins["sub_keys"], ("job", "peer_s", NT - 1, 3)))
    if upto < 4:
        stops = {1: ("kv", 0), 2: ("c_in", 0), 3: ("pq", 0)}
        stream = stream[:[s[0] for s in stream].index(stops[upto])]
    place = {name: c for c, (name, _, _) in enumerate(stream)}

    with ExitStack() as ctx:
        def sb(name, shape, dt=F32):
            return ctx.enter_context(nc.sbuf_tensor(name, shape, dt))

        def sem(name):
            return ctx.enter_context(nc.semaphore(name))

        xres = sb("xres", [P, NT, D])
        ring = sb("ring", [P, NSLOT, SLOT])
        hT = sb("hT", [P, KD, T])
        work = sb("work", [P, 24576])
        tables = sb("tables", [P, 4096])
        tmp = sb("tmp", [P, 2, BANK])
        ysum = sb("ysum", [P, BANK])
        cols = sb("cols", [P, NCOLS])
        rows = sb("rows", [P, NROWS])
        ident = sb("ident", [P, P])
        ones = sb("ones", [P, P])
        trig = sb("trig", [P, 2, NT, HALF])
        minus_half = sb("minus_half", [P, 16])
        stat = sb("stat", [P, 4, NT])
        rstat = sb("rstat", [P, 3, 16])
        hstat = sb("hstat", [P, 4, 3, 8])
        modcol = sb("modcol", [P, 6, KD])
        csil = sb("csil", [P, KD])
        lam = sb("lam", [P, 8])
        astat = sb("astat", [P, 8, 16])

        ps = ctx.enter_context(nc.psum_tensor("ps", [P, NB, BANK], F32))

        def W(at, *dims):
            n = int(np.prod(dims))
            v = work[:, at:at + n]
            if len(dims) == 2:
                v = v.rearrange("p (a b) -> p a b", b=dims[1])
            elif len(dims) == 3:
                v = v.rearrange("p (a b c) -> p a b c", b=dims[1], c=dims[2])
            elif len(dims) == 4:
                v = v.rearrange("p (a b c d) -> p a b c d", b=dims[1], c=dims[2], d=dims[3])
            return v

        def col(name, k=0, n=1):
            at = COLS[name][0] + k
            return cols[:, at:at + n]

        def row(name):
            at, n = ROWS[name]
            return rows[:, at:at + n]

        trigA = tables[:, 0:1024].rearrange("p (a t) -> p a t", a=2)
        decay = tables[:, 1024:3072].rearrange("p (h t) -> p h t", h=RET_H)
        causal = tables[:, 3072:3968]
        gates = tables[:, 0:2048].rearrange("p (a d) -> p a d", a=2)
        a_q, a_k = W(0, RET_H, 2, T), W(4096, RET_H, 2, T)
        a_oT = W(0, RET_K, T)
        a_v, a_z = W(8192, NT, 2048), W(16384, NT, 2048)
        a_sT = hT[:, :, :].rearrange("p (b j) t -> p b j t", b=2)
        a_xn = W(8192, NT, D)
        bias_in = W(7296, 784)
        bias_w, bias_hot, bias_mask = bias_in[0:32, 0:16], bias_in[0:32, 16:400], bias_in[0:SWA_H, 400:784]
        b_kvT, b_qT, b_xn, b_qn = W(0, KD, T), W(4096, KD, T), W(8192, NT, D), W(8192, NT, D)
        b_bias = W(12288, SWA_H, SWA_W)
        b_z = W(16384, NT, D)
        b_kv, b_kn, b_kT = W(20480, NT, 256), W(21504, NT, SWA_KV, 2, SWA_D), W(22528, SWA_KV, 2, T)
        b_s = [W(0, SWA_H, SWA_W), W(8192, SWA_H, SWA_W)]
        b_pT = hT[:, :, :].rearrange("p (a b) t -> p (a b t)", b=1)
        b_zT = W(4096, KD, T)
        c_xn = W(0, NT, D)
        c_ql, c_kvl, c_kpe = W(4096, NT, Q_LAT), W(5632, NT, KV_LAT), W(6656, NT, ROPE)
        c_dq, c_dk, c_dv = W(8192, NT, 512), W(10240, NT, 512), W(12288, NT, 512)
        c_dqr, c_dkr, c_kper = W(0, NT, 512), W(2048, NT, 512), W(7168, NT, 2, ROPE)
        c_qlT, c_kvlT = W(14336, 3, T), W(15872, 2, T)
        c_kpeT, c_qdT, c_kdT = W(16896, 2, T), W(17920, DIFF_H, T), W(19968, DIFF_H, 2, T)
        c_qn, c_qr, c_kn, c_v = W(4096, NT, 512), W(6144, NT, 256), W(8192, NT, 512), W(10240, NT, 512)
        c_qrr, c_qnT, c_qrT, c_knT = W(0, NT, 256), W(1024, MLA_H, T), W(3072, 2, T), W(14336, MLA_H, T)
        c_s = W(4096, 8, BANK)
        c_pT = hT[:, :, :]
        c_om, c_od = W(8192, NT, 512), W(0, NT, 512)
        c_mT = W(4096, KD, T)
        d_xn, d_h2, d_qT, d_s = W(0, NT, D), W(4096, NT, D), W(8192, 2 * PEER_H, T), W(16384, NT, 16, NKEYS)
        r_scr, r_cand, r_cscr, r_eq = W(8192, 16, NKEYS), W(10240, PEER_H, 256), W(12288, PEER_H, 256), W(14336, SLOTS, TOPK)
        r_v, r_idxf = W(0, 2, PEER_H, TOPK), W(256, 2, PEER_H, TOPK)
        r_fv, r_sel = W(512, PEER_H, TOPK), W(640, 2, SLOTS)
        r_posf, r_g, r_sum = W(896, 2, SLOTS), W(1152, NT, SLOTS), W(1664, 2, PEER_H)
        r_a, r_coef, r_astage, r_cstage = W(1680, SLOTS), W(1808, SLOTS), W(1936, 8), W(1944, 8)
        r_y = W(2048, D)
        r_out = W(3072, D)
        idxu = W(14336, 2, PEER_H, TOPK).bitcast(U32)
        fpos = W(3072, 3, SLOTS).bitcast(U32)
        eidx = W(3584, NT, SLOTS).bitcast(U32)
        estage = sb("estage", [P, 2, GATHER], U32)
        absorb = sb("absorb", [P, 1])
        experts = ring[:, :, :].rearrange("p s c -> p (s c)")[:, 0:2 * GATHER * D].rearrange("p (r d) -> p r d", d=D)

        bank_full = [sem(f"bank_full{b}") for b in range(NB)]
        bank_free = [sem(f"bank_free{b}") for b in range(NB)]
        slot_loaded = [sem(f"slot_loaded{s}") for s in range(NSLOT)]
        x_loaded = [sem(f"x_loaded{t}") for t in range(NT)]
        const_loaded = sem("const_loaded")
        ret_loaded = sem("ret_loaded")
        row_loaded = sem("row_loaded")
        gate_bias = sem("gate_bias")
        bias_kept = sem("bias_kept")
        bias_loaded = sem("bias_loaded")
        made = sem("made")
        sq_done = sem("sq_done")
        ms_done = sem("ms_done")
        rr_done = sem("rr_done")
        xn_done = sem("xn_done")
        silu_c = sem("silu_c")
        ada_step = sem("ada_step")
        mod_done = sem("mod_done")
        qk_tmp = sem("qk_tmp")
        qk_done = sem("qk_done")
        z_sq = sem("z_sq")
        z_ms = sem("z_ms")
        z_r = sem("z_r")
        bias_done = sem("bias_done")
        k_sq = sem("k_sq")
        k_ss = sem("k_ss")
        k_ms = sem("k_ms")
        k_r = sem("k_r")
        k_n = sem("k_n")
        padded = sem("padded")
        hn_sq = sem("hn_sq")
        hn_ss = sem("hn_ss")
        hn_ms = sem("hn_ms")
        hn_r = sem("hn_r")
        sw_s = sem("sw_s")
        sw_m = sem("sw_m")
        sw_nm = sem("sw_nm")
        sw_e = sem("sw_e")
        sw_es = sem("sw_es")
        sw_l = sem("sw_l")
        sw_rl = sem("sw_rl")
        sw_z = sem("sw_z")
        sw_zg = sem("sw_zg")
        rope_t = sem("rope_t")
        rope_done = sem("rope_done")
        lam_dve = sem("lam_dve")
        lam_act = sem("lam_act")
        at_s = sem("at_s")
        at_nm = sem("at_nm")
        at_p = sem("at_p")
        at_rl = sem("at_rl")
        at_w = sem("at_w")
        od_clamped = sem("od_clamped")
        od_sq = sem("od_sq")
        od_ms = sem("od_ms")
        od_r = sem("od_r")
        od_rr = sem("od_rr")
        sub_done = sem("sub_done")
        out_tmp = sem("out_tmp")
        route = sem("route")
        route_e = sem("route_e")
        routed = sem("routed")
        g_staged = sem("g_staged")
        g_absorb = sem("g_absorb")
        g_loaded = [sem(f"g_loaded{r}") for r in range(2 * GATHER)]
        g_used = [sem(f"g_used{h}") for h in range(2)]
        g_dve = sem("g_dve")
        a_ready = sem("a_ready")
        gelu_done = sem("gelu_done")
        coef_done = sem("coef_done")
        y_step = sem("y_step")
        out_ready = sem("out_ready")
        stored = sem("stored")

        def full(eng, *key):
            b, use = jobs(*key)
            eng.wait_ge(bank_full[b], use + 1)
            return ps[:, b, :]

        def taken(ins_, *key):
            ins_.then_inc(bank_free[jobs(*key)[0]], 1)

        def drained(eng, *key):
            b, use = jobs(*key)
            eng.wait_ge(bank_free[b], use + 1)

        def weights(kt, width, *name):
            c = place[name]
            return ring[:, c % NSLOT, 0:kt * width].rearrange("p (k c) -> p k c", k=kt)

        def arrived(eng, *name):
            c = place[name]
            eng.wait_ge(slot_loaded[c % NSLOT], 16 * (c // NSLOT + 1))

        def sqbuf(n):
            return tmp[:, n % 2, :]

        block = ctx.enter_context(nc.Block())

        @block.sync
        def _(sp):
            for t in range(NT):
                sp.dma_start(xres[:, t, :], ins["x"][t * P:(t + 1) * P, :]).then_inc(x_loaded[t], 16)
                if t == 0:
                    sp.dma_start(ident[:], ins["ident"]).then_inc(const_loaded, 16)
                    sp.dma_start(cols[:], ins["cols"]).then_inc(const_loaded, 16)
            for c, (name, src, _) in enumerate(stream):
                if c == 2:
                    sp.dma_start(trigA, ins["trig_a"]).then_inc(ret_loaded, 16)
                    sp.dma_start(decay, ins["decay"]).then_inc(ret_loaded, 16)
                if c >= NSLOT:
                    last = stream[c - NSLOT][2]
                    if last[0] == "ada":
                        sp.wait_ge(ada_step, KD * (last[1] + 1))
                    else:
                        full(sp, *last[1:])
                sp.dma_start(ring[:, c % NSLOT, 0:src.shape[1]], src).then_inc(slot_loaded[c % NSLOT], 16)
                if name == ("a_out", 0):
                    drained(sp, "ret_s", RET_H - 1, NT - 1)
                    sp.dma_start(gates, ins["gate_b"]).then_inc(gate_bias, 16)
            for t in range(NT):
                sp.wait_ge(out_ready, t + 1)
                sp.dma_start(out[t * P:(t + 1) * P, :], xres[:, t, :]).then_inc(stored, 16)
            sp.wait_ge(stored, 16 * NT)
            sp.wait_ge(row_loaded, 16 * 6)
            sp.wait_ge(gate_bias, 16)

        @block.tensor
        def _(pe):
            opened = [0]

            def start(*key):
                assert jobs.number[key] == opened[0], key
                opened[0] += 1
                b, use = jobs(*key)
                if use:
                    pe.wait_ge(bank_free[b], use)
                return ps[:, b, :]

            def end(mm, *key):
                mm.then_inc(bank_full[jobs(*key)[0]], 1)

            def transposes(key, src, ready=None):
                o = start(*key)
                for t in range(NT):
                    s = src(t)
                    if ready is not None:
                        ready(t)
                    mm = pe.transpose(o[0:s.shape[1], t * P:(t + 1) * P], s, ident[:])
                end(mm, *key)

            def tokens_by_features(key, lhsT, w, kt, c0, width, t):
                o = start(*key)
                for k in range(kt):
                    mm = pe.matmul(o[:, 0:width], lhsT[:, k, t * P:(t + 1) * P], w[:, k, c0:c0 + width],
                                   start=(k == 0), stop=(k == kt - 1))
                end(mm, *key)

            def output(name, src, kt):
                for half in range(2):
                    os = [start(name, half, t) for t in range(NT)]
                    for kc in range(kt // KD):
                        chunk = (name, half * (kt // KD) + kc)
                        arrived(pe, *chunk)
                        w = weights(KD, BANK, *chunk)
                        for t in range(NT):
                            for k in range(KD):
                                kk = kc * KD + k
                                mm = pe.matmul(os[t], src[:, kk, t * P:(t + 1) * P], w[:, k, :],
                                               start=(kk == 0), stop=(kk == kt - 1))
                            if kc == kt // KD - 1:
                                end(mm, name, half, t)

            def ada(n):
                part = ADA_ORDER[n] // 2
                o = start("ada", n)
                pe.wait_ge(ada_step, KD * (n + 1))
                if part in (2, 5):
                    mm = pe.matmul(o, ones[:], ysum[:], start=True, stop=True)
                else:
                    for i in range(4):
                        mm = pe.matmul(o[:, i:i + 1], ysum[:, i * P:(i + 1) * P], ones[:, 0:1],
                                       start=True, stop=True)
                end(mm, "ada", n)

            pe.wait_ge(const_loaded, 32)
            for k in range(KD):
                transposes(("xT_a", k), lambda t: a_xn[:, t, k * P:(k + 1) * P],
                           (lambda t: pe.wait_ge(xn_done, t + 1)) if k == 0 else None)
            o = start("bias", 0)
            pe.wait_ge(row_loaded, 16 * 6)
            end(pe.matmul(o[0:SWA_H, 0:384], bias_w, bias_hot, start=True, stop=True), "bias", 0)
            pe.wait_ge(made, 1)
            for n in range(12):
                arrived(pe, "a_in", n)
                w = weights(KD, BANK, "a_in", n)
                for i in range(4):
                    if n < RET_H:
                        o = start("a_in", n, i)
                        for k in range(KD):
                            if n == 0 and i == 0:
                                drained(pe, "xT_a", k)
                            mm = pe.matmul(o, w[:, k, i * P:(i + 1) * P], hT[:, k, :],
                                           start=(k == 0), stop=(k == KD - 1))
                        end(mm, "a_in", n, i)
                    else:
                        tokens_by_features(("a_in", n, i), hT, w, KD, 0, BANK, i)
                if 1 <= n <= ADA_IN_A:
                    ada(n - 1)
            for h in range(RET_H + 1):
                if h < RET_H:
                    pe.wait_ge(qk_done, 4 * (h + 1))
                    for j in range(NT):
                        o = start("ret_s", h, j)
                        for e in range(2):
                            mm = pe.matmul(o[:, 0:T - j * P], a_k[:, h, e, j * P:(j + 1) * P],
                                           a_q[:, h, e, j * P:T], start=(e == 0), stop=(e == 1))
                        end(mm, "ret_s", h, j)
                if h >= 1:
                    g = h - 1
                    for t in range(NT):
                        drained(pe, "a_in", RET_H + g, t)
                    for i in range(NT):
                        drained(pe, "ret_s", g, i)
                        o = start("ret_o", g, i)
                        for j in range(i + 1):
                            mm = pe.matmul(o, a_sT[:, g % 2, j, (i - j) * P:(i - j + 1) * P],
                                           a_v[:, j, g * BANK:(g + 1) * BANK], start=(j == 0), stop=(j == i))
                        end(mm, "ret_o", g, i)
            for f in range(RET_K):
                transposes(("zT_a", f), lambda t: a_z[:, t, f * P:(f + 1) * P],
                           lambda t: drained(pe, "ret_o", f // 4, t))
            for f in range(RET_K):
                drained(pe, "zT_a", f)
            output("a_out", a_oT, RET_K)
            if upto <= 1:
                return

            for k in range(KD):
                transposes(("xT_b", k), lambda t: b_xn[:, t, k * P:(k + 1) * P],
                           (lambda t: pe.wait_ge(xn_done, NT + t + 1)) if k == 0 else None)
            for k in range(KD):
                drained(pe, "xT_b", k)
            arrived(pe, "kv", 0)
            for t in range(NT):
                tokens_by_features(("kv", t), b_kvT, weights(KD, 256, "kv", 0), KD, 0, 256, t)
            for n in range(4):
                arrived(pe, "b_in", n)
                for t in range(NT):
                    tokens_by_features(("b_in", n, t), hT, weights(KD, BANK, "b_in", n), KD, 0, BANK, t)
                ada(ADA_IN_A + n)
            pe.wait_ge(k_n, 2)
            for g in range(SWA_KV):
                transposes(("kT", g), lambda t: b_kn[:, t, g, :, :].rearrange("p a d -> p (a d)"))
            for i in range(KD):
                transposes(("qT", i), lambda t: b_qn[:, t, i * P:(i + 1) * P],
                           lambda t: drained(pe, "b_in", i // 4, t))
            for n in range(NT + 1):
                if n < NT:
                    k0 = max(n - 1, 0) * P
                    w0 = P if n == 0 else 0
                    for i in range(8):
                        if n == 0:
                            drained(pe, "kT", i // 4)
                            drained(pe, "qT", 2 * (i // 2))
                            drained(pe, "qT", 2 * (i // 2) + 1)
                        o = start("swa_s", n, i)
                        for m in range(2):
                            mm = pe.matmul(o[:, m * SWA_W + w0:(m + 1) * SWA_W],
                                           b_qT[:, 2 * (i // 2) + m, n * P:(n + 1) * P],
                                           b_kT[:, i // 4, i % 2, k0:(n + 1) * P], start=True, stop=True)
                        end(mm, "swa_s", n, i)
                if n >= 1:
                    q = n - 1
                    for i in range(8):
                        pe.wait_ge(sw_e, SWA_H * q + 2 * i + 2)
                        o = start("swa_pT", q, i)
                        for m in range(2):
                            for kt in range(1 if q == 0 else 0, 2):
                                c = (2 * m + kt) * P
                                mm = pe.transpose(o[:, c:c + P], b_s[q % 2][:, 2 * i + m, kt * P:(kt + 1) * P],
                                                  ident[:])
                        end(mm, "swa_pT", q, i)
                    for g in range(SWA_KV):
                        o = start("swa_o", q, g)
                        for hh in range(8):
                            h = 8 * g + hh
                            drained(pe, "swa_pT", q, h // 2)
                            for kt in range(1 if q == 0 else 0, 2):
                                mm = pe.matmul(o[:, hh * SWA_D:(hh + 1) * SWA_D],
                                               b_pT[:, h * SWA_W + kt * P:h * SWA_W + (kt + 1) * P],
                                               b_kv[:, q - 1 + kt, P + g * SWA_D:P + (g + 1) * SWA_D],
                                               start=(kt == (1 if q == 0 else 0)), stop=(kt == 1))
                        end(mm, "swa_o", q, g)
            for k in range(KD):
                transposes(("zT_b", k), lambda t: b_z[:, t, k * P:(k + 1) * P],
                           lambda t: pe.wait_ge(sw_zg, SWA_KV * (t + 1)))
            for k in range(KD):
                drained(pe, "zT_b", k)
            output("b_out", b_zT, KD)
            if upto <= 2:
                return

            for k in range(KD):
                transposes(("xT_c", k), lambda t: c_xn[:, t, k * P:(k + 1) * P],
                           (lambda t: pe.wait_ge(xn_done, 2 * NT + t + 1)) if k == 0 else None)
            for k in range(KD):
                drained(pe, "xT_c", k)
            arrived(pe, "c_in", 0)
            for t in range(NT):
                tokens_by_features(("c_in", 0, t), hT, weights(KD, Q_LAT, "c_in", 0), KD, 0, Q_LAT, t)
            arrived(pe, "c_in", 1)
            w = weights(KD, KV_LAT + ROPE, "c_in", 1)
            for t in range(NT):
                tokens_by_features(("c_in", 1, t), hT, w, KD, 0, KV_LAT, t)
            for t in range(NT):
                tokens_by_features(("c_in", 2, t), hT, w, KD, KV_LAT, ROPE, t)
            for n in range(3):
                arrived(pe, "c_in", 2 + n)
                for t in range(NT):
                    tokens_by_features(("c_in", 3 + n, t), hT, weights(KD, BANK, "c_in", 2 + n), KD, 0, BANK, t)
            for i in range(3):
                transposes(("qlT", i), lambda t: c_ql[:, t, i * P:(i + 1) * P],
                           lambda t: drained(pe, "c_in", 0, t))
            for i in range(2):
                transposes(("kvlT", i), lambda t: c_kvl[:, t, i * P:(i + 1) * P],
                           lambda t: drained(pe, "c_in", 1, t))
            for i in range(3):
                drained(pe, "qlT", i)
            arrived(pe, "q_up", 0)
            w = weights(3, 768, "q_up", 0)
            for t in range(NT):
                tokens_by_features(("q_nope", t), c_qlT, w, 3, 0, 512, t)
                tokens_by_features(("q_rope", t), c_qlT, w, 3, 512, 256, t)
            for i in range(2):
                drained(pe, "kvlT", i)
            arrived(pe, "kv_up", 0)
            w = weights(2, 1024, "kv_up", 0)
            for t in range(NT):
                tokens_by_features(("k_nope", t), c_kvlT, w, 2, 0, 512, t)
                tokens_by_features(("v_up", t), c_kvlT, w, 2, 512, 512, t)
            pe.wait_ge(rope_done, 3)
            for h in range(DIFF_H):
                transposes(("qdT", h), lambda t: c_dqr[:, t, h * P:(h + 1) * P])
                transposes(("kdT", h), lambda t: c_dkr[:, t, h * P:(h + 1) * P])
            transposes(("kpeT", 0), lambda t: c_kper[:, t, :, :].rearrange("p a d -> p (a d)"))
            for h in range(MLA_H):
                transposes(("qnT", h), lambda t: c_qn[:, t, h * P:(h + 1) * P],
                           lambda t: drained(pe, "q_nope", t))
                transposes(("knT", h), lambda t: c_kn[:, t, h * P:(h + 1) * P],
                           lambda t: drained(pe, "k_nope", t))
            pe.wait_ge(rope_done, 4)
            for i in range(2):
                transposes(("qrT", i), lambda t: c_qrr[:, t, i * P:(i + 1) * P])
            for h in range(MLA_H):
                drained(pe, "qnT", h)
                drained(pe, "knT", h)
                drained(pe, "qdT", h)
                drained(pe, "kdT", h)
            drained(pe, "kpeT", 0)
            for i in range(2):
                drained(pe, "qrT", i)
            n_units = len(att_units)
            for n in range(n_units + 2):
                if n < n_units:
                    kind, h, i = att_units[n]
                    q, N = slice(i * P, (i + 1) * P), (i + 1) * P
                    o = start("att_s", n, 0)
                    if kind == "m":
                        pe.matmul(o[:, 0:N], c_qnT[:, h, q], c_knT[:, h, 0:N], start=True, stop=False)
                        mm = pe.matmul(o[:, 0:N], c_qrT[:, h // 2, q], c_kpeT[:, h % 2, 0:N], start=False, stop=True)
                        end(mm, "att_s", n, 0)
                    else:
                        mm = pe.matmul(o[:, 0:N], c_qdT[:, h, q], c_kdT[:, h, 0, 0:N], start=True, stop=True)
                        end(mm, "att_s", n, 0)
                        o = start("att_s", n, 1)
                        mm = pe.matmul(o[:, 0:N], c_qdT[:, h, q], c_kdT[:, h, 1, 0:N], start=True, stop=True)
                        end(mm, "att_s", n, 1)
                if n >= 2:
                    m = n - 2
                    kind, h, i = att_units[m]
                    o = start("att_pT", m)
                    if kind == "m":
                        pe.wait_ge(at_p, m + 1)
                        sl = m % 8
                    else:
                        pe.wait_ge(at_w, 2 * (m - 16) + 2)
                        sl = (2 * m) % 8
                    for kt in range(i + 1):
                        mm = pe.transpose(o[:, kt * P:(kt + 1) * P], c_s[:, sl, kt * P:(kt + 1) * P], ident[:])
                    end(mm, "att_pT", m)
                    drained(pe, "att_pT", m)
                    v = c_v if kind == "m" else c_dv
                    if kind == "m":
                        for t in range(NT):
                            drained(pe, "v_up", t)
                    else:
                        for t in range(NT):
                            drained(pe, "c_in", 5, t)
                    o = start("att_o", m)
                    for kt in range(i + 1):
                        mm = pe.matmul(o[:, 0:P], c_pT[:, m % 8, kt * P:(kt + 1) * P], v[:, kt, h * P:(h + 1) * P],
                                       start=(kt == 0), stop=(kt == i))
                    end(mm, "att_o", m)
            for k in range(KD):
                src = c_om if k < 4 else c_od
                u0 = (k % 4) * NT + (0 if k < 4 else 16)
                transposes(("mT", k), lambda t: src[:, t, (k % 4) * P:(k % 4 + 1) * P],
                           lambda t: drained(pe, "att_o", u0 + t))
            for k in range(KD):
                drained(pe, "mT", k)
            output("c_out", c_mT, KD)
            if upto <= 3:
                return

            for k in range(KD):
                transposes(("xT_d", k), lambda t: d_xn[:, t, k * P:(k + 1) * P],
                           (lambda t: pe.wait_ge(xn_done, 3 * NT + t + 1)) if k == 0 else None)
            for k in range(KD):
                drained(pe, "xT_d", k)
            for i in range(NT * 2):
                t, half = i // 2, i % 2
                o = start("h2", i)
                for k in range(4):
                    mm = pe.transpose(o[:, k * P:(k + 1) * P], hT[:, half * 4 + k, t * P:(t + 1) * P], ident[:])
                end(mm, "h2", i)
            for i in range(2 * PEER_H):
                if i % 4 == 0:
                    arrived(pe, "pq", i // 4)
                w = weights(KD, BANK, "pq", i // 4)
                o = start("pqT", i)
                for k in range(KD):
                    mm = pe.matmul(o, w[:, k, (i % 4) * P:(i % 4 + 1) * P], hT[:, k, :],
                                   start=(k == 0), stop=(k == KD - 1))
                end(mm, "pqT", i)
            arrived(pe, "keys", 0)
            w = weights(2 * PEER_H, NKEYS, "keys", 0)
            for t in range(NT):
                for i in range(4):
                    o = start("peer_s", t, i)
                    for m in range(4):
                        hp = 4 * i + m
                        drained(pe, "pqT", hp)
                        mm = pe.matmul(o[:, m * NKEYS:(m + 1) * NKEYS], d_qT[:, hp, t * P:(t + 1) * P],
                                       w[:, hp, :], start=True, stop=True)
                    end(mm, "peer_s", t, i)

        @block.vector
        def _(dve):
            xn_n = [0]

            def stream_norm(n, xn):
                dve.wait_ge(rr_done, n + 1)
                for t in range(NT):
                    dve.tensor_scalar(xn[:, t, :], xres[:, t, :], stat[:, 2, t:t + 1], None,
                                      ALU.mult).then_inc(xn_done, 1)

            def add_residual(name, gate=None):
                for half in range(2):
                    for t in range(NT):
                        o = full(dve, name, half, t)
                        x = xres[:, t, half * BANK:(half + 1) * BANK]
                        if gate is None:
                            taken(dve.tensor_tensor(x, x, o, ALU.add), name, half, t)
                        else:
                            i = half * NT + t
                            if i >= 2:
                                drained(dve, name + "_x", i - 2) if False else None
                            dve.tensor_tensor(tmp[:, i % 2, :], o, gate[:, half * BANK:(half + 1) * BANK],
                                              ALU.mult).then_inc(out_tmp, 1)
                            dve.wait_ge(out_tmp, i + 1)
                            taken(dve.tensor_tensor(x, x, tmp[:, i % 2, :], ALU.add), name, half, t)

            def ada(n):
                arrived(dve, "ada", n)
                w = weights(KD, BANK, "ada", n)
                if n >= 1:
                    full(dve, "ada", n - 1)
                for k in range(KD):
                    if k == 0:
                        dve.tensor_scalar(ysum[:], w[:, k, :], csil[:, k:k + 1], None,
                                          ALU.mult).then_inc(ada_step, 1)
                    else:
                        dve.wait_ge(ada_step, KD * n + k)
                        dve.scalar_tensor_tensor(ysum[:], w[:, k, :], csil[:, k:k + 1], ysum[:],
                                                 ALU.mult, ALU.add).then_inc(ada_step, 1)

            def ada_out(n):
                part, half = ADA_ORDER[n] // 2, ADA_ORDER[n] % 2
                o = full(dve, "ada", n)
                if part in (2, 5):
                    g = gates[:, part // 3, half * BANK:(half + 1) * BANK]
                    taken(dve.tensor_tensor(g, o, g, ALU.add), "ada", n)
                else:
                    taken(dve.tensor_tensor(modcol[:, part, half * 4:half * 4 + 4], o[:, 0:4],
                                            col("ada_b", part * KD + half * 4, 4), ALU.add), "ada", n)

            stream_norm(0, a_xn)
            dve.wait_ge(const_loaded, 32)
            for k in range(KD):
                o = full(dve, "xT_a", k)
                taken(dve.tensor_scalar(hT[:, k, :], o, col("a_g", k), None, ALU.mult), "xT_a", k)
            o = full(dve, "bias", 0)
            dve.wait_ge(row_loaded, 16 * 6)
            dve.tensor_tensor(bias_mask, o[0:SWA_H, 0:384], bias_mask, ALU.add).then_inc(bias_done, 1)
            dve.wait_ge(bias_done, 1)
            taken(dve.tensor_scalar(bias_mask, bias_mask, float(SWA_D ** 0.5), None, ALU.mult), "bias", 0)
            dve.wait_ge(silu_c, 1)
            dve.wait_ge(ret_loaded, 32)
            for n in range(12):
                if n < RET_H:
                    for i, dst in enumerate((a_q, a_k)):
                        e, o = full(dve, "a_in", n, 2 * i), full(dve, "a_in", n, 2 * i + 1)
                        u = 2 * n + i
                        if n == RET_H - 1:
                            dve.wait_ge(bias_kept, 16)
                        if u >= 1:
                            dve.wait_ge(qk_done, 2 * u)
                        cos, sin = trigA[:, 0, :], trigA[:, 1, :]
                        dve.tensor_tensor(dst[:, n, 0, :], e, cos, ALU.mult).then_inc(qk_tmp, 1)
                        dve.tensor_tensor(tmp[:, 0, :], o, sin, ALU.mult).then_inc(qk_tmp, 1)
                        taken(dve.tensor_tensor(dst[:, n, 1, :], o, cos, ALU.mult), "a_in", n, 2 * i + 1)
                        taken(dve.tensor_tensor(tmp[:, 1, :], e, sin, ALU.mult), "a_in", n, 2 * i)
                        dve.wait_ge(qk_tmp, 2 * (u + 1))
                        dve.tensor_tensor(dst[:, n, 0, :], dst[:, n, 0, :], tmp[:, 0, :],
                                          ALU.subtract).then_inc(qk_done, 1)
                        drained(dve, "a_in", n, 2 * i + 1)
                        drained(dve, "a_in", n, 2 * i)
                        dve.tensor_tensor(dst[:, n, 1, :], dst[:, n, 1, :], tmp[:, 1, :],
                                          ALU.add).then_inc(qk_done, 1)
                if 1 <= n <= ADA_IN_A:
                    ada_out(n - 1)
                if n < ADA_IN_A:
                    ada(n)
            for h in range(RET_H + 1):
                if h < RET_H:
                    for j in range(NT):
                        o = full(dve, "ret_s", h, j)
                        if h >= 2:
                            full(dve, "ret_o", h - 2, NT - 1)
                        taken(dve.tensor_tensor(a_sT[:, h % 2, j, 0:T - j * P], o[:, 0:T - j * P],
                                                decay[:, h, 0:T - j * P], ALU.mult), "ret_s", h, j)
                if h >= 1:
                    for i in range(NT):
                        u = (h - 1) * NT + i
                        dve.wait_ge(z_r, u + 1)
                        drained(dve, "a_in", 8 + h - 1, i)
                        o = full(dve, "ret_o", h - 1, i)
                        z = a_z[:, i, (h - 1) * BANK:h * BANK]
                        taken(dve.scalar_tensor_tensor(z, o, rstat[:, 2, u:u + 1], z, ALU.mult, ALU.mult),
                              "ret_o", h - 1, i)
            for f in range(0, RET_K, 2):
                o = full(dve, "zT_a", f)
                taken(dve.tensor_copy(a_oT[:, f, :], o), "zT_a", f)
            add_residual("a_out")
            if upto <= 1:
                for t in range(NT):
                    drained(dve, "a_out", 1, t)
                    drained(dve, "a_out", 0, t)
                    dve.sem_inc(out_ready, 1)
                return

            stream_norm(1, b_xn)
            for k in range(KD):
                o = full(dve, "xT_b", k)
                dve.tensor_scalar(b_kvT[:, k, :], o, col("kv_g", k), None, ALU.mult)
                taken(dve.tensor_scalar(hT[:, k, :], o, col("b_g", k), None, ALU.mult), "xT_b", k)
            dve.memset(b_kT[:], 0.0).then_inc(padded, 1)
            for t in range(NT):
                drained(dve, "kv", t)
            kview = b_kv[:, :, 0:P].rearrange("p t (g d) -> p t g d", d=SWA_D)
            ksq = tmp[:, 0, :].rearrange("p (t g d) -> p t g d", g=SWA_KV, d=SWA_D)
            dve.tensor_tensor(ksq, kview, kview, ALU.mult).then_inc(k_sq, 1)
            dve.wait_ge(k_sq, 1)
            kss = astat[:, 0, 0:8].rearrange("p (t g) -> p t g", g=SWA_KV)
            dve.tensor_reduce(kss, ksq, AX.X, ALU.add).then_inc(k_ss, 1)
            dve.wait_ge(k_r, 1)
            kr = astat[:, 2, 0:8].rearrange("p (t g) -> p t g", g=SWA_KV)
            for dup in range(2):
                dve.tensor_tensor(b_kn[:, :, :, dup, :], kview,
                                  kr.unsqueeze(3).to_broadcast([P, NT, SWA_KV, SWA_D]), ALU.mult).then_inc(k_n, 1)
            hn_at = [0, 0]

            def hn_reduce(n):
                key, heads, width = hn_units[n]
                b = n % 4
                sq = sqbuf(n)[:, 0:heads * width].rearrange("p (h d) -> p h d", d=width)
                dve.wait_ge(hn_sq, n + 1)
                if n >= 4:
                    dve.wait_ge(hn_r, n - 3)
                dve.tensor_reduce(hstat[:, b, 0, 0:heads], sq, AX.X, ALU.add).then_inc(hn_ss, 1)

            def hn_scale(n, dst):
                key, heads, width = hn_units[n]
                dve.wait_ge(hn_r, n + 1)
                o = full(dve, *key)
                r = hstat[:, n % 4, 2, 0:heads].unsqueeze(2).to_broadcast([P, heads, width])
                taken(dve.tensor_tensor(dst.rearrange("p (h d) -> p h d", d=width),
                                        o[:, 0:heads * width].rearrange("p (h d) -> p h d", d=width),
                                        r, ALU.mult), *key)

            def hn_run(n0, n1, dst, between=None):
                for n in range(n0, n1 + 2):
                    if n < n1:
                        hn_reduce(n)
                    if n >= n0 + 2:
                        hn_scale(n - 2, dst(n - 2))
                    if between is not None:
                        between(n)

            def b_dst(n):
                key = hn_units[n][0]
                return b_qn[:, key[2], key[1] * BANK:(key[1] + 1) * BANK]

            hn_run(0, 4, b_dst)
            ada(ADA_IN_A)
            dve.wait_ge(gate_bias, 16)
            ada_out(ADA_IN_A)
            hn_run(4, 8, b_dst)
            for n in range(1, 4):
                ada(ADA_IN_A + n)
                ada_out(ADA_IN_A + n)
            for g in range(SWA_KV):
                o = full(dve, "kT", g)
                if g == 0:
                    dve.wait_ge(padded, 1)
                dve.tensor_scalar(b_kT[0:64, g, 0, :], o[0:64, :], col("k_g")[0:64], None, ALU.mult)
                taken(dve.tensor_scalar(b_kT[64:128, g, 1, :], o[64:128, :], col("k_g")[64:128], None,
                                        ALU.mult), "kT", g)
            for i in range(KD):
                o = full(dve, "qT", i)
                taken(dve.tensor_scalar(b_qT[:, i, :], o, col("q_g"), None, ALU.mult), "qT", i)
            for i, (part, g) in enumerate(((1, "n1_g"), (4, "n2_g"))):
                for c in range(2):
                    drained(dve, "ada", (2 if i == 0 else 6) + c)
                dve.scalar_tensor_tensor(modcol[:, part, :], modcol[:, part, :], 1.0, col(g, 0, KD),
                                         ALU.add, ALU.mult).then_inc(mod_done, 1)
            dve.wait_ge(bias_loaded, 16)
            m_, nm_, d_, l_, es_, rl_ = (astat[:, i, :] for i in range(6))
            for n in range(NT + 1):
                if n < NT:
                    w0 = P if n == 0 else 0
                    s = b_s[n % 2]
                    for i in range(8):
                        o = full(dve, "swa_s", n, i)
                        if n >= 2:
                            full(dve, "swa_pT", n - 2, 7)
                        if n >= 1:
                            dve.wait_ge(sw_nm, 2 * n)
                        for m in range(2):
                            h = 2 * i + m
                            mm = dve.tensor_tensor_reduce(
                                out=s[:, h, w0:SWA_W], in0=o[:, m * SWA_W + w0:(m + 1) * SWA_W],
                                in1=b_bias[:, h, w0:SWA_W], scale=float(SWA_D ** -0.5), scalar=LOWEST,
                                op0=ALU.add, op1=ALU.max, accum_out=m_[:, h:h + 1])
                            if m == 0:
                                mm.then_inc(sw_s, 1)
                        mm.then_inc(bank_free[jobs("swa_s", n, i)[0]], 1)
                    for i in range(8):
                        drained(dve, "swa_s", n, i)
                    dve.wait_ge(sw_s, 8 * (n + 1))
                    dve.tensor_tensor(m_, m_, row("sinks"), ALU.max).then_inc(sw_m, 1)
                    dve.wait_ge(sw_m, n + 1)
                    if n >= 1:
                        dve.wait_ge(sw_e, SWA_H * n)
                        dve.wait_ge(sw_es, n)
                    dve.tensor_scalar(nm_, m_, -1.0, None, ALU.mult).then_inc(sw_nm, 1)
                    dve.tensor_tensor(d_, row("sinks"), m_, ALU.subtract).then_inc(sw_nm, 1)
                if n >= 1:
                    q = n - 1
                    pass
                if n < NT:
                    dve.wait_ge(sw_e, SWA_H * (n + 1))
                    dve.wait_ge(sw_es, n + 1)
                    dve.tensor_tensor(l_, l_, es_, ALU.add).then_inc(sw_l, 1)
                    dve.wait_ge(sw_l, n + 1)
                if n >= 1:
                    q = n - 1
                    for i in range(0, 8, 2):
                        o = full(dve, "swa_pT", q, i)
                        c0 = P if q == 0 else 0
                        dst = b_pT[:, 2 * i * SWA_W:(2 * i + 2) * SWA_W].rearrange("p (m c) -> p m c", m=2)
                        src = o.rearrange("p (m c) -> p m c", m=2)
                        if q >= 1:
                            full(dve, "swa_o", q - 1, SWA_KV - 1)
                        taken(dve.tensor_copy(dst[:, :, c0:SWA_W], src[:, :, c0:SWA_W]), "swa_pT", q, i)
                    for g in range(SWA_KV):
                        o = full(dve, "swa_o", q, g)
                        u = SWA_KV * q + g
                        if u >= 2:
                            dve.wait_ge(sw_zg, u - 1)
                        dve.wait_ge(sw_rl, q + 1)
                        ov = o.rearrange("p (h d) -> p h d", d=SWA_D)
                        tv = tmp[:, u % 2, :].rearrange("p (h d) -> p h d", d=SWA_D)
                        rl = rl_[:, 8 * g:8 * g + 8].unsqueeze(2).to_broadcast([P, 8, SWA_D])
                        dve.tensor_tensor(tv, ov, rl, ALU.mult).then_inc(bank_free[jobs("swa_o", q, g)[0]], 1)
                        drained(dve, "swa_o", q, g)
                        drained(dve, "b_in", 2 + g, q)
                        z = b_z[:, q, g * BANK:(g + 1) * BANK]
                        dve.tensor_tensor(z, tmp[:, u % 2, :], z, ALU.mult).then_inc(sw_zg, 1)
                if n < NT:
                    if n >= 1:
                        dve.wait_ge(sw_zg, SWA_KV * n)
                    dve.reciprocal(rl_, l_).then_inc(sw_rl, 1)
            for k in range(0, KD, 2):
                o = full(dve, "zT_b", k)
                taken(dve.tensor_copy(b_zT[:, k, :], o), "zT_b", k)
            add_residual("b_out")
            if upto <= 2:
                for t in range(NT):
                    drained(dve, "b_out", 1, t)
                    drained(dve, "b_out", 0, t)
                    dve.sem_inc(out_ready, 1)
                return

            stream_norm(2, c_xn)
            dve.wait_ge(mod_done, 2)
            for k in range(KD):
                o = full(dve, "xT_c", k)
                taken(dve.tensor_scalar(hT[:, k, :], o, modcol[:, 1, k:k + 1], modcol[:, 0, k:k + 1],
                                        ALU.mult, ALU.add), "xT_c", k)
            for i in range(2):
                dve.tensor_tensor_reduce(out=ysum[:, i * ROPE:(i + 1) * ROPE], in0=row(f"lq{i + 1}"),
                                         in1=row(f"lk{i + 1}"), scale=1.0, scalar=0.0, op0=ALU.mult,
                                         op1=ALU.add, accum_out=lam[:, i:i + 1]).then_inc(lam_dve, 1)
            dve.wait_ge(lam_act, 1)
            dve.tensor_tensor(lam[:, 4:5], lam[:, 2:3], lam[:, 3:4], ALU.subtract).then_inc(lam_dve, 1)
            dve.wait_ge(lam_dve, 3)
            dve.tensor_scalar(lam[:, 5:6], lam[:, 4:5], LAMBDA_INIT, -1.0, ALU.add, ALU.mult).then_inc(lam_dve, 1)
            dve.tensor_scalar(lam[:, 6:7], col("sub_g"), 1.0 - LAMBDA_INIT, None, ALU.mult).then_inc(sub_done, 1)

            def c_dst(n):
                key = hn_units[n][0]
                if key[0] == "c_in":
                    return [c_ql, c_kvl, c_kpe, c_dq, c_dk][key[1]][:, key[2], :]
                return {"q_nope": c_qn, "q_rope": c_qr, "k_nope": c_kn}[key[0]][:, key[1], :]

            rope_n = [0, 0]

            def rope(src, dst, heads, gain):
                for t in range(NT):
                    x = src[:, t, :].rearrange("p (h d) -> p h d", d=ROPE)
                    y = dst[:, t, :].rearrange("p (h d) -> p h d", d=ROPE)
                    g = gain.unsqueeze(1).to_broadcast([P, heads, ROPE])
                    cos = trig[:, 0, t, :].unsqueeze(1).to_broadcast([P, heads, HALF])
                    sin = trig[:, 1, t, :].unsqueeze(1).to_broadcast([P, heads, HALF])
                    n = heads * HALF
                    t0 = tmp[:, 0, 0:n].rearrange("p (h d) -> p h d", d=HALF)
                    t1 = tmp[:, 1, 0:n].rearrange("p (h d) -> p h d", d=HALF)
                    r0 = rope_n[0]
                    dve.wait_ge(rope_t, r0)
                    dve.tensor_tensor(x, x, g, ALU.mult).then_inc(rope_t, 1)
                    dve.wait_ge(rope_t, r0 + 1)
                    a, b = x[:, :, 0:HALF], x[:, :, HALF:ROPE]
                    dve.tensor_tensor(y[:, :, 0:HALF], a, cos, ALU.mult).then_inc(rope_t, 1)
                    dve.tensor_tensor(t0, b, sin, ALU.mult).then_inc(rope_t, 1)
                    dve.tensor_tensor(y[:, :, HALF:ROPE], b, cos, ALU.mult).then_inc(rope_t, 1)
                    dve.tensor_tensor(t1, a, sin, ALU.mult).then_inc(rope_t, 1)
                    dve.wait_ge(rope_t, r0 + 5)
                    dve.tensor_tensor(y[:, :, 0:HALF], y[:, :, 0:HALF], t0, ALU.subtract).then_inc(rope_t, 1)
                    last = dve.tensor_tensor(y[:, :, HALF:ROPE], y[:, :, HALF:ROPE], t1, ALU.add)
                    last.then_inc(rope_t, 1)
                    rope_n[0] = r0 + 7

            def roped():
                dve.wait_ge(rope_t, rope_n[0])
                dve.sem_inc(rope_done, 1)

            hn_run(HN_SWA, HN_PROJ, c_dst)
            dve.memset(c_kpeT[:], 0.0).then_inc(padded, 1)
            dve.memset(c_kdT[:], 0.0).then_inc(padded, 1)
            for i in range(3):
                o = full(dve, "qlT", i)
                taken(dve.tensor_scalar(c_qlT[:, i, :], o, col("qlat_g", i), None, ALU.mult), "qlT", i)
            for i in range(2):
                o = full(dve, "kvlT", i)
                taken(dve.tensor_scalar(c_kvlT[:, i, :], o, col("kvlat_g", i), None, ALU.mult), "kvlT", i)
            for n in range(3):
                for t in range(NT):
                    drained(dve, "c_in", 2 + n, t)
            for t in range(NT):
                pass
            rope(c_kpe, c_kper[:, :, 0, :], 1, row("mk_g"))
            dve.wait_ge(rope_t, rope_n[0])
            dve.tensor_copy(c_kper[:, :, 1, :], c_kper[:, :, 0, :]).then_inc(rope_t, 1)
            rope_n[0] += 1
            hn_run(HN_PROJ, HN_PROJ + 8, lambda n: c_dst(n))
            rope(c_dq, c_dqr, 8, row("dq_g"))
            rope(c_dk, c_dkr, 8, row("dk_g"))
            dve.wait_ge(rope_t, rope_n[0])
            for i in range(3):
                dve.sem_inc(rope_done, 1)
            hn_run(HN_PROJ + 8, HN_ALL, lambda n: c_dst(n))
            dve.wait_ge(padded, 3)
            for h in range(DIFF_H):
                o = full(dve, "qdT", h)
                taken(dve.tensor_copy(c_qdT[:, h, :], o), "qdT", h)
                o = full(dve, "kdT", h)
                dve.tensor_copy(c_kdT[0:64, h, 0, :], o[0:64, :])
                taken(dve.tensor_copy(c_kdT[64:128, h, 1, :], o[64:128, :]), "kdT", h)
            o = full(dve, "kpeT", 0)
            dve.tensor_copy(c_kpeT[0:64, 0, :], o[0:64, :])
            taken(dve.tensor_copy(c_kpeT[64:128, 1, :], o[64:128, :]), "kpeT", 0)
            for t in range(NT):
                drained(dve, "q_rope", t)
            rope(c_qr, c_qrr, 4, row("mq_g"))
            roped()
            for h in range(MLA_H):
                o = full(dve, "qnT", h)
                taken(dve.tensor_scalar(c_qnT[:, h, :], o, col("mq_g"), None, ALU.mult), "qnT", h)
                o = full(dve, "knT", h)
                taken(dve.tensor_scalar(c_knT[:, h, :], o, col("mk_g"), None, ALU.mult), "knT", h)
            for i in range(2):
                o = full(dve, "qrT", i)
                taken(dve.tensor_copy(c_qrT[:, i, :], o), "qrT", i)

            n_units = len(att_units)
            s_count = [0]
            nm_count = [0]

            def att_scores(n):
                kind, h, i = att_units[n]
                N = (i + 1) * P
                mask = causal[:, 384 - i * P:384 - i * P + N]
                for c in range(1 if kind == "m" else 2):
                    sl = (n if kind == "m" else 2 * n + c) % 8
                    o = full(dve, "att_s", n, c)
                    prev = n - (8 if kind == "m" else 4)
                    if kind == "d" and n < 20:
                        prev = 9 + 2 * (n - 16)
                    if prev >= 0:
                        full(dve, "att_pT", prev)
                    taken(dve.tensor_tensor_reduce(
                        out=c_s[:, sl, 0:N], in0=o[:, 0:N], in1=mask,
                        scale=float((NOPE + ROPE) ** -0.5 if kind == "m" else ROPE ** -0.5), scalar=LOWEST,
                        op0=ALU.add, op1=ALU.max, accum_out=astat[:, 6 * 0 + c, n % 16:n % 16 + 1]), "att_s", n, c)
                    drained(dve, "att_s", n, c)
                    if n >= 16:
                        dve.wait_ge(at_rl, n - 15)
                    dve.tensor_scalar(astat[:, 2 + c, n % 16:n % 16 + 1], astat[:, c, n % 16:n % 16 + 1], -1.0, None,
                                      ALU.mult).then_inc(at_nm, 1)

            def att_norm(n):
                kind, h, i = att_units[n]
                N = (i + 1) * P
                at = slice(n % 16, n % 16 + 1)
                if kind == "m":
                    dve.wait_ge(at_p, n + 1)
                    dve.reciprocal(astat[:, 6, at], astat[:, 4, at]).then_inc(at_rl, 1)
                else:
                    m = n - 16
                    dve.wait_ge(at_p, 16 + 2 * m + 2)
                    dve.reciprocal(astat[:, 6:8, at], astat[:, 4:6, at]).then_inc(at_rl, 1)
                    dve.wait_ge(at_rl, n + 1)
                    dve.wait_ge(lam_dve, 4)
                    p0, p1 = c_s[:, (2 * n) % 8, 0:N], c_s[:, (2 * n + 1) % 8, 0:N]
                    dve.tensor_scalar(p1, p1, astat[:, 7, at], lam[:, 5:6], ALU.mult, ALU.mult).then_inc(at_w, 1)
                    dve.wait_ge(at_w, 2 * m + 1)
                    dve.scalar_tensor_tensor(p0, p0, astat[:, 6, at], p1, ALU.mult, ALU.add).then_inc(at_w, 1)

            def att_clamp(n):
                kind, h, i = att_units[n]
                if kind == "d":
                    u = n - 16
                    o = full(dve, "att_o", n)
                    if u >= 2:
                        dve.wait_ge(od_sq, u - 1)
                    dve.tensor_scalar(tmp[:, u % 2, 0:P], o[:, 0:P], BIG, -BIG, ALU.min, ALU.max).then_inc(od_clamped, 1)

            def att_out(n):
                kind, h, i = att_units[n]
                at = slice(n % 16, n % 16 + 1)
                if kind == "m":
                    dve.wait_ge(at_rl, n + 1)
                    o = full(dve, "att_o", n)
                    taken(dve.tensor_scalar(c_om[:, i, h * P:(h + 1) * P], o[:, 0:P], astat[:, 6, at], None,
                                            ALU.mult), "att_o", n)
                else:
                    m = n - 16
                    dve.wait_ge(od_r, m + 1)
                    dve.scalar_tensor_tensor(rstat[:, 2, m:m + 1], rstat[:, 0, m:m + 1], SUM_MAX, rstat[:, 2, m:m + 1],
                                             ALU.is_le, ALU.mult).then_inc(od_rr, 1)
                    dve.wait_ge(od_rr, m + 1)
                    o = full(dve, "att_o", n)
                    taken(dve.tensor_scalar(c_od[:, i, h * P:(h + 1) * P], o[:, 0:P], rstat[:, 2, m:m + 1], None,
                                            ALU.mult), "att_o", n)

            for n in range(n_units + 3):
                if n < n_units:
                    att_scores(n)
                if 1 <= n <= n_units:
                    att_norm(n - 1)
                if 2 <= n < n_units + 2:
                    att_clamp(n - 2)
                if n >= 3:
                    att_out(n - 3)
            for k in range(KD):
                o = full(dve, "mT", k)
                if k < 4:
                    taken(dve.tensor_copy(c_mT[:, k, :], o), "mT", k)
                else:
                    dve.wait_ge(sub_done, 1)
                    taken(dve.tensor_scalar(c_mT[:, k, :], o, lam[:, 6:7], None, ALU.mult), "mT", k)
            for n in range(4):
                drained(dve, "ada", ADA_IN_A + n)
            add_residual("c_out", gates[:, 0, :])
            if upto <= 3:
                for t in range(NT):
                    drained(dve, "c_out", 1, t)
                    drained(dve, "c_out", 0, t)
                    dve.sem_inc(out_ready, 1)
                return

            stream_norm(3, d_xn)
            for k in range(KD):
                o = full(dve, "xT_d", k)
                taken(dve.tensor_scalar(hT[:, k, :], o, modcol[:, 4, k:k + 1], modcol[:, 3, k:k + 1],
                                        ALU.mult, ALU.add), "xT_d", k)
            for i in range(NT * 2):
                o = full(dve, "h2", i)
                taken(dve.tensor_copy(d_h2[:, i // 2, (i % 2) * BANK:(i % 2 + 1) * BANK], o), "h2", i)
            for i in range(0, 2 * PEER_H, 2):
                o = full(dve, "pqT", i)
                taken(dve.tensor_copy(d_qT[:, i, :], o), "pqT", i)
            for t in range(NT):
                for i in range(4):
                    o = full(dve, "peer_s", t, i)
                    taken(dve.tensor_copy(d_s[:, t, 4 * i:4 * i + 4, :].rearrange("p a n -> p (a n)"), o), "peer_s", t, i)

            rt = [0]

            def step(ins_):
                ins_.then_inc(route, 1)
                rt[0] += 1

            def settle():
                dve.wait_ge(route, rt[0])

            def top16(src, scr, values, index):
                n = len(src)
                for a in range(n):
                    step(dve.max(values[a][:, 0:8], src[a]))
                settle()
                for a in range(n):
                    step(dve.max_index(index[a][:, 0:8], values[a][:, 0:8], src[a]))
                    step(dve.match_replace(scr[a], values[a][:, 0:8], src[a], LOWEST))
                settle()
                for a in range(n):
                    step(dve.max(values[a][:, 8:16], scr[a]))
                settle()
                for a in range(n):
                    step(dve.max_index(index[a][:, 8:16], values[a][:, 8:16], scr[a]))
                settle()

            def routing(t):
                for i in range(4):
                    drained(dve, "peer_s", t, i)
                if t >= 1:
                    settle()
                flat = lambda v, a: v[:, a // PEER_H, a % PEER_H, :]
                top16([d_s[:, t, a, :] for a in range(16)], [r_scr[:, a, :] for a in range(16)],
                      [flat(r_v, a) for a in range(16)], [flat(idxu, a) for a in range(16)])
                step(dve.tensor_copy(r_idxf[:], idxu[:]))
                wide = [P, PEER_H, TOPK, TOPK]
                cand = r_cand[:].rearrange("p h (a b) -> p h a b", b=TOPK)
                step(dve.tensor_tensor(cand, r_v[:, 0].unsqueeze(3).to_broadcast(wide),
                                       r_v[:, 1].unsqueeze(2).to_broadcast(wide), ALU.add))
                settle()
                fp = fpos[:, 0, :].rearrange("p (h k) -> p h k", k=TOPK)
                top16([r_cand[:, h, :] for h in range(PEER_H)], [r_cscr[:, h, :] for h in range(PEER_H)],
                      [r_fv[:, h, :] for h in range(PEER_H)], [fp[:, h, :] for h in range(PEER_H)])
                gt = r_g[:, t, :].rearrange("p (h k) -> p h k", k=TOPK)
                step(dve.tensor_tensor(gt, r_fv[:], r_fv[:, :, 0:1].to_broadcast([P, PEER_H, TOPK]), ALU.subtract))
                arg_at = rt[0]
                step(dve.tensor_scalar(fpos[:, 1, :], fpos[:, 0, :], 4, None, ALU.logical_shift_right))
                step(dve.tensor_scalar(fpos[:, 2, :], fpos[:, 0, :], 15, None, ALU.bitwise_and))
                settle()
                step(dve.tensor_copy(r_posf[:], fpos[:, 1:3, :]))
                settle()
                for a in range(2):
                    step(dve.tensor_tensor(r_eq[:], r_posf[:, a, :].unsqueeze(2).to_broadcast([P, SLOTS, TOPK]),
                                           row("iota").unsqueeze(1).to_broadcast([P, SLOTS, TOPK]), ALU.is_equal))
                    settle()
                    eq = r_eq[:].rearrange("p (h k) a -> p h k a", k=TOPK)
                    step(dve.tensor_tensor(eq, eq, r_idxf[:, a].unsqueeze(2).to_broadcast(wide), ALU.mult))
                    settle()
                    step(dve.tensor_reduce(r_sel[:, a, :], r_eq[:], AX.X, ALU.add))
                    settle()
                step(dve.scalar_tensor_tensor(eidx[:, t, :], r_sel[:, 0, :], float(NKEYS), r_sel[:, 1, :],
                                              ALU.mult, ALU.add))
                settle()
                dve.sem_inc(routed, 1)
                dve.wait_ge(route_e, t + 1)
                step(dve.tensor_reduce(r_sum[:, 0, :], gt, AX.X, ALU.add))
                settle()
                step(dve.reciprocal(r_sum[:, 1, :], r_sum[:, 0, :]))
                settle()
                step(dve.tensor_tensor(gt, gt, r_sum[:, 1, :].unsqueeze(2).to_broadcast([P, PEER_H, TOPK]), ALU.mult))
                settle()
                return arg_at

            routing(0)
            blocks = SLOTS // (2 * GATHER)
            for t in range(NT):
                with dve.Fori(0, blocks) as b:
                    turn = b + 2 * t * blocks
                    for half in range(2):
                        for r in range(GATHER):
                            q = half * GATHER + r
                            dve.wait_ge(g_loaded[q], turn * 16 + 16)
                            dve.tensor_tensor_reduce(out=experts[:, q, :], in0=experts[:, q, :], in1=d_h2[:, t, :],
                                                     scale=1.0, scalar=0.0, op0=ALU.mult, op1=ALU.add,
                                                     accum_out=r_astage[:, q:q + 1]).then_inc(g_used[half], 1)
                    for half in range(2):
                        dve.wait_ge(g_used[half], turn * GATHER + 2 * GATHER)
                    dve.tensor_copy(r_a[:, bass.ds(b * 2 * GATHER, 2 * GATHER)], r_astage[:]).then_inc(g_dve, 1)
                    dve.wait_ge(g_dve, b + (t * blocks + 1))
                dve.sem_inc(a_ready, 1)
                dve.wait_ge(gelu_done, t + 1)
                dve.tensor_tensor(r_coef[:], r_coef[:], r_g[:, t, :], ALU.mult).then_inc(coef_done, 1)
                if t + 1 < NT:
                    routing(t + 1)
                dve.memset(r_y[:], 0.0).then_inc(coef_done, 1)
                dve.wait_ge(coef_done, 2 * t + 2)
                with dve.Fori(0, blocks) as b:
                    turn = b + (2 * t + 1) * blocks
                    dve.tensor_copy(r_cstage[:], r_coef[:, bass.ds(b * 2 * GATHER, 2 * GATHER)]).then_inc(y_step, 1)
                    base = (b + t * blocks) * (2 * GATHER + 1)
                    for half in range(2):
                        for r in range(GATHER):
                            q = half * GATHER + r
                            dve.wait_ge(y_step, base + q + 1)
                            dve.wait_ge(g_loaded[q], turn * 16 + 16)
                            dve.scalar_tensor_tensor(r_y[:], experts[:, q, :], r_cstage[:, q:q + 1], r_y[:],
                                                     ALU.mult, ALU.add).then_inc(y_step, 1)
                        dve.wait_ge(y_step, base + (half + 1) * GATHER + 1)
                        dve.sem_inc(g_used[half], GATHER)
                dve.tensor_tensor(r_y[:], r_y[:], gates[:, 1, :], ALU.mult).then_inc(out_tmp, 1)
                dve.wait_ge(out_tmp, 8 + t + 1)
                dve.tensor_tensor(xres[:, t, :], xres[:, t, :], r_y[:], ALU.add).then_inc(out_ready, 1)
                dve.wait_ge(out_ready, t + 1)

        @block.scalar
        def _(act):
            act.dma_start(rows[:], ins["rows"]).then_inc(row_loaded, 16)
            act.dma_start(causal, ins["causal"]).then_inc(row_loaded, 16)
            act.dma_start(trig[:], ins["trig"]).then_inc(row_loaded, 16)
            act.dma_start(bias_w, ins["rel_bias"]).then_inc(row_loaded, 16)
            act.dma_start(bias_hot, ins["bias_hot"]).then_inc(row_loaded, 16)
            act.dma_start(bias_mask, ins["bias_mask"]).then_inc(row_loaded, 16)

            def stream_squares(n, xn, ready):
                for t in range(NT):
                    ready(t)
                    act.activation(xn[:, t, :], xres[:, t, :], ACT.Square,
                                   accum_out=stat[:, 0, t:t + 1]).then_inc(sq_done, 1)

            stream_squares(0, a_xn, lambda t: act.wait_ge(x_loaded[t], 16))
            act.wait_ge(const_loaded, 32)
            act.activation(csil[:], col("c", 0, KD), ACT.Silu).then_inc(silu_c, 1)
            drained(act, "bias", 0)
            act.dma_start(ins["bias_rows"].rearrange("p h u -> h p u"),
                          bias_mask.unsqueeze(1).to_broadcast([SWA_H, P, 384])).then_inc(bias_kept, 16)
            for n in range(RET_H, 12):
                for t in range(NT):
                    o = full(act, "a_in", n, t)
                    if n < 2 * RET_H:
                        taken(act.activation(a_v[:, t, (n - 4) * BANK:(n - 3) * BANK], o, ACT.Copy), "a_in", n, t)
                    else:
                        taken(act.activation(a_z[:, t, (n - 8) * BANK:(n - 7) * BANK], o, ACT.Silu), "a_in", n, t)
            for h in range(RET_H):
                for i in range(NT):
                    u = h * NT + i
                    o = full(act, "ret_o", h, i)
                    if u >= 2:
                        act.wait_ge(z_sq, u - 1)
                    elif u == 0:
                        act.wait_ge(qk_done, 16)
                    act.activation(tmp[:, u % 2, :], o, ACT.Square, accum_out=rstat[:, 0, u:u + 1]).then_inc(z_sq, 1)
            for f in range(1, RET_K, 2):
                o = full(act, "zT_a", f)
                taken(act.activation(a_oT[:, f, :], o, ACT.Copy), "zT_a", f)
            if upto <= 1:
                return

            def from_out(name):
                def ready(t):
                    drained(act, name, 0, t)
                    drained(act, name, 1, t)
                return ready

            stream_squares(1, b_xn, from_out("a_out"))
            act.wait_ge(bias_kept, 16)
            for f in range(RET_K):
                drained(act, "zT_a", f)
            act.dma_start(b_bias, bass.AP(ins["bias_rows"].tensor, P - 1, [[SWA_H * 384 - 1, P], [384, SWA_H], [1, SWA_W]]))\
               .then_inc(bias_loaded, 16)
            for t in range(NT):
                o = full(act, "kv", t)
                taken(act.activation(b_kv[:, t, :], o[:, 0:256], ACT.Copy), "kv", t)

            def hn_square(n):
                key, heads, width = hn_units[n]
                o = full(act, *key)
                if n >= 2:
                    act.wait_ge(hn_ss, n - 1)
                act.activation(sqbuf(n)[:, 0:heads * width], o[:, 0:heads * width], ACT.Square).then_inc(hn_sq, 1)

            act.wait_ge(k_ss, 1)
            for n in range(HN_SWA):
                hn_square(n)
            for n in range(2, 4):
                for t in range(NT):
                    o = full(act, "b_in", n, t)
                    taken(act.activation(b_z[:, t, (n - 2) * BANK:(n - 1) * BANK], o, ACT.Silu), "b_in", n, t)
            m_, nm_, d_, l_, es_, rl_ = (astat[:, i, :] for i in range(6))
            for n in range(NT + 1):
                if n < NT:
                    w0 = P if n == 0 else 0
                    act.wait_ge(sw_nm, 2 * (n + 1))
                    if n >= 1:
                        act.wait_ge(sw_rl, n)
                    for h in range(SWA_H):
                        s = b_s[n % 2][:, h, w0:SWA_W]
                        act.activation(s, s, ACT.Exp, bias=nm_[:, h:h + 1], accum_out=l_[:, h:h + 1]).then_inc(sw_e, 1)
                    act.activation(es_, d_, ACT.Exp).then_inc(sw_es, 1)
                if n >= 1:
                    q = n - 1
                    for i in range(1, 8, 2):
                        o = full(act, "swa_pT", q, i)
                        c0 = P if q == 0 else 0
                        dst = b_pT[:, 2 * i * SWA_W:(2 * i + 2) * SWA_W].rearrange("p (m c) -> p m c", m=2)
                        src = o.rearrange("p (m c) -> p m c", m=2)
                        if q >= 1:
                            full(act, "swa_o", q - 1, SWA_KV - 1)
                        taken(act.activation(dst[:, :, c0:SWA_W], src[:, :, c0:SWA_W], ACT.Copy), "swa_pT", q, i)
            for k in range(1, KD, 2):
                o = full(act, "zT_b", k)
                taken(act.activation(b_zT[:, k, :], o, ACT.Copy), "zT_b", k)
            if upto <= 2:
                return

            stream_squares(2, c_xn, from_out("b_out"))
            act.wait_ge(lam_dve, 2)
            act.activation(lam[:, 2:4], lam[:, 0:2], ACT.Exp).then_inc(lam_act, 1)
            for n in range(HN_SWA, HN_PROJ):
                hn_square(n)
            for t in range(NT):
                o = full(act, "c_in", 5, t)
                taken(act.activation(c_dv[:, t, :], o, ACT.Copy), "c_in", 5, t)
            for n in range(HN_PROJ, HN_PROJ + 8):
                if n == HN_PROJ:
                    act.wait_ge(rope_t, 7 * NT + 1)
                hn_square(n)
            act.wait_ge(rope_done, 3)
            for t in range(NT):
                if True:
                    n = HN_PROJ + 8 + t
                    hn_square(n)
                    o = full(act, "v_up", t)
                    taken(act.activation(c_v[:, t, :], o, ACT.Copy), "v_up", t)
            n_units = len(att_units)
            for n in range(n_units + 2):
                if n < n_units:
                    kind, h, i = att_units[n]
                    N = (i + 1) * P
                    for c in range(1 if kind == "m" else 2):
                        sl = (n if kind == "m" else 2 * n + c) % 8
                        act.wait_ge(at_nm, (n if n < 16 else 16 + 2 * (n - 16)) + c + 1)
                        s = c_s[:, sl, 0:N]
                        at = slice(n % 16, n % 16 + 1)
                        act.activation(s, s, ACT.Exp, bias=astat[:, 2 + c, at],
                                       accum_out=astat[:, 4 + c, at]).then_inc(at_p, 1)
                if n >= 2:
                    m = n - 2
                    kind, h, i = att_units[m]
                    N = (i + 1) * P
                    o = full(act, "att_pT", m)
                    if m >= 8:
                        full(act, "att_o", m - 8)
                    taken(act.activation(c_pT[:, m % 8, 0:N], o[:, 0:N], ACT.Copy), "att_pT", m)
                    if kind == "d":
                        u = m - 16
                        act.wait_ge(od_clamped, u + 1)
                        act.activation(tmp[:, u % 2, 0:P], tmp[:, u % 2, 0:P], ACT.Square, scale=SQ_SCALE,
                                       accum_out=rstat[:, 0, u:u + 1]).then_inc(od_sq, 1)
            if upto <= 3:
                return

            stream_squares(3, d_xn, from_out("c_out"))
            for i in range(1, 2 * PEER_H, 2):
                o = full(act, "pqT", i)
                taken(act.activation(d_qT[:, i, :], o, ACT.Copy), "pqT", i)
            def softmax_exp(t):
                act.wait_ge(routed, t + 1)
                act.activation(r_g[:, t, :], r_g[:, t, :], ACT.Exp).then_inc(route_e, 1)

            softmax_exp(0)
            for t in range(NT):
                act.wait_ge(a_ready, t + 1)
                if t >= 1:
                    act.wait_ge(out_ready, t)
                act.activation(r_coef[:], r_a[:], ACT.Gelu).then_inc(gelu_done, 1)
                if t + 1 < NT:
                    softmax_exp(t + 1)

        @block.gpsimd
        def _(pool):
            pool.memset(ones[:], 1.0).then_inc(made, 1)
            pool.memset(minus_half[:], -0.5).then_inc(made, 1)
            pool.wait_ge(made, 2)

            def rsqrt(ss, ms, r, n, width, ms_sem, ms_at, r_sem):
                pool.tensor_scalar(ms, ss, 1.0 / width, EPS, ALU.mult, ALU.add).then_inc(ms_sem, 1)
                pool.wait_ge(ms_sem, ms_at)
                pool.tensor_tensor(r, ms, minus_half[:, 0:n], ALU.pow).then_inc(r_sem, 1)

            def stream_rsqrt(n):
                pool.wait_ge(sq_done, NT * (n + 1))
                if n >= 1:
                    pool.wait_ge(xn_done, NT * n)
                rsqrt(stat[:, 0, :], stat[:, 1, :], stat[:, 2, :], NT, D, ms_done, n + 1, rr_done)

            def hn_rsqrt(n):
                key, heads, width = hn_units[n]
                pool.wait_ge(hn_ss, n + 1)
                if n >= 4:
                    drained(pool, *hn_units[n - 4][0])
                s = hstat[:, n % 4, :, 0:heads]
                rsqrt(s[:, 0, :], s[:, 1, :], s[:, 2, :], heads, width, hn_ms, n + 1, hn_r)

            stream_rsqrt(0)
            for u in range(RET_H * NT):
                pool.wait_ge(z_sq, u + 1)
                rsqrt(rstat[:, 0, u:u + 1], rstat[:, 1, u:u + 1], rstat[:, 2, u:u + 1], 1, BANK, z_ms, u + 1, z_r)
            if upto <= 1:
                return
            stream_rsqrt(1)
            pool.wait_ge(k_ss, 1)
            rsqrt(astat[:, 0, 0:8], astat[:, 1, 0:8], astat[:, 2, 0:8], 8, SWA_D, k_ms, 1, k_r)
            for n in range(HN_SWA):
                hn_rsqrt(n)
            if upto <= 2:
                return
            stream_rsqrt(2)
            for n in range(HN_SWA, HN_ALL):
                hn_rsqrt(n)
            for u in range(DIFF_H * NT):
                pool.wait_ge(od_sq, u + 1)
                if u == 0:
                    drained(pool, "ret_o", RET_H - 1, NT - 1)
                pool.tensor_scalar(rstat[:, 1, u:u + 1], rstat[:, 0, u:u + 1], SUM_MAX, SQ_SCALE ** -2 / P,
                                   ALU.min, ALU.mult).then_inc(od_ms, 1)
                pool.wait_ge(od_ms, 2 * u + 1)
                pool.tensor_scalar(rstat[:, 1, u:u + 1], rstat[:, 1, u:u + 1], EPS, None, ALU.add).then_inc(od_ms, 1)
                pool.wait_ge(od_ms, 2 * u + 2)
                pool.tensor_tensor(rstat[:, 2, u:u + 1], rstat[:, 1, u:u + 1], minus_half[:, 0:1], ALU.pow).then_inc(od_r, 1)
            if upto <= 3:
                return
            stream_rsqrt(3)

            pool.memset(absorb[:], 0.0).then_inc(g_absorb, 1)
            pool.wait_ge(g_absorb, 1)
            for half in range(2):
                pool.sem_inc(g_used[half], GATHER)
            blocks = SLOTS // (2 * GATHER)
            full(pool, "peer_s", NT - 1, 3)
            for t in range(NT):
                for phase, table in enumerate((ins["peer_u"], ins["peer_v"])):
                    pool.wait_ge(routed, t + 1)
                    with pool.Fori(0, blocks) as b:
                        turn = b + (2 * t + phase) * blocks
                        for half in range(2):
                            pool.wait_ge(g_used[half], turn * GATHER + GATHER)
                            at = b * 2 * GATHER + half * GATHER
                            pool.tensor_copy(estage[:, half, :], eidx[:, t, bass.ds(at, GATHER)]).then_inc(g_staged, 1)
                            pool.wait_ge(g_staged, turn * 2 + half + 1)
                            pool.tensor_tensor(absorb[:], absorb[:], absorb[:], ALU.mult).then_inc(g_absorb, 1)
                            for r in range(GATHER):
                                q = half * GATHER + r
                                pool.indirect_dma_start(
                                    experts[:, q, :], None, table,
                                    bass.IndirectOffsetOnAxis(ap=estage[:, half, r:r + 1], axis=0)).then_inc(g_loaded[q], 16)



def _chunks(w, width):
    k, n = w.shape
    return np.ascontiguousarray(
        w.reshape(k // P, P, n // width, width).transpose(2, 1, 0, 3)).reshape(n // width, P, (k // P) * width)


def _colvec(v):
    return np.ascontiguousarray(v.reshape(-1, P).T)


def shape_constants():
    f = np.float32
    c = {"ident": np.eye(P, dtype=f)}
    half = np.arange(P, dtype=f)
    lin = (half / f(P - 1)).astype(f)
    angle = (f(1.0) / np.power(f(10000.0), lin, dtype=f)).astype(f)
    arg = (np.arange(T, dtype=f)[None, :] * angle[:, None]).astype(f)
    c["trig_a"] = np.stack([np.cos(arg), np.sin(arg)], 1).astype(f)
    log_gamma = np.log((1.0 - 2.0 ** (-5.0 - np.arange(RET_H))).astype(f)).astype(f)
    diff = np.arange(T)[None, :] - np.arange(P)[:, None]
    dec = np.exp(np.maximum(diff, 0).astype(f)[:, None, :] * log_gamma[None, :, None]).astype(f)
    c["decay"] = (np.where(diff[:, None, :] >= 0, dec, 0) / 16).astype(f)
    col = np.arange(896)[None, :] - 384
    c["causal"] = np.where(col <= np.arange(P)[:, None], 0.0, NEG).astype(f)
    inv = (f(1.0) / np.power(f(10000.0), (np.arange(HALF, dtype=f) / f(HALF)), dtype=f)).astype(f)
    ang = (np.arange(T, dtype=f)[:, None] * inv[None, :]).astype(f).reshape(NT, P, HALF).transpose(1, 0, 2)
    c["trig"] = np.stack([np.cos(ang), np.sin(ang)], 1).astype(f)
    dist = 255 - np.arange(384)
    inside = (dist >= 0) & (dist < P)
    d = np.clip(dist, 0, P - 1)
    large = 16 + (np.log(np.maximum(d, 1).astype(f) / f(16)) / f(np.log(8.0)) * f(16)).astype(np.int32)
    bucket = np.where(d < 16, d, np.minimum(large, 31))
    c["bias_hot"] = ((np.arange(32)[:, None] == bucket[None, :]) & inside[None, :]).astype(f)
    c["bias_mask"] = np.broadcast_to(np.where(inside, 0.0, NEG).astype(f), (SWA_H, 384)).copy()
    return c


def lay_out(i):
    a = shape_constants()
    a["x"] = np.ascontiguousarray(i["x"].reshape(T, D))
    w = i["a_w_in"][0]
    qk = np.stack([w[:, :D].reshape(D, RET_H, P, 2), w[:, D:2 * D].reshape(D, RET_H, P, 2)], 2)
    qk = qk.transpose(0, 1, 2, 4, 3).reshape(D, 2 * D)
    a["a_w_in"] = _chunks(np.concatenate([qk, w[:, 2 * D:]], 1), BANK)
    wo = i["a_w_out"][0].reshape(2, KD, P, 2, BANK).transpose(3, 0, 2, 1, 4)
    a["a_w_out"] = np.ascontiguousarray(wo).reshape(4, P, SLOT)
    a["w_kv"] = _chunks(i["w_kv"], 256)[0]
    wb = i["b_w_in"][0]
    order = [4 * (t // 2) + 2 * half + t % 2 for t in range(8) for half in range(2)]
    q = wb[:, :D].reshape(D, SWA_H, SWA_D)[:, order, :].reshape(D, D)
    a["b_w_in"] = _chunks(np.concatenate([q, wb[:, D:]], 1), BANK)
    a["b_w_out"] = _chunks(i["b_w_out"][0], BANK)
    a["rel_bias"] = np.ascontiguousarray(i["rel_bias"])
    wc = i["w_in_2"][0]
    a["c_in0"] = _chunks(wc[:, :Q_LAT], Q_LAT)[0]
    a["c_in1"] = _chunks(wc[:, Q_LAT:Q_LAT + KV_LAT + ROPE], KV_LAT + ROPE)[0]
    a["c_in2"] = _chunks(wc[:, Q_LAT + KV_LAT + ROPE:], BANK)
    wq = i["mla_w_q_up_2"][0].reshape(Q_LAT, MLA_H, NOPE + ROPE)
    a["w_q_up"] = _chunks(np.concatenate([wq[:, :, :NOPE].reshape(Q_LAT, -1), wq[:, :, NOPE:].reshape(Q_LAT, -1)], 1), 768)[0]
    wk = i["mla_w_kv_up_2"][0].reshape(KV_LAT, MLA_H, 2, NOPE)
    a["w_kv_up"] = _chunks(np.ascontiguousarray(wk.transpose(0, 2, 1, 3)).reshape(KV_LAT, 1024), 1024)[0]
    a["c_w_out"] = _chunks(i["w_out_2"][0], BANK)
    wa = i["ada_w_2"][0]
    a["ada_w"] = _chunks(wa, BANK)[ADA_ORDER]
    wp = i["peer_w_q_2"][0].reshape(D, PEER_H, 2, P).transpose(0, 2, 1, 3).reshape(D, 2 * PEER_H * P)
    a["peer_w_q"] = _chunks(wp, BANK)
    a["sub_keys"] = np.ascontiguousarray(i["peer_sub_keys_2"][0].transpose(3, 1, 0, 2)).reshape(P, 2 * PEER_H * NKEYS)
    a["peer_u"] = np.ascontiguousarray(i["peer_u_2"][0])
    a["peer_v"] = np.ascontiguousarray(i["peer_v_2"][0])
    two = lambda v: np.concatenate([v.reshape(-1), v.reshape(-1)])
    col = {"a_g": i["a_norm_g"], "kv_g": i["kv_norm_g"], "b_g": i["b_norm_g"], "n1_g": i["norm1_g_2"],
           "n2_g": i["norm2_g_2"], "c": i["c_2"], "ada_b": i["ada_b_2"], "k_g": two(i["k_norm_g"]),
           "q_g": two(i["b_q_norm_g"]), "qlat_g": i["mla_q_lat_g_2"], "kvlat_g": i["mla_kv_lat_g_2"],
           "mq_g": i["mla_q_g_2"][0, :NOPE], "mk_g": i["mla_k_g_2"][0, :NOPE], "sub_g": i["diff_subln_g_2"]}
    a["cols"] = np.ascontiguousarray(np.concatenate([_colvec(np.asarray(col[n])) for n in COLS], 1))
    row = {"sinks": i["b_sinks"], "mq_g": i["mla_q_g_2"][0, NOPE:], "mk_g": i["mla_k_g_2"][0, NOPE:],
           "dq_g": i["diff_q_g_2"], "dk_g": i["diff_k_g_2"], "lq1": i["diff_lq1_2"], "lk1": i["diff_lk1_2"],
           "lq2": i["diff_lq2_2"], "lk2": i["diff_lk2_2"], "iota": np.arange(TOPK, dtype=np.float32)}
    every = lambda v: np.broadcast_to(v, (P, v.size)).copy()
    a["rows"] = every(np.concatenate([np.asarray(row[n]).reshape(-1) for n in ROWS]))
    ab = i["ada_b_2"].reshape(6, D)
    a["gate_b"] = every(np.concatenate([ab[2], ab[5]]))
    return {k: np.ascontiguousarray(v) for k, v in a.items()}


def build(nc, arrays, upto=99):
    ins = {n: nc.dram_tensor(f"in_{n}", v.shape, F32, kind="ExternalInput").ap() for n, v in arrays.items()}
    ins["bias_rows"] = nc.dram_tensor("bias_rows", [P, SWA_H, 384], F32, kind="Internal").ap()
    out = nc.dram_tensor("out", [T, D], F32, kind="ExternalOutput").ap()
    v = dict(ins)
    v["trig_a"], v["decay"], v["trig"] = ins["trig_a"], ins["decay"], ins["trig"]
    network(nc, v, out, upto)


def kernel(**inputs):
    import concourse.bacc as bacc
    from concourse.bass_utils import run_bass_kernel_spmd

    inputs = {n: np.asarray(v) for n, v in inputs.items()}
    arrays = lay_out(inputs)
    nc = bacc.Bacc("TRN2", target_bir_lowering=False, num_devices=1)
    build(nc, arrays)
    r = run_bass_kernel_spmd(nc, [{f"in_{n}": v for n, v in arrays.items()}], core_ids=[0])
    return r.results[0]["out"].reshape(1, T, D)
```

```python
from collections import namedtuple
from contextlib import ExitStack

import numpy as np

import concourse.bass as bass
from concourse import mybir

F32 = mybir.dt.float32
U32 = mybir.dt.uint32
BF16 = mybir.dt.bfloat16
ALU = mybir.AluOpType
ACT = mybir.ActivationFunctionType
AX = mybir.AxisListType

P = 128
T = 512
NT = T // P
D = 1024
KD = D // P
NB = 8
BANK = 512
RET_H = 4
RET_K = KD * 2
SWA_H, SWA_D, SWA_KV = 16, 64, 2
SWA_W = 2 * P
MLA_H, NOPE, ROPE = 4, 128, 64
Q_LAT, KV_LAT = 384, 256
DIFF_H = 4
HALF = ROPE // 2
PEER_H, NKEYS, TOPK = 8, 128, 16
SLOTS = PEER_H * TOPK
GATHERED = 2
DENSE = NT - GATHERED
DT = DENSE * P
PAIR = 2
STEPS = NKEYS // PAIR
QUARTERS = 2 * GATHERED
QKEYS = NKEYS // QUARTERS
QSTEPS = STEPS // QUARTERS
BATCH = DT // QSTEPS
PARTS = 3
EARLY = [0] + list(range(GATHERED, NT))
LATE = 1
NE = len(EARLY)
EPS = 1e-6
LAMBDA_INIT = 0.8 - 0.6
NEG = -1.0e30
LOWEST = -3.0e38
SQ_SCALE = 2.0 ** -32
SUM_MAX = float(np.finfo(np.float32).max) * 2.0 ** -64
BIG = 1.9e19
SLOT = 4096
NSLOT = 3
GATHER = 4

COLS = {}
for _name, _n in (("a_g", KD), ("kv_g", KD), ("b_g", KD), ("n1_g", KD), ("n2_g", KD), ("c", KD),
                  ("ada_b", 48), ("k_g", 1), ("q_g", 1), ("qlat_g", 3), ("kvlat_g", 2),
                  ("mq_g", 1), ("mk_g", 1), ("sub_g", 1)):
    _at = sum(n for _, n in COLS.values())
    COLS[_name] = (_at, _n)
NCOLS = sum(n for _, n in COLS.values())

ROWS = {}
for _name, _n in (("sinks", SWA_H), ("mq_g", ROPE), ("mk_g", ROPE), ("dq_g", ROPE), ("dk_g", ROPE),
                  ("lq1", ROPE), ("lk1", ROPE), ("lq2", ROPE), ("lk2", ROPE)):
    _at = sum(n for _, n in ROWS.values())
    ROWS[_name] = (_at, _n)
NROWS = sum(n for _, n in ROWS.values())

ADA_ORDER = [0, 1, 2, 3, 6, 7, 8, 9, 4, 5, 10, 11]
ADA_IN_A = 8


Ranking = namedtuple("Ranking", "scr cand cscr eq v idxf idx pos posf")


class Jobs:

    def __init__(self):
        self.number = {}

    def add(self, *key):
        self.number[key] = len(self.number)

    def __call__(self, *key):
        j = self.number[key]
        return j % NB, j // NB


def plan_jobs():
    jobs = Jobs()
    for k in range(KD):
        jobs.add("xT_a", k)
    jobs.add("bias", 0)
    for n in range(12):
        for i in range(4):
            jobs.add("a_in", n, i)
        if 1 <= n <= ADA_IN_A:
            jobs.add("ada", n - 1)
    for h in range(RET_H + 1):
        if h < RET_H:
            for j in range(NT):
                jobs.add("ret_s", h, j)
        if h >= 1:
            for i in range(NT):
                jobs.add("ret_o", h - 1, i)
    for f in range(RET_K):
        jobs.add("zT_a", f)
    for half in range(2):
        for t in range(NT):
            jobs.add("a_out", half, t)
    for k in range(KD):
        jobs.add("xT_b", k)
    for t in range(NT):
        jobs.add("kv", t)
    for n in range(4):
        for t in range(NT):
            jobs.add("b_in", n, t)
        if n >= 1:
            jobs.add("ada", ADA_IN_A + n - 1)
    for g in range(SWA_KV):
        jobs.add("kT", g)
    for i in range(KD):
        jobs.add("qT", i)
    jobs.add("ada", ADA_IN_A + 3)
    for n in range(NT + 1):
        if n < NT:
            for i in range(8):
                jobs.add("swa_s", n, i)
        if n >= 1:
            for i in range(8):
                jobs.add("swa_pT", n - 1, i)
            for g in range(SWA_KV):
                jobs.add("swa_o", n - 1, g)
    for k in range(KD):
        jobs.add("zT_b", k)
    for half in range(2):
        for t in range(NT):
            jobs.add("b_out", half, t)
    for k in range(KD):
        jobs.add("xT_c", k)
    for n in range(6):
        for t in range(NT):
            jobs.add("c_in", n, t)
    for i in range(3):
        jobs.add("qlT", i)
    for i in range(2):
        jobs.add("kvlT", i)
    for t in range(NT):
        jobs.add("q_nope", t)
        jobs.add("q_rope", t)
    for t in range(NT):
        jobs.add("k_nope", t)
        jobs.add("v_up", t)
    for h in range(DIFF_H):
        jobs.add("qdT", h)
        jobs.add("kdT", h)
    jobs.add("kpeT", 0)
    for h in range(MLA_H):
        jobs.add("qnT", h)
        jobs.add("knT", h)
    for i in range(2):
        jobs.add("qrT", i)
    units = [("m", h, i) for h in range(MLA_H) for i in range(NT)] + \
            [("d", h, i) for h in range(DIFF_H) for i in range(NT)]
    for n in range(len(units) + 3):
        if n < len(units):
            jobs.add("att_s", n, 0)
            if units[n][0] == "d":
                jobs.add("att_s", n, 1)
        if n >= 3:
            jobs.add("att_o", n - 3)
        if 2 <= n < len(units) + 2:
            jobs.add("att_pT", n - 2)
    for k in range(KD):
        jobs.add("mT", k)
    for half in range(2):
        for t in range(NT):
            jobs.add("c_out", half, t)
    for k in range(KD):
        jobs.add("xT_d", k)
    for f in range(2 * PEER_H + 1):
        if f < 2 * PEER_H:
            jobs.add("pqT", f)
        if f >= 1:
            jobs.add("peer_s", f - 1)
        if f == 2 * PEER_H - 2:
            for i in range(GATHERED * 2):
                jobs.add("h2", i)
    for i in range(3):
        jobs.add("pairs", i)
    return jobs, units


def plan_headnorms():
    units = []
    for n in range(2):
        units += [(("b_in", n, t), 8, SWA_D) for t in range(NT)]
    swa = len(units)
    for n, (heads, width) in enumerate(((1, Q_LAT), (1, KV_LAT), (1, ROPE), (8, ROPE), (8, ROPE))):
        units += [(("c_in", n, t), heads, width) for t in range(NT)]
    proj = len(units)
    for t in range(NT):
        units += [(("q_nope", t), MLA_H, NOPE), (("q_rope", t), MLA_H, ROPE)]
    units += [(("k_nope", t), MLA_H, NOPE) for t in range(NT)]
    return units, swa, proj


def network(nc, ins, out, upto=99):
    jobs, att_units = plan_jobs()
    hn_units, HN_SWA, HN_PROJ = plan_headnorms()
    HN_ALL = len(hn_units)

    stream = []
    for n in range(12):
        stream.append((("a_in", n), ins["a_w_in"][n], ("job", "a_in", n, 3)))
        if n < ADA_IN_A:
            stream.append((("ada", n), ins["ada_w"][n], ("ada", n)))
    for n in range(4):
        stream.append((("a_out", n), ins["a_w_out"][n], ("job", "a_out", n // 2, NT - 1)))
    stream.append((("kv", 0), ins["w_kv"], ("job", "kv", NT - 1)))
    for n in range(4):
        stream.append((("b_in", n), ins["b_w_in"][n], ("job", "b_in", n, NT - 1)))
        stream.append((("ada", ADA_IN_A + n), ins["ada_w"][ADA_IN_A + n], ("ada", ADA_IN_A + n)))
    for n in range(2):
        stream.append((("b_out", n), ins["b_w_out"][n], ("job", "b_out", n, NT - 1)))
    stream.append((("c_in", 0), ins["c_in0"], ("job", "c_in", 0, NT - 1)))
    stream.append((("c_in", 1), ins["c_in1"], ("job", "c_in", 2, NT - 1)))
    for n in range(3):
        stream.append((("c_in", 2 + n), ins["c_in2"][n], ("job", "c_in", 3 + n, NT - 1)))
    stream.append((("q_up", 0), ins["w_q_up"], ("job", "q_rope", NT - 1)))
    stream.append((("kv_up", 0), ins["w_kv_up"], ("job", "v_up", NT - 1)))
    for n in range(2):
        stream.append((("c_out", n), ins["c_w_out"][n], ("job", "c_out", n, NT - 1)))
    for n in range(4):
        stream.append((("pq", n), ins["peer_w_q"][n], ("job", "pqT", 4 * n + 3)))
    if upto < 4:
        stops = {1: ("kv", 0), 2: ("c_in", 0), 3: ("pq", 0)}
        stream = stream[:[s[0] for s in stream].index(stops[upto])]
    place = {name: c for c, (name, _, _) in enumerate(stream)}

    with ExitStack() as ctx:
        def sb(name, shape, dt=F32):
            return ctx.enter_context(nc.sbuf_tensor(name, shape, dt))

        def sem(name):
            return ctx.enter_context(nc.semaphore(name))

        xres = sb("xres", [P, NT, D])
        ring = sb("ring", [P, NSLOT, SLOT])
        hT = sb("hT", [P, KD, T])
        work = sb("work", [P, 24576])
        tables = sb("tables", [P, 4096])
        tmp = sb("tmp", [P, 2, BANK])
        ysum = sb("ysum", [P, BANK])
        hot_j2 = sb("hot_j2", [P, BANK])
        cols = sb("cols", [P, NCOLS])
        iota = sb("iota", [P, NKEYS])
        consts = sb("consts", [P, NROWS + 2 * NT * HALF + P + 8 * 16])
        rows = consts[:, 0:NROWS]
        ident = sb("ident", [P, P])
        trig = consts[:, NROWS:NROWS + 2 * NT * HALF].rearrange("p (a t d) -> p a t d", a=2, d=HALF)
        ones = consts[:, NROWS + 2 * NT * HALF:NROWS + 2 * NT * HALF + P]
        minus_half = sb("minus_half", [P, 16])
        stat = sb("stat", [P, 4, NT])
        rstat = sb("rstat", [P, 3, 16])
        hstat = sb("hstat", [P, 4, 3, 8])
        modcol = sb("modcol", [P, 6, KD])
        csil = sb("csil", [P, KD])
        lam = sb("lam", [P, 8])
        astat = consts[:, NROWS + 2 * NT * HALF + P:].rearrange("p (a n) -> p a n", n=16)

        ps = ctx.enter_context(nc.psum_tensor("ps", [P, NB, BANK], F32))

        def W(at, *dims):
            n = int(np.prod(dims))
            v = work[:, at:at + n]
            if len(dims) == 2:
                v = v.rearrange("p (a b) -> p a b", b=dims[1])
            elif len(dims) == 3:
                v = v.rearrange("p (a b c) -> p a b c", b=dims[1], c=dims[2])
            elif len(dims) == 4:
                v = v.rearrange("p (a b c d) -> p a b c d", b=dims[1], c=dims[2], d=dims[3])
            return v

        def col(name, k=0, n=1):
            at = COLS[name][0] + k
            return cols[:, at:at + n]

        def row(name):
            at, n = ROWS[name]
            return rows[:, at:at + n]

        trigA = tables[:, 0:1024].rearrange("p (a t) -> p a t", a=2)
        decay = tables[:, 1024:3072].rearrange("p (h t) -> p h t", h=RET_H)
        causal = tables[:, 3072:3968]
        gates = tables[:, 0:2048].rearrange("p (a d) -> p a d", a=2)
        a_q, a_k = W(0, RET_H, 2, T), W(4096, RET_H, 2, T)
        a_oT = W(0, RET_K, T)
        a_v, a_z = W(8192, NT, 2048), W(16384, NT, 2048)
        a_sT = hT[:, :, :].rearrange("p (b j) t -> p b j t", b=2)
        a_xn = W(8192, NT, D)
        bias_in = W(7296, 784)
        bias_w, bias_hot, bias_mask = bias_in[0:32, 0:16], bias_in[0:32, 16:400], bias_in[0:SWA_H, 400:784]
        b_kvT, b_qT, b_xn, b_qn = W(0, KD, T), W(4096, KD, T), W(8192, NT, D), W(8192, NT, D)
        b_bias = W(12288, SWA_H, SWA_W)
        b_z = W(16384, NT, D)
        b_kv, b_kn, b_kT = W(20480, NT, 256), W(21504, NT, SWA_KV, 2, SWA_D), W(22528, SWA_KV, 2, T)
        b_s = [W(0, SWA_H, SWA_W), W(8192, SWA_H, SWA_W)]
        b_pT = hT[:, :, :].rearrange("p (a b) t -> p (a b t)", b=1)
        b_zT = W(4096, KD, T)
        c_xn = W(0, NT, D)
        c_ql, c_kvl, c_kpe = W(4096, NT, Q_LAT), W(5632, NT, KV_LAT), W(6656, NT, ROPE)
        c_dq, c_dk, c_dv = W(8192, NT, 512), W(10240, NT, 512), W(12288, NT, 512)
        c_dqr, c_dkr, c_kper = W(0, NT, 512), W(2048, NT, 512), W(7168, NT, 2, ROPE)
        c_qlT, c_kvlT = W(14336, 3, T), W(15872, 2, T)
        c_kpeT, c_qdT, c_kdT = W(16896, 2, T), W(17920, DIFF_H, T), W(19968, DIFF_H, 2, T)
        c_qn, c_qr, c_kn, c_v = W(4096, NT, 512), W(6144, NT, 256), W(8192, NT, 512), W(10240, NT, 512)
        c_qnT, c_qrT, c_knT = W(1024, MLA_H, T), W(3072, 2, T), W(14336, MLA_H, T)
        c_qrr = [W(7680, 256), W(7936, 256), W(24064, 256), W(24320, 256)]
        c_s = W(4096, 8, BANK)
        c_pT = hT[:, :, :]
        c_om, c_od = W(8192, NT, 512), W(0, NT, 512)
        c_mT = W(4096, KD, T)
        d_xn, d_qT, d_s = W(0, NT, D), W(4096, 2, T), W(5120, 4, NT, NKEYS)
        EK = NE * TOPK
        early = Ranking(
            scr=W(7168, 2 * NE, NKEYS), cand=W(8192, NE, 256), cscr=W(9216, NE, 256), eq=W(10240, EK, TOPK),
            v=W(11264, 2, NE, TOPK), idxf=W(11392, 2, NE, TOPK), idx=W(11520, 2, NE, TOPK).bitcast(U32),
            pos=W(11648, 3, EK).bitcast(U32), posf=W(11840, 2, EK))
        r_sel, r_g, r_sum = W(12288, 2, NE, PEER_H, TOPK), W(13312, NE, PEER_H, TOPK), W(13824, 2, NE * PEER_H)
        late_s = W(14336, 2 * PEER_H, NKEYS)
        keys = W(16384, 2 * PEER_H, NKEYS)
        kept = [hT[:, k, 0:GATHERED * P] for k in range(KD)]
        iT, jT = kept[0][:, 0:P].bitcast(BF16), kept[0][:, P:2 * P].bitcast(BF16)
        gT = [kept[1][:, 0:P].bitcast(BF16), kept[1][:, P:2 * P].bitcast(BF16), kept[2][:, 0:P].bitcast(BF16)]
        r_astage, r_cstage = kept[2][:, P:P + 8], kept[2][:, P + 8:P + 16]
        eidx = kept[3].bitcast(U32)
        late_sel = [kept[3][:, P:2 * P], kept[5][:, P:2 * P]]
        g_kept = kept[4]
        r_a, r_coef = kept[5][:, 0:SLOTS], kept[5][:, SLOTS:2 * SLOTS]
        r_y = tables[:, 0:D]
        late_keep = ring[:, 2, 2048:4096].rearrange("p (f n) -> p f n", n=NKEYS)

        def Y(at, *dims):
            n = int(np.prod(dims))
            return r_y[:, at:at + n].rearrange("p (a b) -> p a b", b=dims[-1]) if len(dims) == 2 else \
                r_y[:, at:at + n].rearrange("p (a b c) -> p a b c", b=dims[1], c=dims[2])

        late_stage = Y(0, 2, NKEYS)
        late = Ranking(
            scr=Y(256, 2, NKEYS), cand=Y(512, 1, 256), cscr=Y(0, 1, 256), eq=Y(256, TOPK, TOPK),
            v=Y(768, 2, 1, TOPK), idxf=Y(800, 2, 1, TOPK), idx=Y(832, 2, 1, TOPK).bitcast(U32),
            pos=Y(864, 3, TOPK).bitcast(U32), posf=Y(912, 2, TOPK))
        late_g, late_out = Y(944, 1, TOPK), Y(960, 2, TOPK)
        late_sum, late_hold = Y(992, 2, PEER_H), r_y[:, 1008:1009]
        d_h2 = tables[:, 2048:4096].rearrange("p (t d) -> p t d", d=D)
        spread = [W(0, QKEYS, DT), W(QKEYS * DT, QKEYS, DT)]
        u_ring, v_ring = W(16384, 2, PAIR, KD, P), W(20480, 2, PAIR, D)
        wide_iota = consts[:, 0:NKEYS * BATCH // 2].bitcast(BF16).rearrange("p (i t) -> p i t", t=BATCH)
        hot_i = [ring[:, 2, b * 1024:(b + 1) * 1024].bitcast(BF16).rearrange("p (i t) -> p i t", t=BATCH)
                 for b in range(2)]
        hot_j = [[v.bitcast(BF16).rearrange("p (j t) -> p j t", t=BATCH) for v in vs]
                 for vs in ((ysum[:, 0:256], ysum[:, 256:512], kept[6]), (hot_j2[:, 0:256], hot_j2[:, 256:512], kept[7]))]
        g_rest = [tmp[:, 0, 0:DT], tmp[:, 1, 0:DT]]
        estage = sb("estage", [P, 2, GATHER], U32)
        absorb = sb("absorb", [P, 1])
        experts = ring[:, :, :].rearrange("p s c -> p (s c)")[:, 0:2 * GATHER * D].rearrange("p (r d) -> p r d", d=D)

        bank_full = [sem(f"bank_full{b}") for b in range(NB)]
        bank_free = [sem(f"bank_free{b}") for b in range(NB)]
        slot_loaded = [sem(f"slot_loaded{s}") for s in range(NSLOT)]
        x_loaded = [sem(f"x_loaded{t}") for t in range(NT)]
        const_loaded = sem("const_loaded")
        ret_loaded = sem("ret_loaded")
        row_loaded = sem("row_loaded")
        gate_bias = sem("gate_bias")
        bias_kept = sem("bias_kept")
        bias_loaded = sem("bias_loaded")
        made = sem("made")
        sq_done = sem("sq_done")
        ms_done = sem("ms_done")
        rr_done = sem("rr_done")
        xn_done = sem("xn_done")
        silu_c = sem("silu_c")
        ada_step = sem("ada_step")
        mod_done = sem("mod_done")
        qk_tmp = sem("qk_tmp")
        qk_done = sem("qk_done")
        z_sq = sem("z_sq")
        z_ms = sem("z_ms")
        z_r = sem("z_r")
        bias_done = sem("bias_done")
        k_sq = sem("k_sq")
        k_ss = sem("k_ss")
        k_ms = sem("k_ms")
        k_r = sem("k_r")
        k_n = sem("k_n")
        padded = sem("padded")
        hn_sq = sem("hn_sq")
        hn_ss = sem("hn_ss")
        hn_ms = sem("hn_ms")
        hn_r = sem("hn_r")
        sw_s = sem("sw_s")
        sw_m = sem("sw_m")
        sw_nm = sem("sw_nm")
        sw_e = sem("sw_e")
        sw_es = sem("sw_es")
        sw_l = sem("sw_l")
        sw_rl = sem("sw_rl")
        sw_z = sem("sw_z")
        sw_zg = sem("sw_zg")
        rope_t = sem("rope_t")
        rope_done = sem("rope_done")
        lam_dve = sem("lam_dve")
        lam_act = sem("lam_act")
        at_s = sem("at_s")
        at_nm = sem("at_nm")
        at_p = sem("at_p")
        at_rl = sem("at_rl")
        at_w = sem("at_w")
        od_clamped = sem("od_clamped")
        od_sq = sem("od_sq")
        od_ms = sem("od_ms")
        od_r = sem("od_r")
        od_rr = sem("od_rr")
        sub_done = sem("sub_done")
        out_tmp = sem("out_tmp")
        route = sem("route")
        route_e = sem("route_e")
        routed = sem("routed")
        keys_loaded = sem("keys_loaded")
        late_kept = sem("late_kept")
        late_step = sem("late_step")
        late_done = sem("late_done")
        iota_ready = sem("iota_ready")
        gate_part = sem("gate_part")
        ranked = sem("ranked")
        u_loaded = [sem(f"u_loaded{b}") for b in range(2)]
        v_loaded = [sem(f"v_loaded{b}") for b in range(2)]
        hot_step = sem("hot_step")
        hot_ready = sem("hot_ready")
        spread_summed = sem("spread_summed")
        spread_kept = sem("spread_kept")
        u_done = sem("u_done")
        dense_gelu = sem("dense_gelu")
        dense_coef = sem("dense_coef")
        v_done = sem("v_done")
        g_staged = sem("g_staged")
        g_absorb = sem("g_absorb")
        g_loaded = [sem(f"g_loaded{r}") for r in range(2 * GATHER)]
        g_used = [sem(f"g_used{h}") for h in range(2)]
        g_dve = sem("g_dve")
        a_ready = sem("a_ready")
        gelu_done = sem("gelu_done")
        coef_done = sem("coef_done")
        y_step = sem("y_step")
        y_zero = sem("y_zero")
        out_ready = sem("out_ready")
        out_half = sem("out_half")
        gathering = sem("gathering")
        stored = sem("stored")

        def full(eng, *key):
            b, use = jobs(*key)
            eng.wait_ge(bank_full[b], use + 1)
            return ps[:, b, :]

        def taken(ins_, *key):
            ins_.then_inc(bank_free[jobs(*key)[0]], 1)

        def drained(eng, *key):
            b, use = jobs(*key)
            eng.wait_ge(bank_free[b], use + 1)

        def weights(kt, width, *name):
            c = place[name]
            return ring[:, c % NSLOT, 0:kt * width].rearrange("p (k c) -> p k c", k=kt)

        def arrived(eng, *name):
            c = place[name]
            eng.wait_ge(slot_loaded[c % NSLOT], 16 * (c // NSLOT + 1))

        def sqbuf(n):
            return tmp[:, n % 2, :]

        block = ctx.enter_context(nc.Block())

        @block.sync
        def _(sp):
            for t in range(NT):
                sp.dma_start(xres[:, t, :], ins["x"][t * P:(t + 1) * P, :]).then_inc(x_loaded[t], 16)
                if t == 0:
                    sp.dma_start(ident[:], ins["ident"]).then_inc(const_loaded, 16)
                    sp.dma_start(cols[:], ins["cols"]).then_inc(const_loaded, 16)
            for c, (name, src, _) in enumerate(stream):
                if c == 2:
                    sp.dma_start(trigA, ins["trig_a"]).then_inc(ret_loaded, 16)
                    sp.dma_start(decay, ins["decay"]).then_inc(ret_loaded, 16)
                if c >= NSLOT:
                    last = stream[c - NSLOT][2]
                    if last[0] == "ada":
                        sp.wait_ge(ada_step, KD * (last[1] + 1))
                    else:
                        full(sp, *last[1:])
                sp.dma_start(ring[:, c % NSLOT, 0:src.shape[1]], src).then_inc(slot_loaded[c % NSLOT], 16)
                if name == ("pq", 0):
                    full(sp, "c_out", 1, NT - 1)
                    sp.dma_start(keys[:], ins["sub_keys"].rearrange("p (a n) -> p a n", n=NKEYS)).then_inc(keys_loaded, 16)
                if name == ("a_out", 0):
                    drained(sp, "ret_s", RET_H - 1, NT - 1)
                    sp.dma_start(gates, ins["gate_b"]).then_inc(gate_bias, 16)
            full(sp, "peer_s", 2 * PEER_H - 1)
            u_rows = ins["u_steps"].rearrange("n p c -> p n c")
            v_rows = ins["peer_v"].rearrange("(i n) d -> i n d", i=NKEYS)

            def load_u(n, b):
                sp.dma_start(u_ring[:, b, :, :, :].rearrange("p j k i -> p (j k i)").unsqueeze(1),
                             u_rows[:, bass.ds(n, 1), :]).then_inc(u_loaded[b], 16)

            def load_v(n, b):
                sp.dma_start(v_ring[:, b, :, :], v_rows[:, bass.ds(n * PAIR, PAIR), :]).then_inc(v_loaded[b], 16)

            for n in range(2):
                load_u(n, n)
                load_v(n, n)
            with sp.Fori(1, STEPS // 2) as turn:
                for b in range(2):
                    n = turn * 2 + b
                    sp.wait_ge(u_done, n - 1)
                    load_u(n, b)
                    sp.wait_ge(v_done, n + 1)
                    load_v(n, b)
            for t in range(NT):
                sp.wait_ge(out_ready, t + 1)
                sp.dma_start(out[t * P:(t + 1) * P, :], xres[:, t, :]).then_inc(stored, 16)
            sp.wait_ge(stored, 16 * NT)
            sp.wait_ge(row_loaded, 16 * 7)
            sp.wait_ge(gate_bias, 16)

        @block.tensor
        def _(pe):
            opened = [0]

            def start(*key):
                assert jobs.number[key] == opened[0], key
                opened[0] += 1
                b, use = jobs(*key)
                if use:
                    pe.wait_ge(bank_free[b], use)
                return ps[:, b, :]

            def end(mm, *key):
                mm.then_inc(bank_full[jobs(*key)[0]], 1)

            def transposes(key, src, ready=None):
                o = start(*key)
                for t in range(NT):
                    s = src(t)
                    if ready is not None:
                        ready(t)
                    mm = pe.transpose(o[0:s.shape[1], t * P:(t + 1) * P], s, ident[:])
                end(mm, *key)

            def stream_transposes(name, xn, n):
                def one(k, t):
                    mm = pe.transpose(ps[:, jobs(name, k)[0], t * P:(t + 1) * P], xn[:, t, k * P:(k + 1) * P], ident[:])
                    if t == NT - 1:
                        end(mm, name, k)

                for k in range(KD):
                    start(name, k)
                    for t in range(NT - 1):
                        if k == 0:
                            pe.wait_ge(xn_done, NT * n + t + 1)
                        one(k, t)
                pe.wait_ge(xn_done, NT * n + NT)
                for k in range(KD):
                    one(k, NT - 1)

            def tokens_by_features(key, lhsT, w, kt, c0, width, t, ready=None):
                o = start(*key)
                for k in range(kt):
                    if ready is not None and t == 0:
                        drained(pe, ready, k)
                    mm = pe.matmul(o[:, 0:width], lhsT[:, k, t * P:(t + 1) * P], w[:, k, c0:c0 + width],
                                   start=(k == 0), stop=(k == kt - 1))
                end(mm, *key)

            def output(name, src, kt):
                for half in range(2):
                    os = [start(name, half, t) for t in range(NT)]
                    for kc in range(kt // KD):
                        chunk = (name, half * (kt // KD) + kc)
                        arrived(pe, *chunk)
                        w = weights(KD, BANK, *chunk)
                        for t in range(NT):
                            for k in range(KD):
                                kk = kc * KD + k
                                mm = pe.matmul(os[t], src[:, kk, t * P:(t + 1) * P], w[:, k, :],
                                               start=(kk == 0), stop=(kk == kt - 1))
                            if kc == kt // KD - 1:
                                end(mm, name, half, t)

            def ada(n):
                part = ADA_ORDER[n] // 2
                o = start("ada", n)
                pe.wait_ge(ada_step, KD * (n + 1))
                if part in (2, 5):
                    mm = pe.matmul(o, ones[:], ysum[:], start=True, stop=True)
                else:
                    for i in range(4):
                        mm = pe.matmul(o[:, i:i + 1], ysum[:, i * P:(i + 1) * P], ones[:, 0:1],
                                       start=True, stop=True)
                end(mm, "ada", n)

            pe.wait_ge(const_loaded, 32)
            stream_transposes("xT_a", a_xn, 0)
            o = start("bias", 0)
            pe.wait_ge(row_loaded, 16 * 7)
            end(pe.matmul(o[0:SWA_H, 0:384], bias_w, bias_hot, start=True, stop=True), "bias", 0)
            pe.wait_ge(made, 1)
            for n in range(12):
                arrived(pe, "a_in", n)
                w = weights(KD, BANK, "a_in", n)
                for i in range(4):
                    if n < RET_H:
                        o = start("a_in", n, i)
                        for k in range(KD):
                            if n == 0 and i == 0:
                                drained(pe, "xT_a", k)
                            mm = pe.matmul(o, w[:, k, i * P:(i + 1) * P], hT[:, k, :],
                                           start=(k == 0), stop=(k == KD - 1))
                        end(mm, "a_in", n, i)
                    else:
                        tokens_by_features(("a_in", n, i), hT, w, KD, 0, BANK, i)
                if 1 <= n <= ADA_IN_A:
                    ada(n - 1)
            for h in range(RET_H + 1):
                if h < RET_H:
                    pe.wait_ge(qk_done, 4 * (h + 1))
                    for j in range(NT):
                        o = start("ret_s", h, j)
                        for e in range(2):
                            mm = pe.matmul(o[:, 0:T - j * P], a_k[:, h, e, j * P:(j + 1) * P],
                                           a_q[:, h, e, j * P:T], start=(e == 0), stop=(e == 1))
                        end(mm, "ret_s", h, j)
                if h >= 1:
                    g = h - 1
                    for t in range(NT):
                        drained(pe, "a_in", RET_H + g, t)
                    for i in range(NT):
                        drained(pe, "ret_s", g, i)
                        o = start("ret_o", g, i)
                        for j in range(i + 1):
                            mm = pe.matmul(o, a_sT[:, g % 2, j, (i - j) * P:(i - j + 1) * P],
                                           a_v[:, j, g * BANK:(g + 1) * BANK], start=(j == 0), stop=(j == i))
                        end(mm, "ret_o", g, i)
            for f in range(RET_K):
                transposes(("zT_a", f), lambda t: a_z[:, t, f * P:(f + 1) * P],
                           lambda t: drained(pe, "ret_o", f // 4, t))
            for f in range(RET_K):
                drained(pe, "zT_a", f)
            output("a_out", a_oT, RET_K)
            if upto <= 1:
                return

            stream_transposes("xT_b", b_xn, 1)
            arrived(pe, "kv", 0)
            for t in range(NT):
                tokens_by_features(("kv", t), b_kvT, weights(KD, 256, "kv", 0), KD, 0, 256, t, "xT_b")
            for n in range(4):
                arrived(pe, "b_in", n)
                for t in range(NT):
                    tokens_by_features(("b_in", n, t), hT, weights(KD, BANK, "b_in", n), KD, 0, BANK, t)
                if n >= 1:
                    ada(ADA_IN_A + n - 1)
            pe.wait_ge(k_n, 2)
            for g in range(SWA_KV):
                transposes(("kT", g), lambda t: b_kn[:, t, g, :, :].rearrange("p a d -> p (a d)"))
            for i in range(KD):
                transposes(("qT", i), lambda t: b_qn[:, t, i * P:(i + 1) * P],
                           lambda t: drained(pe, "b_in", i // 4, t))
            ada(ADA_IN_A + 3)
            for n in range(NT + 1):
                if n < NT:
                    k0 = max(n - 1, 0) * P
                    w0 = P if n == 0 else 0
                    for i in range(8):
                        if n == 0:
                            drained(pe, "kT", i // 4)
                            drained(pe, "qT", 2 * (i // 2))
                            drained(pe, "qT", 2 * (i // 2) + 1)
                        o = start("swa_s", n, i)
                        for m in range(2):
                            mm = pe.matmul(o[:, m * SWA_W + w0:(m + 1) * SWA_W],
                                           b_qT[:, 2 * (i // 2) + m, n * P:(n + 1) * P],
                                           b_kT[:, i // 4, i % 2, k0:(n + 1) * P], start=True, stop=True)
                        end(mm, "swa_s", n, i)
                if n >= 1:
                    q = n - 1
                    for i in range(8):
                        pe.wait_ge(sw_e, SWA_H * q + 2 * i + 2)
                        o = start("swa_pT", q, i)
                        for m in range(2):
                            for kt in range(1 if q == 0 else 0, 2):
                                c = (2 * m + kt) * P
                                mm = pe.transpose(o[:, c:c + P], b_s[q % 2][:, 2 * i + m, kt * P:(kt + 1) * P],
                                                  ident[:])
                        end(mm, "swa_pT", q, i)
                    for g in range(SWA_KV):
                        o = start("swa_o", q, g)
                        for hh in range(8):
                            h = 8 * g + hh
                            drained(pe, "swa_pT", q, h // 2)
                            for kt in range(1 if q == 0 else 0, 2):
                                mm = pe.matmul(o[:, hh * SWA_D:(hh + 1) * SWA_D],
                                               b_pT[:, h * SWA_W + kt * P:h * SWA_W + (kt + 1) * P],
                                               b_kv[:, q - 1 + kt, P + g * SWA_D:P + (g + 1) * SWA_D],
                                               start=(kt == (1 if q == 0 else 0)), stop=(kt == 1))
                        end(mm, "swa_o", q, g)
            for k in range(KD):
                transposes(("zT_b", k), lambda t: b_z[:, t, k * P:(k + 1) * P],
                           lambda t: pe.wait_ge(sw_zg, SWA_KV * (t + 1)))
            for k in range(KD):
                drained(pe, "zT_b", k)
            output("b_out", b_zT, KD)
            if upto <= 2:
                return

            stream_transposes("xT_c", c_xn, 2)
            arrived(pe, "c_in", 0)
            for t in range(NT):
                tokens_by_features(("c_in", 0, t), hT, weights(KD, Q_LAT, "c_in", 0), KD, 0, Q_LAT, t, "xT_c")
            arrived(pe, "c_in", 1)
            w = weights(KD, KV_LAT + ROPE, "c_in", 1)
            for t in range(NT):
                tokens_by_features(("c_in", 1, t), hT, w, KD, 0, KV_LAT, t)
            for t in range(NT):
                tokens_by_features(("c_in", 2, t), hT, w, KD, KV_LAT, ROPE, t)
            for n in range(3):
                arrived(pe, "c_in", 2 + n)
                for t in range(NT):
                    tokens_by_features(("c_in", 3 + n, t), hT, weights(KD, BANK, "c_in", 2 + n), KD, 0, BANK, t)
            for i in range(3):
                transposes(("qlT", i), lambda t: c_ql[:, t, i * P:(i + 1) * P],
                           lambda t: drained(pe, "c_in", 0, t))
            for i in range(2):
                transposes(("kvlT", i), lambda t: c_kvl[:, t, i * P:(i + 1) * P],
                           lambda t: drained(pe, "c_in", 1, t))
            for i in range(3):
                drained(pe, "qlT", i)
            arrived(pe, "q_up", 0)
            w = weights(3, 768, "q_up", 0)
            for t in range(NT):
                tokens_by_features(("q_nope", t), c_qlT, w, 3, 0, 512, t)
                tokens_by_features(("q_rope", t), c_qlT, w, 3, 512, 256, t)
            for i in range(2):
                drained(pe, "kvlT", i)
            arrived(pe, "kv_up", 0)
            w = weights(2, 1024, "kv_up", 0)
            for t in range(NT):
                tokens_by_features(("k_nope", t), c_kvlT, w, 2, 0, 512, t)
                tokens_by_features(("v_up", t), c_kvlT, w, 2, 512, 512, t)
            pe.wait_ge(rope_done, 3)
            for h in range(DIFF_H):
                transposes(("qdT", h), lambda t: c_dqr[:, t, h * P:(h + 1) * P])
                transposes(("kdT", h), lambda t: c_dkr[:, t, h * P:(h + 1) * P])
            transposes(("kpeT", 0), lambda t: c_kper[:, t, :, :].rearrange("p a d -> p (a d)"))
            for h in range(MLA_H):
                transposes(("qnT", h), lambda t: c_qn[:, t, h * P:(h + 1) * P],
                           lambda t: drained(pe, "q_nope", t))
                transposes(("knT", h), lambda t: c_kn[:, t, h * P:(h + 1) * P],
                           lambda t: drained(pe, "k_nope", t))
            pe.wait_ge(rope_done, 4)
            for i in range(2):
                transposes(("qrT", i), lambda t: c_qrr[t][:, i * P:(i + 1) * P])
            for h in range(MLA_H):
                drained(pe, "qnT", h)
                drained(pe, "knT", h)
                drained(pe, "qdT", h)
                drained(pe, "kdT", h)
            drained(pe, "kpeT", 0)
            for i in range(2):
                drained(pe, "qrT", i)
            n_units = len(att_units)
            for n in range(n_units + 3):
                if n < n_units:
                    kind, h, i = att_units[n]
                    q, N = slice(i * P, (i + 1) * P), (i + 1) * P
                    o = start("att_s", n, 0)
                    if kind == "m":
                        pe.matmul(o[:, 0:N], c_qnT[:, h, q], c_knT[:, h, 0:N], start=True, stop=False)
                        mm = pe.matmul(o[:, 0:N], c_qrT[:, h // 2, q], c_kpeT[:, h % 2, 0:N], start=False, stop=True)
                        end(mm, "att_s", n, 0)
                    else:
                        mm = pe.matmul(o[:, 0:N], c_qdT[:, h, q], c_kdT[:, h, 0, 0:N], start=True, stop=True)
                        end(mm, "att_s", n, 0)
                        o = start("att_s", n, 1)
                        mm = pe.matmul(o[:, 0:N], c_qdT[:, h, q], c_kdT[:, h, 1, 0:N], start=True, stop=True)
                        end(mm, "att_s", n, 1)
                if n >= 3:
                    m = n - 3
                    kind, h, i = att_units[m]
                    drained(pe, "att_pT", m)
                    v = c_v if kind == "m" else c_dv
                    if m in (0, MLA_H * NT):
                        for t in range(NT):
                            drained(pe, *(("v_up", t) if kind == "m" else ("c_in", 5, t)))
                    o = start("att_o", m)
                    for kt in range(i + 1):
                        mm = pe.matmul(o[:, 0:P], c_pT[:, m % 8, kt * P:(kt + 1) * P], v[:, kt, h * P:(h + 1) * P],
                                       start=(kt == 0), stop=(kt == i))
                    end(mm, "att_o", m)
                if 2 <= n < n_units + 2:
                    m = n - 2
                    kind, h, i = att_units[m]
                    o = start("att_pT", m)
                    if kind == "m":
                        pe.wait_ge(at_p, m + 1)
                        sl = m % 8
                    else:
                        pe.wait_ge(at_w, 2 * (m - 16) + 2)
                        sl = (2 * m) % 8
                    for kt in range(i + 1):
                        mm = pe.transpose(o[:, kt * P:(kt + 1) * P], c_s[:, sl, kt * P:(kt + 1) * P], ident[:])
                    end(mm, "att_pT", m)
            for k in range(KD):
                src = c_om if k < 4 else c_od
                u0 = (k % 4) * NT + (0 if k < 4 else 16)
                transposes(("mT", k), lambda t: src[:, t, (k % 4) * P:(k % 4 + 1) * P],
                           lambda t: drained(pe, "att_o", u0 + t))
            for k in range(KD):
                drained(pe, "mT", k)
            output("c_out", c_mT, KD)
            if upto <= 3:
                return

            stream_transposes("xT_d", d_xn, 3)
            for f in range(2 * PEER_H + 1):
                if f < 2 * PEER_H:
                    if f % 4 == 0:
                        arrived(pe, "pq", f // 4)
                    w = weights(KD, BANK, "pq", f // 4)
                    o = start("pqT", f)
                    for k in range(KD):
                        if f == 0:
                            drained(pe, "xT_d", k)
                        mm = pe.matmul(o, w[:, k, (f % 4) * P:(f % 4 + 1) * P], hT[:, k, :],
                                       start=(k == 0), stop=(k == KD - 1))
                    end(mm, "pqT", f)
                if f >= 1:
                    g = f - 1
                    if g == 0:
                        pe.wait_ge(keys_loaded, 16)
                    drained(pe, "pqT", g)
                    o = start("peer_s", g)
                    for t in range(NT):
                        mm = pe.matmul(o[:, t * NKEYS:(t + 1) * NKEYS], d_qT[:, g % 2, t * P:(t + 1) * P],
                                       keys[:, g, :], start=True, stop=True)
                    end(mm, "peer_s", g)
                if f == 2 * PEER_H - 2:
                    for i in range(GATHERED * 2):
                        t, half = i // 2, i % 2
                        o = start("h2", i)
                        for k in range(4):
                            mm = pe.transpose(o[:, k * P:(k + 1) * P], hT[:, half * 4 + k, t * P:(t + 1) * P], ident[:])
                        end(mm, "h2", i)
            pe.wait_ge(routed, 2)
            for i in range(3):
                o = start("pairs", i)
                src = r_sel[:, i, :, :, :] if i < 2 else r_g
                for t in range(DENSE):
                    mm = pe.transpose(o[:, t * P:(t + 1) * P],
                                      src[:, EARLY.index(GATHERED + t), :, :].rearrange("p h k -> p (h k)"), ident[:])
                end(mm, "pairs", i)

            for b in range(NB):
                last = max(j for j in jobs.number.values() if j % NB == b)
                pe.wait_ge(bank_free[b], last // NB + 1)
            pe.wait_ge(y_zero, 1)
            for b in range(2 * DENSE):
                pe.matmul(ps[:, b, :], r_y[:, 0:P], r_y[:, 0:BANK], start=True, stop=True)

            def spread_gates(m, s):
                pe.wait_ge(hot_ready, m + 1)
                pe.wait_ge(spread_kept, m + 1)
                for t in range(BATCH):
                    for part in range(PARTS):
                        mm = pe.matmul(ps[:, 6 + s, t * QKEYS:(t + 1) * QKEYS], hot_i[s][:, :, t],
                                       hot_j[s][part][:, :, t], start=(part == 0), stop=(part == PARTS - 1))
                mm.then_inc(spread_summed, 1)

            def dense_u(s, load):
                pe.wait_ge(u_loaded[s], load)
                for j in range(PAIR):
                    for k in range(KD):
                        mm = pe.matmul(ps[:, 4 + s, j * DT:(j + 1) * DT], u_ring[:, s, j, k, :],
                                       hT[:, k, GATHERED * P:T], start=(k == 0), stop=(k == KD - 1))
                mm.then_inc(u_done, 1)

            def dense_v(n, s, load, last=False):
                pe.wait_ge(v_loaded[s], load)
                pe.wait_ge(dense_coef, n + 1)
                for j in range(PAIR):
                    for t in range(DENSE):
                        for half in range(2):
                            mm = pe.matmul(ps[:, 2 * t + half, :],
                                           tmp[:, s, j * DT + t * P:j * DT + (t + 1) * P],
                                           v_ring[:, s, j, half * BANK:(half + 1) * BANK],
                                           start=False, stop=last and j == PAIR - 1, skip_group_check=True)
                mm.then_inc(v_done, 1)

            pe.sem_inc(spread_summed, 2)
            pe.sem_inc(v_done, 2)
            with pe.Fori(0, QSTEPS // 2) as turn:
                for s in range(2):
                    spread_gates(turn * 2 + s, s)
            dense_u(0, 16)
            for q in range(QUARTERS):
                with pe.Fori(0, QSTEPS // 2 - (q == QUARTERS - 1)) as turn:
                    for s in range(2):
                        n = turn * 2 + (q * QSTEPS + s)
                        pe.wait_ge(dense_gelu, n + 1)
                        dense_u(1 - s, (turn + (q * QSTEPS // 2 + s)) * 16 + 16)
                        if q + 1 < QUARTERS:
                            spread_gates(n + QSTEPS, s)
                        dense_v(n, s, (turn + q * QSTEPS // 2) * 16 + 16)
            pe.wait_ge(dense_gelu, STEPS - 1)
            dense_u(1, STEPS // 2 * 16)
            for n in (STEPS - 2, STEPS - 1):
                dense_v(n, n % 2, STEPS // 2 * 16, n == STEPS - 1)

        @block.vector
        def _(dve):
            xn_n = [0]

            def stream_norm(n, xn, t):
                dve.wait_ge(rr_done, NT * n + t + 1)
                dve.tensor_scalar(xn[:, t, :], xres[:, t, :], stat[:, 2, t:t + 1], None, ALU.mult).then_inc(xn_done, 1)

            def add_residual(name, n, xn, gate=None):
                for half in range(2):
                    for t in range(NT):
                        if half == 1 and t >= 1:
                            stream_norm(n, xn, t - 1)
                        o = full(dve, name, half, t)
                        x = xres[:, t, half * BANK:(half + 1) * BANK]
                        if gate is None:
                            taken(dve.tensor_tensor(x, x, o, ALU.add), name, half, t)
                        else:
                            i = half * NT + t
                            dve.tensor_tensor(tmp[:, i % 2, :], o, gate[:, half * BANK:(half + 1) * BANK],
                                              ALU.mult).then_inc(out_tmp, 1)
                            dve.wait_ge(out_tmp, i + 1)
                            taken(dve.tensor_tensor(x, x, tmp[:, i % 2, :], ALU.add), name, half, t)
                stream_norm(n, xn, NT - 1)

            def ada(n):
                arrived(dve, "ada", n)
                w = weights(KD, BANK, "ada", n)
                if n >= 1:
                    full(dve, "ada", n - 1)
                for k in range(KD):
                    if k == 0:
                        dve.tensor_scalar(ysum[:], w[:, k, :], csil[:, k:k + 1], None,
                                          ALU.mult).then_inc(ada_step, 1)
                    else:
                        dve.wait_ge(ada_step, KD * n + k)
                        dve.scalar_tensor_tensor(ysum[:], w[:, k, :], csil[:, k:k + 1], ysum[:],
                                                 ALU.mult, ALU.add).then_inc(ada_step, 1)

            def ada_out(n):
                part, half = ADA_ORDER[n] // 2, ADA_ORDER[n] % 2
                o = full(dve, "ada", n)
                if part in (2, 5):
                    g = gates[:, part // 3, half * BANK:(half + 1) * BANK]
                    taken(dve.tensor_tensor(g, o, g, ALU.add), "ada", n)
                else:
                    taken(dve.tensor_tensor(modcol[:, part, half * 4:half * 4 + 4], o[:, 0:4],
                                            col("ada_b", part * KD + half * 4, 4), ALU.add), "ada", n)

            for t in range(NT):
                stream_norm(0, a_xn, t)
            dve.wait_ge(const_loaded, 32)
            for k in range(0, KD, 2):
                o = full(dve, "xT_a", k)
                taken(dve.tensor_scalar(hT[:, k, :], o, col("a_g", k), None, ALU.mult), "xT_a", k)
            o = full(dve, "bias", 0)
            dve.wait_ge(row_loaded, 16 * 7)
            dve.tensor_tensor(bias_mask, o[0:SWA_H, 0:384], bias_mask, ALU.add).then_inc(bias_done, 1)
            dve.wait_ge(bias_done, 1)
            taken(dve.tensor_scalar(bias_mask, bias_mask, float(SWA_D ** 0.5), None, ALU.mult), "bias", 0)
            dve.wait_ge(silu_c, 1)
            dve.wait_ge(ret_loaded, 32)
            for n in range(12):
                if n < RET_H:
                    for i, dst in enumerate((a_q, a_k)):
                        e, o = full(dve, "a_in", n, 2 * i), full(dve, "a_in", n, 2 * i + 1)
                        u = 2 * n + i
                        if n == RET_H - 1:
                            dve.wait_ge(bias_kept, 16)
                        if u >= 1:
                            dve.wait_ge(qk_done, 2 * u)
                        cos, sin = trigA[:, 0, :], trigA[:, 1, :]
                        dve.tensor_tensor(dst[:, n, 0, :], e, cos, ALU.mult).then_inc(qk_tmp, 1)
                        dve.tensor_tensor(tmp[:, 0, :], o, sin, ALU.mult).then_inc(qk_tmp, 1)
                        taken(dve.tensor_tensor(dst[:, n, 1, :], o, cos, ALU.mult), "a_in", n, 2 * i + 1)
                        taken(dve.tensor_tensor(tmp[:, 1, :], e, sin, ALU.mult), "a_in", n, 2 * i)
                        dve.wait_ge(qk_tmp, 2 * (u + 1))
                        dve.tensor_tensor(dst[:, n, 0, :], dst[:, n, 0, :], tmp[:, 0, :],
                                          ALU.subtract).then_inc(qk_done, 1)
                        drained(dve, "a_in", n, 2 * i + 1)
                        drained(dve, "a_in", n, 2 * i)
                        dve.tensor_tensor(dst[:, n, 1, :], dst[:, n, 1, :], tmp[:, 1, :],
                                          ALU.add).then_inc(qk_done, 1)
                if 1 <= n <= ADA_IN_A:
                    ada_out(n - 1)
                if n < ADA_IN_A:
                    ada(n)
            for h in range(RET_H + 1):
                if h < RET_H:
                    for j in range(NT):
                        o = full(dve, "ret_s", h, j)
                        if h >= 2:
                            full(dve, "ret_o", h - 2, NT - 1)
                        taken(dve.tensor_tensor(a_sT[:, h % 2, j, 0:T - j * P], o[:, 0:T - j * P],
                                                decay[:, h, 0:T - j * P], ALU.mult), "ret_s", h, j)
                if h >= 1:
                    for i in range(NT):
                        u = (h - 1) * NT + i
                        dve.wait_ge(z_r, u + 1)
                        drained(dve, "a_in", 8 + h - 1, i)
                        o = full(dve, "ret_o", h - 1, i)
                        z = a_z[:, i, (h - 1) * BANK:h * BANK]
                        taken(dve.scalar_tensor_tensor(z, o, rstat[:, 2, u:u + 1], z, ALU.mult, ALU.mult),
                              "ret_o", h - 1, i)
            for f in range(0, RET_K, 2):
                o = full(dve, "zT_a", f)
                taken(dve.tensor_copy(a_oT[:, f, :], o), "zT_a", f)
            add_residual("a_out", 1, b_xn)
            if upto <= 1:
                for t in range(NT):
                    drained(dve, "a_out", 1, t)
                    drained(dve, "a_out", 0, t)
                    dve.sem_inc(out_ready, 1)
                return

            for k in range(0, KD, 2):
                o = full(dve, "xT_b", k)
                dve.tensor_scalar(b_kvT[:, k, :], o, col("kv_g", k), None, ALU.mult)
                taken(dve.tensor_scalar(hT[:, k, :], o, col("b_g", k), None, ALU.mult), "xT_b", k)
            dve.memset(b_kT[:], 0.0).then_inc(padded, 1)
            for t in range(NT):
                drained(dve, "kv", t)
            kview = b_kv[:, :, 0:P].rearrange("p t (g d) -> p t g d", d=SWA_D)
            ksq = tmp[:, 0, :].rearrange("p (t g d) -> p t g d", g=SWA_KV, d=SWA_D)
            dve.tensor_tensor(ksq, kview, kview, ALU.mult).then_inc(k_sq, 1)
            dve.wait_ge(k_sq, 1)
            kss = astat[:, 0, 0:8].rearrange("p (t g) -> p t g", g=SWA_KV)
            dve.tensor_reduce(kss, ksq, AX.X, ALU.add).then_inc(k_ss, 1)
            dve.wait_ge(k_r, 1)
            kr = astat[:, 2, 0:8].rearrange("p (t g) -> p t g", g=SWA_KV)
            for dup in range(2):
                dve.tensor_tensor(b_kn[:, :, :, dup, :], kview,
                                  kr.unsqueeze(3).to_broadcast([P, NT, SWA_KV, SWA_D]), ALU.mult).then_inc(k_n, 1)
            hn_at = [0, 0]

            def hn_reduce(n):
                key, heads, width = hn_units[n]
                b = n % 4
                sq = sqbuf(n)[:, 0:heads * width].rearrange("p (h d) -> p h d", d=width)
                dve.wait_ge(hn_sq, n + 1)
                if n >= 4:
                    dve.wait_ge(hn_r, n - 3)
                dve.tensor_reduce(hstat[:, b, 0, 0:heads], sq, AX.X, ALU.add).then_inc(hn_ss, 1)

            def hn_scale(n, dst):
                key, heads, width = hn_units[n]
                dve.wait_ge(hn_r, n + 1)
                o = full(dve, *key)
                r = hstat[:, n % 4, 2, 0:heads].unsqueeze(2).to_broadcast([P, heads, width])
                taken(dve.tensor_tensor(dst.rearrange("p (h d) -> p h d", d=width),
                                        o[:, 0:heads * width].rearrange("p (h d) -> p h d", d=width),
                                        r, ALU.mult), *key)

            def hn_run(n0, n1, dst, after=None):
                for n in range(n0, n1 + 2):
                    if n < n1:
                        hn_reduce(n)
                    if n >= n0 + 2:
                        hn_scale(n - 2, dst(n - 2))
                        if after is not None:
                            after(n - 2)

            def b_dst(n):
                key = hn_units[n][0]
                return b_qn[:, key[2], key[1] * BANK:(key[1] + 1) * BANK]

            hn_run(0, 4, b_dst)
            ada(ADA_IN_A)
            hn_run(4, 8, b_dst)
            dve.wait_ge(gate_bias, 16)
            for n in range(3):
                ada_out(ADA_IN_A + n)
                ada(ADA_IN_A + n + 1)
            for g in range(SWA_KV):
                o = full(dve, "kT", g)
                if g == 0:
                    dve.wait_ge(padded, 1)
                dve.tensor_scalar(b_kT[0:64, g, 0, :], o[0:64, :], col("k_g")[0:64], None, ALU.mult)
                taken(dve.tensor_scalar(b_kT[64:128, g, 1, :], o[64:128, :], col("k_g")[64:128], None,
                                        ALU.mult), "kT", g)
            for i in range(KD):
                o = full(dve, "qT", i)
                taken(dve.tensor_scalar(b_qT[:, i, :], o, col("q_g"), None, ALU.mult), "qT", i)
            ada_out(ADA_IN_A + 3)
            for i, (part, g) in enumerate(((1, "n1_g"), (4, "n2_g"))):
                for c in range(2):
                    drained(dve, "ada", (2 if i == 0 else 6) + c)
                dve.scalar_tensor_tensor(modcol[:, part, :], modcol[:, part, :], 1.0, col(g, 0, KD),
                                         ALU.add, ALU.mult).then_inc(mod_done, 1)
            dve.wait_ge(bias_loaded, 16)
            m_, nm_, d_, l_, es_, rl_ = (astat[:, i, :] for i in range(6))
            for n in range(NT + 1):
                if n < NT:
                    w0 = P if n == 0 else 0
                    s = b_s[n % 2]
                    for i in range(8):
                        o = full(dve, "swa_s", n, i)
                        if n >= 2:
                            full(dve, "swa_pT", n - 2, 7)
                        if n >= 1:
                            dve.wait_ge(sw_nm, 2 * n)
                        for m in range(2):
                            h = 2 * i + m
                            mm = dve.tensor_tensor_reduce(
                                out=s[:, h, w0:SWA_W], in0=o[:, m * SWA_W + w0:(m + 1) * SWA_W],
                                in1=b_bias[:, h, w0:SWA_W], scale=float(SWA_D ** -0.5), scalar=LOWEST,
                                op0=ALU.add, op1=ALU.max, accum_out=m_[:, h:h + 1])
                            if m == 0:
                                mm.then_inc(sw_s, 1)
                        mm.then_inc(bank_free[jobs("swa_s", n, i)[0]], 1)
                    for i in range(8):
                        drained(dve, "swa_s", n, i)
                    dve.wait_ge(sw_s, 8 * (n + 1))
                    dve.tensor_tensor(m_, m_, row("sinks"), ALU.max).then_inc(sw_m, 1)
                    dve.wait_ge(sw_m, n + 1)
                    if n >= 1:
                        dve.wait_ge(sw_e, SWA_H * n)
                        dve.wait_ge(sw_es, n)
                    dve.tensor_scalar(nm_, m_, -1.0, None, ALU.mult).then_inc(sw_nm, 1)
                    dve.tensor_tensor(d_, row("sinks"), m_, ALU.subtract).then_inc(sw_nm, 1)
                if n >= 1:
                    q = n - 1
                    for i in range(0, 8, 2):
                        o = full(dve, "swa_pT", q, i)
                        c0 = P if q == 0 else 0
                        dst = b_pT[:, 2 * i * SWA_W:(2 * i + 2) * SWA_W].rearrange("p (m c) -> p m c", m=2)
                        src = o.rearrange("p (m c) -> p m c", m=2)
                        if q >= 1:
                            full(dve, "swa_o", q - 1, SWA_KV - 1)
                        taken(dve.tensor_copy(dst[:, :, c0:SWA_W], src[:, :, c0:SWA_W]), "swa_pT", q, i)
                    for g in range(SWA_KV):
                        o = full(dve, "swa_o", q, g)
                        u = SWA_KV * q + g
                        if u >= 2:
                            dve.wait_ge(sw_zg, u - 1)
                        dve.wait_ge(sw_rl, q + 1)
                        ov = o.rearrange("p (h d) -> p h d", d=SWA_D)
                        tv = tmp[:, u % 2, :].rearrange("p (h d) -> p h d", d=SWA_D)
                        rl = rl_[:, 8 * g:8 * g + 8].unsqueeze(2).to_broadcast([P, 8, SWA_D])
                        dve.tensor_tensor(tv, ov, rl, ALU.mult).then_inc(bank_free[jobs("swa_o", q, g)[0]], 1)
                        drained(dve, "swa_o", q, g)
                        drained(dve, "b_in", 2 + g, q)
                        z = b_z[:, q, g * BANK:(g + 1) * BANK]
                        dve.tensor_tensor(z, tmp[:, u % 2, :], z, ALU.mult).then_inc(sw_zg, 1)
                if n < NT:
                    dve.wait_ge(sw_e, SWA_H * (n + 1))
                    dve.wait_ge(sw_es, n + 1)
                    dve.tensor_tensor(l_, l_, es_, ALU.add).then_inc(sw_l, 1)
                    dve.wait_ge(sw_l, n + 1)
                    if n >= 1:
                        dve.wait_ge(sw_zg, SWA_KV * n)
                    dve.reciprocal(rl_, l_).then_inc(sw_rl, 1)
            for k in range(0, KD, 2):
                o = full(dve, "zT_b", k)
                taken(dve.tensor_copy(b_zT[:, k, :], o), "zT_b", k)
            add_residual("b_out", 2, c_xn)
            if upto <= 2:
                for t in range(NT):
                    drained(dve, "b_out", 1, t)
                    drained(dve, "b_out", 0, t)
                    dve.sem_inc(out_ready, 1)
                return

            dve.wait_ge(mod_done, 2)
            for k in range(0, KD, 2):
                o = full(dve, "xT_c", k)
                taken(dve.tensor_scalar(hT[:, k, :], o, modcol[:, 1, k:k + 1], modcol[:, 0, k:k + 1],
                                        ALU.mult, ALU.add), "xT_c", k)
            for i in range(2):
                dve.tensor_tensor_reduce(out=ysum[:, i * ROPE:(i + 1) * ROPE], in0=row(f"lq{i + 1}"),
                                         in1=row(f"lk{i + 1}"), scale=1.0, scalar=0.0, op0=ALU.mult,
                                         op1=ALU.add, accum_out=lam[:, i:i + 1]).then_inc(lam_dve, 1)
            dve.wait_ge(lam_act, 1)
            dve.tensor_tensor(lam[:, 4:5], lam[:, 2:3], lam[:, 3:4], ALU.subtract).then_inc(lam_dve, 1)
            dve.wait_ge(lam_dve, 3)
            dve.tensor_scalar(lam[:, 5:6], lam[:, 4:5], LAMBDA_INIT, -1.0, ALU.add, ALU.mult).then_inc(lam_dve, 1)
            dve.tensor_scalar(lam[:, 6:7], col("sub_g"), 1.0 - LAMBDA_INIT, None, ALU.mult).then_inc(sub_done, 1)

            def c_dst(n):
                key = hn_units[n][0]
                if key[0] == "c_in":
                    return [c_ql, c_kvl, c_kpe, c_dq, c_dk][key[1]][:, key[2], :]
                return {"q_nope": c_qn, "q_rope": c_qr, "k_nope": c_kn}[key[0]][:, key[1], :]

            rope_n = [0, 0]

            def rope(src, dst, heads, gain, t):
                x = src[:, t, :].rearrange("p (h d) -> p h d", d=ROPE)
                y = dst(t).rearrange("p (h d) -> p h d", d=ROPE)
                g = gain.unsqueeze(1).to_broadcast([P, heads, ROPE])
                cos = trig[:, 0, t, :].unsqueeze(1).to_broadcast([P, heads, HALF])
                sin = trig[:, 1, t, :].unsqueeze(1).to_broadcast([P, heads, HALF])
                n = heads * HALF
                t0 = hot_j2[:, 0:n].rearrange("p (h d) -> p h d", d=HALF)
                t1 = hot_j2[:, 256:256 + n].rearrange("p (h d) -> p h d", d=HALF)
                r0 = rope_n[0]
                if r0:
                    dve.wait_ge(rope_t, r0)
                dve.tensor_tensor(x, x, g, ALU.mult).then_inc(rope_t, 1)
                dve.wait_ge(rope_t, r0 + 1)
                a, b = x[:, :, 0:HALF], x[:, :, HALF:ROPE]
                dve.tensor_tensor(y[:, :, 0:HALF], a, cos, ALU.mult).then_inc(rope_t, 1)
                dve.tensor_tensor(t0, b, sin, ALU.mult).then_inc(rope_t, 1)
                dve.tensor_tensor(y[:, :, HALF:ROPE], b, cos, ALU.mult).then_inc(rope_t, 1)
                dve.tensor_tensor(t1, a, sin, ALU.mult).then_inc(rope_t, 1)
                dve.wait_ge(rope_t, r0 + 5)
                dve.tensor_tensor(y[:, :, 0:HALF], y[:, :, 0:HALF], t0, ALU.subtract).then_inc(rope_t, 1)
                dve.tensor_tensor(y[:, :, HALF:ROPE], y[:, :, HALF:ROPE], t1, ALU.add).then_inc(rope_t, 1)
                rope_n[0] = r0 + 7

            def roped():
                dve.wait_ge(rope_t, rope_n[0])
                dve.sem_inc(rope_done, 1)

            def c_rope(n):
                key, heads, width = hn_units[n]
                if key[1] >= 2:
                    drained(dve, *key)
                    src, dst, gain = ((c_kpe, lambda t: c_kper[:, t, 0, :], "mk_g"),
                                      (c_dq, lambda t: c_dqr[:, t, :], "dq_g"),
                                      (c_dk, lambda t: c_dkr[:, t, :], "dk_g"))[key[1] - 2]
                    rope(src, dst, heads, row(gain), key[2])

            hn_run(HN_SWA, HN_PROJ, c_dst, c_rope)
            dve.memset(c_kpeT[:], 0.0).then_inc(padded, 1)
            dve.memset(c_kdT[:], 0.0).then_inc(padded, 1)
            for i in range(3):
                o = full(dve, "qlT", i)
                taken(dve.tensor_scalar(c_qlT[:, i, :], o, col("qlat_g", i), None, ALU.mult), "qlT", i)
            for i in range(2):
                o = full(dve, "kvlT", i)
                taken(dve.tensor_scalar(c_kvlT[:, i, :], o, col("kvlat_g", i), None, ALU.mult), "kvlT", i)
            dve.wait_ge(rope_t, rope_n[0])
            dve.tensor_copy(c_kper[:, :, 1, :], c_kper[:, :, 0, :]).then_inc(rope_t, 1)
            rope_n[0] += 1
            dve.wait_ge(rope_t, rope_n[0])
            dve.sem_inc(rope_done, 3)

            def q_rope(n):
                key, heads, width = hn_units[n]
                if key[0] == "q_rope":
                    drained(dve, *key)
                    rope(c_qr, lambda t: c_qrr[t], heads, row("mq_g"), key[1])

            hn_run(HN_PROJ, HN_PROJ + 8, c_dst, q_rope)
            roped()
            hn_run(HN_PROJ + 8, HN_ALL, c_dst)
            for h in range(DIFF_H):
                o = full(dve, "qdT", h)
                taken(dve.tensor_copy(c_qdT[:, h, :], o), "qdT", h)
            o = full(dve, "kpeT", 0)
            dve.wait_ge(padded, 3)
            dve.tensor_copy(c_kpeT[0:64, 0, :], o[0:64, :])
            taken(dve.tensor_copy(c_kpeT[64:128, 1, :], o[64:128, :]), "kpeT", 0)
            for h in range(MLA_H):
                o = full(dve, "qnT", h)
                taken(dve.tensor_scalar(c_qnT[:, h, :], o, col("mq_g"), None, ALU.mult), "qnT", h)
            for i in range(2):
                o = full(dve, "qrT", i)
                taken(dve.tensor_copy(c_qrT[:, i, :], o), "qrT", i)

            n_units = len(att_units)
            s_count = [0]
            nm_count = [0]

            def att_scores(n):
                kind, h, i = att_units[n]
                N = (i + 1) * P
                mask = causal[:, 384 - i * P:384 - i * P + N]
                for c in range(1 if kind == "m" else 2):
                    sl = (n if kind == "m" else 2 * n + c) % 8
                    o = full(dve, "att_s", n, c)
                    prev = n - (8 if kind == "m" else 4)
                    if kind == "d" and n < 20:
                        prev = 9 + 2 * (n - 16)
                    if prev >= 0:
                        full(dve, "att_pT", prev)
                    taken(dve.tensor_tensor_reduce(
                        out=c_s[:, sl, 0:N], in0=o[:, 0:N], in1=mask,
                        scale=float((NOPE + ROPE) ** -0.5 if kind == "m" else ROPE ** -0.5), scalar=LOWEST,
                        op0=ALU.add, op1=ALU.max, accum_out=astat[:, 6 * 0 + c, n % 16:n % 16 + 1]), "att_s", n, c)
                    drained(dve, "att_s", n, c)
                    if n >= 16:
                        dve.wait_ge(at_rl, n - 15)
                    dve.tensor_scalar(astat[:, 2 + c, n % 16:n % 16 + 1], astat[:, c, n % 16:n % 16 + 1], -1.0, None,
                                      ALU.mult).then_inc(at_nm, 1)

            def att_norm(n):
                kind, h, i = att_units[n]
                N = (i + 1) * P
                at = slice(n % 16, n % 16 + 1)
                if kind == "m":
                    dve.wait_ge(at_p, n + 1)
                    dve.reciprocal(astat[:, 6, at], astat[:, 4, at]).then_inc(at_rl, 1)
                else:
                    m = n - 16
                    dve.wait_ge(at_p, 16 + 2 * m + 2)
                    dve.reciprocal(astat[:, 6:8, at], astat[:, 4:6, at]).then_inc(at_rl, 1)
                    dve.wait_ge(at_rl, n + 1)
                    dve.wait_ge(lam_dve, 4)
                    p0, p1 = c_s[:, (2 * n) % 8, 0:N], c_s[:, (2 * n + 1) % 8, 0:N]
                    dve.tensor_scalar(p1, p1, astat[:, 7, at], lam[:, 5:6], ALU.mult, ALU.mult).then_inc(at_w, 1)
                    dve.wait_ge(at_w, 2 * m + 1)
                    dve.scalar_tensor_tensor(p0, p0, astat[:, 6, at], p1, ALU.mult, ALU.add).then_inc(at_w, 1)

            def att_clamp(n):
                kind, h, i = att_units[n]
                if kind == "d":
                    u = n - 16
                    o = full(dve, "att_o", n)
                    if u >= 2:
                        dve.wait_ge(od_sq, u - 1)
                    dve.tensor_scalar(tmp[:, u % 2, 0:P], o[:, 0:P], BIG, -BIG, ALU.min, ALU.max).then_inc(od_clamped, 1)

            def att_out(n):
                kind, h, i = att_units[n]
                at = slice(n % 16, n % 16 + 1)
                if kind == "m":
                    dve.wait_ge(at_rl, n + 1)
                    o = full(dve, "att_o", n)
                    taken(dve.tensor_scalar(c_om[:, i, h * P:(h + 1) * P], o[:, 0:P], astat[:, 6, at], None,
                                            ALU.mult), "att_o", n)
                else:
                    m = n - 16
                    dve.wait_ge(od_r, m + 1)
                    dve.scalar_tensor_tensor(rstat[:, 2, m:m + 1], rstat[:, 0, m:m + 1], SUM_MAX, rstat[:, 2, m:m + 1],
                                             ALU.is_le, ALU.mult).then_inc(od_rr, 1)
                    dve.wait_ge(od_rr, m + 1)
                    o = full(dve, "att_o", n)
                    taken(dve.tensor_scalar(c_od[:, i, h * P:(h + 1) * P], o[:, 0:P], rstat[:, 2, m:m + 1], None,
                                            ALU.mult), "att_o", n)

            for n in range(n_units + 4):
                if n < n_units:
                    att_scores(n)
                if 1 <= n <= n_units:
                    att_norm(n - 1)
                if 3 <= n < n_units + 3:
                    att_clamp(n - 3)
                if n >= 4:
                    att_out(n - 4)
            for k in range(KD):
                o = full(dve, "mT", k)
                if k < 4:
                    taken(dve.tensor_copy(c_mT[:, k, :], o), "mT", k)
                else:
                    dve.wait_ge(sub_done, 1)
                    taken(dve.tensor_scalar(c_mT[:, k, :], o, lam[:, 6:7], None, ALU.mult), "mT", k)
            for n in range(4):
                drained(dve, "ada", ADA_IN_A + n)
            add_residual("c_out", 3, d_xn, gates[:, 0, :])
            if upto <= 3:
                for t in range(NT):
                    drained(dve, "c_out", 1, t)
                    drained(dve, "c_out", 0, t)
                    dve.sem_inc(out_ready, 1)
                return

            for k in range(0, KD, 2):
                o = full(dve, "xT_d", k)
                taken(dve.tensor_scalar(hT[:, k, :], o, modcol[:, 4, k:k + 1], modcol[:, 3, k:k + 1],
                                        ALU.mult, ALU.add), "xT_d", k)

            class Steps:

                def __init__(self, semaphore, before=0, hold=None):
                    self.semaphore, self.before, self.done, self.hold = semaphore, before, 0, hold

                def __call__(self, ins_):
                    ins_.then_inc(self.semaphore, 1)
                    self.done += 1

                def settle(self):
                    dve.wait_ge(self.semaphore, self.before + self.done)
                    if self.hold is not None:
                        self(dve.tensor_copy(self.hold, iota[:, 0:1]))

            def top16(step, src, scr, values, index):
                n = len(src)
                for a in range(n):
                    step(dve.max(values[a][:, 0:8], src[a]))
                step.settle()
                for a in range(n):
                    step(dve.max_index(index[a][:, 0:8], values[a][:, 0:8], src[a]))
                    step(dve.match_replace(scr[a], values[a][:, 0:8], src[a], LOWEST))
                step.settle()
                for a in range(n):
                    step(dve.max(values[a][:, 8:16], scr[a]))
                step.settle()
                for a in range(n):
                    step(dve.max_index(index[a][:, 8:16], values[a][:, 8:16], scr[a]))
                step.settle()

            def rank_keys(step, r, n, src):
                both = [(p, t) for p in range(2) for t in range(n)]
                top16(step, src, [r.scr[:, a, :] for a in range(2 * n)], [r.v[:, p, t, :] for p, t in both],
                      [r.idx[:, p, t, :] for p, t in both])
                step(dve.tensor_copy(r.idxf[:], r.idx[:]))
                wide = [P, n, TOPK, TOPK]
                step(dve.tensor_tensor(r.cand[:].rearrange("p t (a b) -> p t a b", b=TOPK),
                                       r.v[:, 0].unsqueeze(3).to_broadcast(wide),
                                       r.v[:, 1].unsqueeze(2).to_broadcast(wide), ALU.add))
                step.settle()

            def rank_pairs(step, r, n, sums, numbers):
                wide = [P, n, TOPK, TOPK]
                pos = r.pos[:, 0, :].rearrange("p (t k) -> p t k", k=TOPK)
                top16(step, [r.cand[:, t, :] for t in range(n)], [r.cscr[:, t, :] for t in range(n)],
                      [sums[:, t, :] for t in range(n)], [pos[:, t, :] for t in range(n)])
                step(dve.tensor_scalar(r.pos[:, 1, :], r.pos[:, 0, :], 4, None, ALU.logical_shift_right))
                step(dve.tensor_scalar(r.pos[:, 2, :], r.pos[:, 0, :], 15, None, ALU.bitwise_and))
                step.settle()
                step(dve.tensor_copy(r.posf[:], r.pos[:, 1:3, :]))
                step.settle()
                for a in range(2):
                    step(dve.tensor_tensor(r.eq[:], r.posf[:, a, :].unsqueeze(2).to_broadcast([P, n * TOPK, TOPK]),
                                           iota[:, 0:TOPK].unsqueeze(1).to_broadcast([P, n * TOPK, TOPK]),
                                           ALU.is_equal))
                    step.settle()
                    eq = r.eq[:].rearrange("p (t k) a -> p t k a", k=TOPK)
                    step(dve.tensor_tensor(eq, eq, r.idxf[:, a].unsqueeze(2).to_broadcast(wide), ALU.mult))
                    step.settle()
                    step(dve.tensor_reduce(numbers[a], eq, AX.X, ALU.add))
                    step.settle()

            step = Steps(route)
            for h in range(PEER_H):
                for p in range(2):
                    drained(dve, "peer_s", 2 * h + p)
                rank_keys(step, early, NE, [d_s[:, (2 * h + p) % 4, t, :] for p in range(2) for t in EARLY])
                dve.sem_inc(ranked, 1)
                rank_pairs(step, early, NE, r_g[:, :, h, :], [r_sel[:, a, :, h, :] for a in range(2)])
            full(dve, "pqT", 2 * PEER_H - 1)
            by_head = [P, NE * PEER_H, TOPK]
            g_all = r_g[:].rearrange("p t h k -> p (t h) k")
            choices = lambda v: v[:, 0, :, :].rearrange("p h k -> p (h k)")
            step(dve.tensor_reduce(r_sum[:, 0, :], g_all, AX.X, ALU.max))
            step(dve.scalar_tensor_tensor(eidx[:, 0:SLOTS], choices(r_sel[:, 0]), float(NKEYS), choices(r_sel[:, 1]),
                                          ALU.mult, ALU.add))
            step.settle()
            dve.sem_inc(gathering, 1)
            step(dve.tensor_tensor(g_all, g_all, r_sum[:, 0, :].unsqueeze(2).to_broadcast(by_head), ALU.subtract))
            step.settle()
            dve.sem_inc(routed, 1)
            dve.memset(r_y, 0.0).then_inc(y_zero, 1)
            dve.wait_ge(route_e, 1)
            step(dve.tensor_reduce(r_sum[:, 0, :], g_all, AX.X, ALU.add))
            step.settle()
            step(dve.reciprocal(r_sum[:, 1, :], r_sum[:, 0, :]))
            step.settle()
            step(dve.tensor_tensor(g_all, g_all, r_sum[:, 1, :].unsqueeze(2).to_broadcast(by_head), ALU.mult))
            step.settle()
            dve.sem_inc(routed, 1)
            step(dve.tensor_copy(g_kept[:, 0:SLOTS], choices(r_g)))
            for i, dst in enumerate((iT, jT)):
                o = full(dve, "pairs", i)
                taken(dve.tensor_copy(dst, o[:, 0:DT]), "pairs", i)
            o = full(dve, "pairs", 2)
            split = Steps(gate_part)
            split(dve.tensor_copy(gT[0], o[:, 0:DT]))
            split.settle()
            split(dve.tensor_tensor(g_rest[0], o[:, 0:DT], gT[0], ALU.subtract))
            split.settle()
            split(dve.tensor_copy(gT[1], g_rest[0]))
            split.settle()
            split(dve.tensor_tensor(g_rest[1], g_rest[0], gT[1], ALU.subtract))
            split.settle()
            taken(dve.tensor_copy(gT[2], g_rest[1]), "pairs", 2)
            for i in range(3):
                drained(dve, "pairs", i)
            step.settle()
            dve.wait_ge(iota_ready, 1)

            def one_hots(q, m, t0, s):
                of = lambda v, n: v[:, bass.ds(t0, BATCH)].unsqueeze(1).to_broadcast([P, n, BATCH])
                dve.wait_ge(spread_summed, m + 1)
                dve.tensor_tensor(hot_j[s][2], of(jT, QKEYS), wide_iota[:, q * QKEYS:(q + 1) * QKEYS, :],
                                  ALU.is_equal).then_inc(hot_step, 1)
                dve.tensor_tensor(hot_i[s], of(iT, NKEYS), wide_iota, ALU.is_equal)
                dve.wait_ge(hot_step, m + 1)
                for part in range(PARTS):
                    last = dve.tensor_tensor(hot_j[s][part], hot_j[s][2], of(gT[part], QKEYS), ALU.mult)
                last.then_inc(hot_ready, 1)

            with dve.Fori(0, QSTEPS // 2) as turn:
                for s in range(2):
                    one_hots(0, turn * 2 + s, turn * (2 * BATCH) + s * BATCH, s)

            def gather_u(u, block):
                turn = block + 2 * u * QSTEPS
                for r in range(2 * GATHER):
                    dve.wait_ge(g_loaded[r], turn * 16 + 16)
                    dve.tensor_tensor_reduce(out=experts[:, r, :], in0=experts[:, r, :], in1=d_h2[:, u, :],
                                             scale=1.0, scalar=0.0, op0=ALU.mult, op1=ALU.add,
                                             accum_out=r_astage[:, r:r + 1]).then_inc(g_used[r // GATHER], 1)
                for half in range(2):
                    dve.wait_ge(g_used[half], turn * GATHER + 2 * GATHER)
                dve.tensor_copy(r_a[:, bass.ds(block * 2 * GATHER, 2 * GATHER)], r_astage[:]).then_inc(g_dve, 1)
                dve.wait_ge(g_dve, block + (u * QSTEPS + 1))

            def gather_v(u, block):
                turn = block + (2 * u + 1) * QSTEPS
                dve.tensor_copy(r_cstage[:], r_coef[:, bass.ds(block * 2 * GATHER, 2 * GATHER)]).then_inc(y_step, 1)
                base = (block + u * QSTEPS) * (2 * GATHER + 1)
                for half in range(2):
                    for r in range(half * GATHER, (half + 1) * GATHER):
                        dve.wait_ge(y_step, base + r + 1)
                        dve.wait_ge(g_loaded[r], turn * 16 + 16)
                        dve.scalar_tensor_tensor(r_y, experts[:, r, :], r_cstage[:, r:r + 1], r_y,
                                                 ALU.mult, ALU.add).then_inc(y_step, 1)
                    dve.wait_ge(y_step, base + (half + 1) * GATHER + 1)
                    dve.sem_inc(g_used[half], GATHER)

            LATE_KEYS, LATE_PAIRS = 19, 30

            def late_keys(h):
                step = Steps(late_step, h * (LATE_KEYS + LATE_PAIRS), late_hold)
                step(dve.tensor_copy(late_stage[:], late_keep[:, bass.ds(h * 2, 2), :]))
                step.settle()
                rank_keys(step, late, 1, [late_stage[:, p, :] for p in range(2)])
                assert step.done == LATE_KEYS, step.done

            def late_pairs(h):
                step = Steps(late_step, h * (LATE_KEYS + LATE_PAIRS) + LATE_KEYS, late_hold)
                rank_pairs(step, late, 1, late_g, [late_out[:, a, :].unsqueeze(1) for a in range(2)])
                at = bass.ds(h * TOPK, TOPK)
                step(dve.tensor_copy(g_kept[:, SLOTS:2 * SLOTS][:, at], late_g[:, 0, :]))
                for a in range(2):
                    step(dve.tensor_copy(late_sel[a][:, at], late_out[:, a, :]))
                step.settle()
                assert step.done == LATE_PAIRS, step.done

            def late_softmax():
                step = Steps(late_step, PEER_H * (LATE_KEYS + LATE_PAIRS))
                g = g_kept[:, SLOTS:2 * SLOTS].rearrange("p (h k) -> p h k", k=TOPK)
                by_head = [P, PEER_H, TOPK]
                step(dve.scalar_tensor_tensor(eidx[:, SLOTS:2 * SLOTS], late_sel[0], float(NKEYS), late_sel[1],
                                              ALU.mult, ALU.add))
                step(dve.tensor_reduce(late_sum[:, 0, :], g, AX.X, ALU.max))
                step.settle()
                dve.sem_inc(gathering, 1)
                step(dve.tensor_tensor(g, g, late_sum[:, 0, :].unsqueeze(2).to_broadcast(by_head), ALU.subtract))
                step.settle()
                dve.sem_inc(late_done, 1)
                dve.wait_ge(route_e, 2)
                step(dve.tensor_reduce(late_sum[:, 0, :], g, AX.X, ALU.add))
                step.settle()
                step(dve.reciprocal(late_sum[:, 1, :], late_sum[:, 0, :]))
                step.settle()
                step(dve.tensor_tensor(g, g, late_sum[:, 1, :].unsqueeze(2).to_broadcast(by_head), ALU.mult))
                step.settle()

            for q in range(QUARTERS):
                u, phase = q // 2, q % 2
                dve.wait_ge(spread_kept, (q + 1) * QSTEPS + 2)
                if q == 0:
                    dve.wait_ge(late_kept, 1)
                with dve.Fori(0, QSTEPS // 2) as turn:
                    for s in range(2):
                        n = turn * 2 + (q * QSTEPS + s)
                        dve.wait_ge(dense_gelu, n + 2)
                        gated = tmp[:, s, :].rearrange("p (j t) -> p j t", t=DT)
                        dve.tensor_tensor(gated, gated, spread[q % 2][:, bass.ds(turn * (2 * PAIR) + s * PAIR, PAIR), :],
                                          ALU.mult).then_inc(dense_coef, 1)
                        if q + 1 < QUARTERS:
                            one_hots(q + 1, n + QSTEPS, turn * (2 * BATCH) + s * BATCH, s)
                        if q == 0:
                            (late_keys, late_pairs)[s](turn)
                        if phase == 0:
                            gather_u(u, turn * 2 + s)
                        else:
                            gather_v(u, turn * 2 + s)
                if q == 0:
                    late_softmax()
                if phase == 0:
                    dve.sem_inc(a_ready, 1)
                    dve.wait_ge(gelu_done, u + 1)
                    dve.tensor_tensor(r_coef[:], r_coef[:], g_kept[:, u * SLOTS:(u + 1) * SLOTS],
                                      ALU.mult).then_inc(coef_done, 1)
                    dve.memset(r_y, 0.0).then_inc(y_zero, 1)
                    dve.wait_ge(y_zero, u + 2)
                    dve.wait_ge(coef_done, u + 1)
                else:
                    dve.tensor_tensor(r_y, r_y, gates[:, 1, :], ALU.mult).then_inc(out_tmp, 1)
                    dve.wait_ge(out_tmp, 8 + u + 1)
                    dve.tensor_tensor(xres[:, u, :], xres[:, u, :], r_y, ALU.add).then_inc(out_ready, 1)
                    dve.wait_ge(out_ready, u + 1)
            dve.wait_ge(v_done, STEPS + 2)
            for t in range(DENSE):
                for half in range(2):
                    i = 2 * t + half
                    at = slice(half * BANK, (half + 1) * BANK)
                    dve.tensor_tensor(tmp[:, i % 2, :], ps[:, i, :], gates[:, 1, at], ALU.mult).then_inc(out_tmp, 1)
                    dve.wait_ge(out_tmp, 8 + GATHERED + i + 1)
                    x = xres[:, GATHERED + t, at]
                    add = dve.tensor_tensor(x, x, tmp[:, i % 2, :], ALU.add)
                    add.then_inc(out_half, 1)
                    dve.wait_ge(out_half, i + 1)
                dve.sem_inc(out_ready, 1)

        @block.scalar
        def _(act):
            act.dma_start(rows[:], ins["rows"]).then_inc(row_loaded, 16)
            act.dma_start(iota[:], ins["iota"]).then_inc(row_loaded, 16)
            act.dma_start(causal, ins["causal"]).then_inc(row_loaded, 16)
            act.dma_start(trig[:], ins["trig"]).then_inc(row_loaded, 16)
            act.dma_start(bias_w, ins["rel_bias"]).then_inc(row_loaded, 16)
            act.dma_start(bias_hot, ins["bias_hot"]).then_inc(row_loaded, 16)
            act.dma_start(bias_mask, ins["bias_mask"]).then_inc(row_loaded, 16)

            def stream_squares(n, xn, ready):
                for t in range(NT):
                    ready(t)
                    act.activation(xn[:, t, :], xres[:, t, :], ACT.Square,
                                   accum_out=stat[:, 0, t:t + 1]).then_inc(sq_done, 1)

            stream_squares(0, a_xn, lambda t: act.wait_ge(x_loaded[t], 16))
            act.wait_ge(const_loaded, 32)
            for k in range(1, KD, 2):
                o = full(act, "xT_a", k)
                taken(act.activation(hT[:, k, :], o, ACT.Copy, scale=col("a_g", k)), "xT_a", k)
            act.activation(csil[:], col("c", 0, KD), ACT.Silu).then_inc(silu_c, 1)
            drained(act, "bias", 0)
            act.dma_start(ins["bias_rows"].rearrange("p h u -> h p u"),
                          bias_mask.unsqueeze(1).to_broadcast([SWA_H, P, 384])).then_inc(bias_kept, 16)
            for n in range(RET_H, 12):
                for t in range(NT):
                    o = full(act, "a_in", n, t)
                    if n < 2 * RET_H:
                        taken(act.activation(a_v[:, t, (n - 4) * BANK:(n - 3) * BANK], o, ACT.Copy), "a_in", n, t)
                    else:
                        taken(act.activation(a_z[:, t, (n - 8) * BANK:(n - 7) * BANK], o, ACT.Silu), "a_in", n, t)
            for h in range(RET_H):
                for i in range(NT):
                    u = h * NT + i
                    o = full(act, "ret_o", h, i)
                    if u >= 2:
                        act.wait_ge(z_sq, u - 1)
                    elif u == 0:
                        act.wait_ge(qk_done, 16)
                    act.activation(tmp[:, u % 2, :], o, ACT.Square, accum_out=rstat[:, 0, u:u + 1]).then_inc(z_sq, 1)
            for f in range(1, RET_K, 2):
                o = full(act, "zT_a", f)
                taken(act.activation(a_oT[:, f, :], o, ACT.Copy), "zT_a", f)
            if upto <= 1:
                return

            def from_out(name):
                def ready(t):
                    drained(act, name, 0, t)
                    drained(act, name, 1, t)
                return ready

            stream_squares(1, b_xn, from_out("a_out"))
            for k in range(1, KD, 2):
                o = full(act, "xT_b", k)
                act.activation(b_kvT[:, k, :], o, ACT.Copy, scale=col("kv_g", k))
                taken(act.activation(hT[:, k, :], o, ACT.Copy, scale=col("b_g", k)), "xT_b", k)
            act.wait_ge(bias_kept, 16)
            for f in range(RET_K):
                drained(act, "zT_a", f)
            act.dma_start(b_bias, bass.AP(ins["bias_rows"].tensor, P - 1, [[SWA_H * 384 - 1, P], [384, SWA_H], [1, SWA_W]]))\
               .then_inc(bias_loaded, 16)
            for t in range(NT):
                o = full(act, "kv", t)
                taken(act.activation(b_kv[:, t, :], o[:, 0:256], ACT.Copy), "kv", t)

            def hn_square(n):
                key, heads, width = hn_units[n]
                o = full(act, *key)
                if n >= 2:
                    act.wait_ge(hn_ss, n - 1)
                act.activation(sqbuf(n)[:, 0:heads * width], o[:, 0:heads * width], ACT.Square).then_inc(hn_sq, 1)

            act.wait_ge(k_ss, 1)
            for n in range(HN_SWA):
                hn_square(n)
            for n in range(2, 4):
                for t in range(NT):
                    o = full(act, "b_in", n, t)
                    taken(act.activation(b_z[:, t, (n - 2) * BANK:(n - 1) * BANK], o, ACT.Silu), "b_in", n, t)
            m_, nm_, d_, l_, es_, rl_ = (astat[:, i, :] for i in range(6))
            for n in range(NT + 1):
                if n >= 1:
                    q = n - 1
                    for i in range(1, 8, 2):
                        o = full(act, "swa_pT", q, i)
                        c0 = P if q == 0 else 0
                        dst = b_pT[:, 2 * i * SWA_W:(2 * i + 2) * SWA_W].rearrange("p (m c) -> p m c", m=2)
                        src = o.rearrange("p (m c) -> p m c", m=2)
                        if q >= 1:
                            full(act, "swa_o", q - 1, SWA_KV - 1)
                        taken(act.activation(dst[:, :, c0:SWA_W], src[:, :, c0:SWA_W], ACT.Copy), "swa_pT", q, i)
                if n < NT:
                    w0 = P if n == 0 else 0
                    act.wait_ge(sw_nm, 2 * (n + 1))
                    if n >= 1:
                        act.wait_ge(sw_rl, n)
                    for h in range(SWA_H):
                        s = b_s[n % 2][:, h, w0:SWA_W]
                        act.activation(s, s, ACT.Exp, bias=nm_[:, h:h + 1], accum_out=l_[:, h:h + 1]).then_inc(sw_e, 1)
                    act.activation(es_, d_, ACT.Exp).then_inc(sw_es, 1)
            for k in range(1, KD, 2):
                o = full(act, "zT_b", k)
                taken(act.activation(b_zT[:, k, :], o, ACT.Copy), "zT_b", k)
            if upto <= 2:
                return

            stream_squares(2, c_xn, from_out("b_out"))
            act.wait_ge(mod_done, 2)
            for k in range(1, KD, 2):
                o = full(act, "xT_c", k)
                taken(act.activation(hT[:, k, :], o, ACT.Identity, scale=modcol[:, 1, k:k + 1],
                                     bias=modcol[:, 0, k:k + 1]), "xT_c", k)
            act.wait_ge(lam_dve, 2)
            act.activation(lam[:, 2:4], lam[:, 0:2], ACT.Exp).then_inc(lam_act, 1)
            for n in range(HN_SWA, HN_PROJ):
                hn_square(n)
            for t in range(NT):
                o = full(act, "c_in", 5, t)
                taken(act.activation(c_dv[:, t, :], o, ACT.Copy), "c_in", 5, t)
            for n in range(HN_PROJ, HN_PROJ + 8):
                hn_square(n)
            for t in range(NT):
                hn_square(HN_PROJ + 8 + t)
                o = full(act, "v_up", t)
                taken(act.activation(c_v[:, t, :], o, ACT.Copy), "v_up", t)
            act.wait_ge(padded, 3)
            for h in range(DIFF_H):
                o = full(act, "kdT", h)
                act.activation(c_kdT[0:64, h, 0, :], o[0:64, :], ACT.Copy)
                taken(act.activation(c_kdT[64:128, h, 1, :], o[64:128, :], ACT.Copy), "kdT", h)
            for h in range(MLA_H):
                o = full(act, "knT", h)
                taken(act.activation(c_knT[:, h, :], o, ACT.Copy, scale=col("mk_g")), "knT", h)
            n_units = len(att_units)
            for n in range(n_units + 3):
                if n < n_units:
                    kind, h, i = att_units[n]
                    N = (i + 1) * P
                    for c in range(1 if kind == "m" else 2):
                        sl = (n if kind == "m" else 2 * n + c) % 8
                        act.wait_ge(at_nm, (n if n < 16 else 16 + 2 * (n - 16)) + c + 1)
                        s = c_s[:, sl, 0:N]
                        at = slice(n % 16, n % 16 + 1)
                        act.activation(s, s, ACT.Exp, bias=astat[:, 2 + c, at],
                                       accum_out=astat[:, 4 + c, at]).then_inc(at_p, 1)
                if 2 <= n < n_units + 2:
                    m = n - 2
                    kind, h, i = att_units[m]
                    N = (i + 1) * P
                    o = full(act, "att_pT", m)
                    if m >= 8:
                        full(act, "att_o", m - 8)
                    taken(act.activation(c_pT[:, m % 8, 0:N], o[:, 0:N], ACT.Copy), "att_pT", m)
                if n >= 3:
                    kind, h, i = att_units[n - 3]
                    if kind == "d":
                        u = n - 3 - 16
                        act.wait_ge(od_clamped, u + 1)
                        act.activation(tmp[:, u % 2, 0:P], tmp[:, u % 2, 0:P], ACT.Square, scale=SQ_SCALE,
                                       accum_out=rstat[:, 0, u:u + 1]).then_inc(od_sq, 1)
            if upto <= 3:
                return

            stream_squares(3, d_xn, from_out("c_out"))
            for k in range(1, KD, 2):
                o = full(act, "xT_d", k)
                taken(act.activation(hT[:, k, :], o, ACT.Identity, scale=modcol[:, 4, k:k + 1],
                                     bias=modcol[:, 3, k:k + 1]), "xT_d", k)
            for f in range(2 * PEER_H + 1):
                if f < 2 * PEER_H:
                    o = full(act, "pqT", f)
                    if f >= 2:
                        full(act, "peer_s", f - 2)
                    taken(act.activation(d_qT[:, f % 2, :], o, ACT.Copy), "pqT", f)
                if f >= 1:
                    g = f - 1
                    o = full(act, "peer_s", g)
                    if g >= 4:
                        act.wait_ge(ranked, g // 2 - 1)
                    act.activation(late_s[:, g, :], o[:, LATE * P:(LATE + 1) * P], ACT.Copy)
                    taken(act.activation(d_s[:, g % 4, :, :].rearrange("p t n -> p (t n)"), o, ACT.Copy), "peer_s", g)
                if f == 2 * PEER_H - 2:
                    for i in range(GATHERED * 2):
                        o = full(act, "h2", i)
                        taken(act.activation(d_h2[:, i // 2, (i % 2) * BANK:(i % 2 + 1) * BANK], o, ACT.Copy), "h2", i)
            for b in range(2):
                drained(act, "peer_s", 2 * PEER_H - 1 - b)
            full(act, "pqT", 2 * PEER_H - 1)
            act.activation(late_keep[:], late_s[:], ACT.Copy).then_inc(late_kept, 1)
            act.activation(wide_iota, iota[:].unsqueeze(2).to_broadcast([P, NKEYS, BATCH]), ACT.Copy)\
               .then_inc(iota_ready, 1)
            act.wait_ge(routed, 1)
            g_flat = r_g[:].rearrange("p t h k -> p (t h k)")
            act.activation(g_flat, g_flat, ACT.Exp).then_inc(route_e, 1)

            def keep_gates(q, m, t0, s):
                act.wait_ge(spread_summed, m + 3)
                act.activation(spread[q % 2][:, :, bass.ds(t0, BATCH)],
                               ps[:, 6 + s, :].rearrange("p (t j) -> p j t", j=QKEYS), ACT.Copy).then_inc(spread_kept, 1)

            act.sem_inc(spread_kept, 2)
            act.sem_inc(dense_gelu, 1)
            with act.Fori(0, QSTEPS // 2) as turn:
                for s in range(2):
                    keep_gates(0, turn * 2 + s, turn * (2 * BATCH) + s * BATCH, s)
            for q in range(QUARTERS):
                if q >= 1:
                    act.wait_ge(dense_coef, q * QSTEPS)
                with act.Fori(0, QSTEPS // 2) as turn:
                    for s in range(2):
                        n = turn * 2 + (q * QSTEPS + s)
                        act.wait_ge(u_done, n + 1)
                        act.wait_ge(v_done, n + 1)
                        act.activation(tmp[:, s, :], ps[:, 4 + s, :], ACT.Gelu).then_inc(dense_gelu, 1)
                        if q + 1 < QUARTERS:
                            keep_gates(q + 1, n + QSTEPS, turn * (2 * BATCH) + s * BATCH, s)
                if q == 0:
                    act.wait_ge(late_done, 1)
                    act.activation(g_kept[:, SLOTS:2 * SLOTS], g_kept[:, SLOTS:2 * SLOTS], ACT.Exp).then_inc(route_e, 1)
                if q % 2 == 0:
                    act.wait_ge(a_ready, q // 2 + 1)
                    if q >= 2:
                        act.wait_ge(out_ready, q // 2)
                    act.activation(r_coef[:], r_a[:], ACT.Gelu).then_inc(gelu_done, 1)

        @block.gpsimd
        def _(pool):
            pool.memset(ones[:], 1.0).then_inc(made, 1)
            pool.memset(minus_half[:], -0.5).then_inc(made, 1)
            pool.wait_ge(made, 2)

            def rsqrt(ss, ms, r, n, width, ms_sem, ms_at, r_sem):
                pool.tensor_scalar(ms, ss, 1.0 / width, EPS, ALU.mult, ALU.add).then_inc(ms_sem, 1)
                pool.wait_ge(ms_sem, ms_at)
                pool.tensor_tensor(r, ms, minus_half[:, 0:n], ALU.pow).then_inc(r_sem, 1)

            def stream_rsqrt(n):
                for t in range(NT):
                    pool.wait_ge(sq_done, NT * n + t + 1)
                    if n >= 1:
                        pool.wait_ge(xn_done, NT * (n - 1) + t + 1)
                    at = slice(t, t + 1)
                    rsqrt(stat[:, 0, at], stat[:, 1, at], stat[:, 2, at], 1, D, ms_done, NT * n + t + 1, rr_done)

            def hn_rsqrt(n):
                key, heads, width = hn_units[n]
                pool.wait_ge(hn_ss, n + 1)
                if n >= 4:
                    drained(pool, *hn_units[n - 4][0])
                s = hstat[:, n % 4, :, 0:heads]
                rsqrt(s[:, 0, :], s[:, 1, :], s[:, 2, :], heads, width, hn_ms, n + 1, hn_r)

            stream_rsqrt(0)
            for u in range(RET_H * NT):
                pool.wait_ge(z_sq, u + 1)
                rsqrt(rstat[:, 0, u:u + 1], rstat[:, 1, u:u + 1], rstat[:, 2, u:u + 1], 1, BANK, z_ms, u + 1, z_r)
            if upto <= 1:
                return
            stream_rsqrt(1)
            pool.wait_ge(k_ss, 1)
            rsqrt(astat[:, 0, 0:8], astat[:, 1, 0:8], astat[:, 2, 0:8], 8, SWA_D, k_ms, 1, k_r)
            for n in range(HN_SWA):
                hn_rsqrt(n)
            if upto <= 2:
                return
            stream_rsqrt(2)
            for n in range(HN_SWA, HN_ALL):
                hn_rsqrt(n)
            for u in range(DIFF_H * NT):
                pool.wait_ge(od_sq, u + 1)
                if u == 0:
                    drained(pool, "ret_o", RET_H - 1, NT - 1)
                pool.tensor_scalar(rstat[:, 1, u:u + 1], rstat[:, 0, u:u + 1], SUM_MAX, SQ_SCALE ** -2 / P,
                                   ALU.min, ALU.mult).then_inc(od_ms, 1)
                pool.wait_ge(od_ms, 2 * u + 1)
                pool.tensor_scalar(rstat[:, 1, u:u + 1], rstat[:, 1, u:u + 1], EPS, None, ALU.add).then_inc(od_ms, 1)
                pool.wait_ge(od_ms, 2 * u + 2)
                pool.tensor_tensor(rstat[:, 2, u:u + 1], rstat[:, 1, u:u + 1], minus_half[:, 0:1], ALU.pow).then_inc(od_r, 1)
            if upto <= 3:
                return
            stream_rsqrt(3)

            pool.memset(absorb[:], 0.0).then_inc(g_absorb, 1)
            pool.wait_ge(g_absorb, 1)
            for half in range(2):
                pool.sem_inc(g_used[half], GATHER)
            blocks = SLOTS // (2 * GATHER)
            full(pool, "pqT", 2 * PEER_H - 1)
            for t in range(GATHERED):
                pool.wait_ge(gathering, t + 1)
                for phase, table in enumerate((ins["peer_u"], ins["peer_v"])):
                    with pool.Fori(0, blocks) as b:
                        turn = b + (2 * t + phase) * blocks
                        for half in range(2):
                            pool.wait_ge(g_used[half], turn * GATHER + GATHER)
                            at = b * 2 * GATHER + half * GATHER
                            pool.tensor_copy(estage[:, half, :], eidx[:, bass.ds(at + t * SLOTS, GATHER)]).then_inc(g_staged, 1)
                            pool.wait_ge(g_staged, turn * 2 + half + 1)
                            pool.tensor_tensor(absorb[:], absorb[:], absorb[:], ALU.mult).then_inc(g_absorb, 1)
                            for r in range(GATHER):
                                q = half * GATHER + r
                                pool.indirect_dma_start(
                                    experts[:, q, :], None, table,
                                    bass.IndirectOffsetOnAxis(ap=estage[:, half, r:r + 1], axis=0)).then_inc(g_loaded[q], 16)



def _chunks(w, width):
    k, n = w.shape
    return np.ascontiguousarray(
        w.reshape(k // P, P, n // width, width).transpose(2, 1, 0, 3)).reshape(n // width, P, (k // P) * width)


def _colvec(v):
    return np.ascontiguousarray(v.reshape(-1, P).T)


def shape_constants():
    f = np.float32
    c = {"ident": np.eye(P, dtype=f)}
    half = np.arange(P, dtype=f)
    lin = (half / f(P - 1)).astype(f)
    angle = (f(1.0) / np.power(f(10000.0), lin, dtype=f)).astype(f)
    arg = (np.arange(T, dtype=f)[None, :] * angle[:, None]).astype(f)
    c["trig_a"] = np.stack([np.cos(arg), np.sin(arg)], 1).astype(f)
    log_gamma = np.log((1.0 - 2.0 ** (-5.0 - np.arange(RET_H))).astype(f)).astype(f)
    diff = np.arange(T)[None, :] - np.arange(P)[:, None]
    dec = np.exp(np.maximum(diff, 0).astype(f)[:, None, :] * log_gamma[None, :, None]).astype(f)
    c["decay"] = (np.where(diff[:, None, :] >= 0, dec, 0) / 16).astype(f)
    col = np.arange(896)[None, :] - 384
    c["causal"] = np.where(col <= np.arange(P)[:, None], 0.0, NEG).astype(f)
    inv = (f(1.0) / np.power(f(10000.0), (np.arange(HALF, dtype=f) / f(HALF)), dtype=f)).astype(f)
    ang = (np.arange(T, dtype=f)[:, None] * inv[None, :]).astype(f).reshape(NT, P, HALF).transpose(1, 0, 2)
    c["trig"] = np.stack([np.cos(ang), np.sin(ang)], 1).astype(f)
    dist = 255 - np.arange(384)
    inside = (dist >= 0) & (dist < P)
    d = np.clip(dist, 0, P - 1)
    large = 16 + (np.log(np.maximum(d, 1).astype(f) / f(16)) / f(np.log(8.0)) * f(16)).astype(np.int32)
    bucket = np.where(d < 16, d, np.minimum(large, 31))
    c["bias_hot"] = ((np.arange(32)[:, None] == bucket[None, :]) & inside[None, :]).astype(f)
    c["bias_mask"] = np.broadcast_to(np.where(inside, 0.0, NEG).astype(f), (SWA_H, 384)).copy()
    return c


def lay_out(i):
    a = shape_constants()
    a["x"] = np.ascontiguousarray(i["x"].reshape(T, D))
    w = i["a_w_in"][0]
    qk = np.stack([w[:, :D].reshape(D, RET_H, P, 2), w[:, D:2 * D].reshape(D, RET_H, P, 2)], 2)
    qk = qk.transpose(0, 1, 2, 4, 3).reshape(D, 2 * D)
    a["a_w_in"] = _chunks(np.concatenate([qk, w[:, 2 * D:]], 1), BANK)
    wo = i["a_w_out"][0].reshape(2, KD, P, 2, BANK).transpose(3, 0, 2, 1, 4)
    a["a_w_out"] = np.ascontiguousarray(wo).reshape(4, P, SLOT)
    a["w_kv"] = _chunks(i["w_kv"], 256)[0]
    wb = i["b_w_in"][0]
    order = [4 * (t // 2) + 2 * half + t % 2 for t in range(8) for half in range(2)]
    q = wb[:, :D].reshape(D, SWA_H, SWA_D)[:, order, :].reshape(D, D)
    a["b_w_in"] = _chunks(np.concatenate([q, wb[:, D:]], 1), BANK)
    a["b_w_out"] = _chunks(i["b_w_out"][0], BANK)
    a["rel_bias"] = np.ascontiguousarray(i["rel_bias"])
    wc = i["w_in_2"][0]
    a["c_in0"] = _chunks(wc[:, :Q_LAT], Q_LAT)[0]
    a["c_in1"] = _chunks(wc[:, Q_LAT:Q_LAT + KV_LAT + ROPE], KV_LAT + ROPE)[0]
    a["c_in2"] = _chunks(wc[:, Q_LAT + KV_LAT + ROPE:], BANK)
    wq = i["mla_w_q_up_2"][0].reshape(Q_LAT, MLA_H, NOPE + ROPE)
    a["w_q_up"] = _chunks(np.concatenate([wq[:, :, :NOPE].reshape(Q_LAT, -1), wq[:, :, NOPE:].reshape(Q_LAT, -1)], 1), 768)[0]
    wk = i["mla_w_kv_up_2"][0].reshape(KV_LAT, MLA_H, 2, NOPE)
    a["w_kv_up"] = _chunks(np.ascontiguousarray(wk.transpose(0, 2, 1, 3)).reshape(KV_LAT, 1024), 1024)[0]
    a["c_w_out"] = _chunks(i["w_out_2"][0], BANK)
    wa = i["ada_w_2"][0]
    a["ada_w"] = _chunks(wa, BANK)[ADA_ORDER]
    a["peer_w_q"] = _chunks(i["peer_w_q_2"][0], BANK)
    a["sub_keys"] = np.ascontiguousarray(i["peer_sub_keys_2"][0].transpose(3, 0, 1, 2)).reshape(P, 2 * PEER_H * NKEYS)
    a["peer_u"] = np.ascontiguousarray(i["peer_u_2"][0])
    u = a["peer_u"].reshape(NKEYS, STEPS, PAIR, KD, P)
    a["u_steps"] = np.ascontiguousarray(u.transpose(1, 4, 2, 3, 0)).reshape(STEPS, P, PAIR * D)
    a["peer_v"] = np.ascontiguousarray(i["peer_v_2"][0])
    two = lambda v: np.concatenate([v.reshape(-1), v.reshape(-1)])
    col = {"a_g": i["a_norm_g"], "kv_g": i["kv_norm_g"], "b_g": i["b_norm_g"], "n1_g": i["norm1_g_2"],
           "n2_g": i["norm2_g_2"], "c": i["c_2"], "ada_b": i["ada_b_2"], "k_g": two(i["k_norm_g"]),
           "q_g": two(i["b_q_norm_g"]), "qlat_g": i["mla_q_lat_g_2"], "kvlat_g": i["mla_kv_lat_g_2"],
           "mq_g": i["mla_q_g_2"][0, :NOPE], "mk_g": i["mla_k_g_2"][0, :NOPE], "sub_g": i["diff_subln_g_2"]}
    a["cols"] = np.ascontiguousarray(np.concatenate([_colvec(np.asarray(col[n])) for n in COLS], 1))
    row = {"sinks": i["b_sinks"], "mq_g": i["mla_q_g_2"][0, NOPE:], "mk_g": i["mla_k_g_2"][0, NOPE:],
           "dq_g": i["diff_q_g_2"], "dk_g": i["diff_k_g_2"], "lq1": i["diff_lq1_2"], "lk1": i["diff_lk1_2"],
           "lq2": i["diff_lq2_2"], "lk2": i["diff_lk2_2"]}
    every = lambda v: np.broadcast_to(v, (P, v.size)).copy()
    a["rows"] = every(np.concatenate([np.asarray(row[n]).reshape(-1) for n in ROWS]))
    a["iota"] = every(np.arange(NKEYS, dtype=np.float32))
    ab = i["ada_b_2"].reshape(6, D)
    a["gate_b"] = every(np.concatenate([ab[2], ab[5]]))
    return {k: np.ascontiguousarray(v) for k, v in a.items()}


def build(nc, arrays, upto=99):
    ins = {n: nc.dram_tensor(f"in_{n}", v.shape, F32, kind="ExternalInput").ap() for n, v in arrays.items()}
    ins["bias_rows"] = nc.dram_tensor("bias_rows", [P, SWA_H, 384], F32, kind="Internal").ap()
    out = nc.dram_tensor("out", [T, D], F32, kind="ExternalOutput").ap()
    v = dict(ins)
    v["trig_a"], v["decay"], v["trig"] = ins["trig_a"], ins["decay"], ins["trig"]
    network(nc, v, out, upto)


def kernel(**inputs):
    import concourse.bacc as bacc
    from concourse.bass_utils import run_bass_kernel_spmd

    inputs = {n: np.asarray(v) for n, v in inputs.items()}
    arrays = lay_out(inputs)
    nc = bacc.Bacc("TRN2", target_bir_lowering=False, num_devices=1)
    build(nc, arrays)
    r = run_bass_kernel_spmd(nc, [{f"in_{n}": v for n, v in arrays.items()}], core_ids=[0])
    return r.results[0]["out"].reshape(1, T, D)
```

```python
from collections import namedtuple
from contextlib import ExitStack

import numpy as np

import concourse.bass as bass
from concourse import mybir

F32 = mybir.dt.float32
U32 = mybir.dt.uint32
F32R = mybir.dt.float32r
BF16 = mybir.dt.bfloat16
ALU = mybir.AluOpType
ACT = mybir.ActivationFunctionType
AX = mybir.AxisListType

P = 128
T = 512
NT = T // P
D = 1024
KD = D // P
NB = 8
BANK = 512
RET_H = 4
RET_K = KD * 2
SWA_H, SWA_D, SWA_KV = 16, 64, 2
SWA_W = 2 * P
MLA_H, NOPE, ROPE = 4, 128, 64
Q_LAT, KV_LAT = 384, 256
DIFF_H = 4
HALF = ROPE // 2
PEER_H, NKEYS, TOPK = 8, 128, 16
WHOLE = TOPK // 2
SUMS = WHOLE * TOPK + TOPK - WHOLE
SLOTS = PEER_H * TOPK
GATHERED = 2
DENSE = NT - GATHERED
DT = DENSE * P
PAIR = 2
STEPS = NKEYS // PAIR
QUARTERS = 2 * GATHERED
QKEYS = NKEYS // QUARTERS
QSTEPS = STEPS // QUARTERS
BATCH = DT // QSTEPS
PARTS = 3
EARLY = [0] + list(range(GATHERED, NT))
LATE = 1
NE = len(EARLY)
EPS = 1e-6
LAMBDA_INIT = 0.8 - 0.6
NEG = -1.0e30
LOWEST = -3.0e38
SQ_SCALE = 2.0 ** -32
SUM_MAX = float(np.finfo(np.float32).max) * 2.0 ** -64
BIG = 1.9e19
PIECE = 1024
NPIECE = 4
GATHER = 4

COLS = {}
for _name, _n in (("a_g", KD), ("kv_g", KD), ("b_g", KD), ("n1_g", KD), ("n2_g", KD), ("c", KD),
                  ("ada_b", 48), ("k_g", 1), ("q_g", 1), ("qlat_g", 3), ("kvlat_g", 2),
                  ("mq_g", 1), ("mk_g", 1), ("sub_g", 1)):
    _at = sum(n for _, n in COLS.values())
    COLS[_name] = (_at, _n)
NCOLS = sum(n for _, n in COLS.values())

ROWS = {}
for _name, _n in (("sinks", SWA_H), ("mq_g", ROPE), ("mk_g", ROPE), ("dq_g", ROPE), ("dk_g", ROPE),
                  ("lq1", ROPE), ("lk1", ROPE), ("lq2", ROPE), ("lk2", ROPE)):
    _at = sum(n for _, n in ROWS.values())
    ROWS[_name] = (_at, _n)
NROWS = sum(n for _, n in ROWS.values())

ADA_ORDER = [0, 1, 2, 3, 6, 7, 8, 9, 4, 5, 10, 11]
ADA_IN_A = 8


Ranking = namedtuple("Ranking", "scr cand cscr eq v idxf idx pos posf past")


class Jobs:

    def __init__(self):
        self.number = {}

    def add(self, *key):
        self.number[key] = len(self.number)

    def __call__(self, *key):
        j = self.number[key]
        return j % NB, j // NB


def plan_jobs():
    jobs = Jobs()
    for k in range(KD):
        jobs.add("xT_a", k)
    jobs.add("bias", 0)
    for n in range(12):
        for i in range(4):
            jobs.add("a_in", n, i)
        if n < ADA_IN_A:
            jobs.add("ada", n)
    for h in range(RET_H + 1):
        if h < RET_H:
            for j in range(NT):
                jobs.add("ret_s", h, j)
        if h >= 1:
            for i in range(NT):
                jobs.add("ret_o", h - 1, i)
    for f in range(RET_K):
        jobs.add("zT_a", f)
    for half in range(2):
        for t in range(NT):
            jobs.add("a_out", half, t)
    for k in range(KD):
        jobs.add("xT_b", k)
    for t in range(NT):
        jobs.add("kv", t)
    for n in range(4):
        for t in range(NT):
            jobs.add("b_in", n, t)
        if n >= 1:
            jobs.add("ada", ADA_IN_A + n - 1)
    for g in range(SWA_KV):
        jobs.add("kT", g)
    for i in range(KD):
        jobs.add("qT", i)
    jobs.add("ada", ADA_IN_A + 3)
    for n in range(NT + 1):
        if n < NT:
            for i in range(8):
                jobs.add("swa_s", n, i)
        if n >= 1:
            for i in range(8):
                jobs.add("swa_pT", n - 1, i)
            for g in range(SWA_KV):
                jobs.add("swa_o", n - 1, g)
    for k in range(KD):
        jobs.add("zT_b", k)
    for half in range(2):
        for t in range(NT):
            jobs.add("b_out", half, t)
    for k in range(KD):
        jobs.add("xT_c", k)
    for n in range(6):
        for t in range(NT):
            jobs.add("c_in", n, t)
    for i in range(3):
        jobs.add("qlT", i)
    for i in range(2):
        jobs.add("kvlT", i)
    for t in range(NT):
        jobs.add("q_nope", t)
        jobs.add("q_rope", t)
    for t in range(NT):
        jobs.add("k_nope", t)
        jobs.add("v_up", t)
    for h in range(DIFF_H):
        jobs.add("qdT", h)
        jobs.add("kdT", h)
    jobs.add("kpeT", 0)
    for h in range(MLA_H):
        jobs.add("qnT", h)
        jobs.add("knT", h)
    for i in range(2):
        jobs.add("qrT", i)
    units = [("m", h, i) for h in range(MLA_H) for i in range(NT)] + \
            [("d", h, i) for h in range(DIFF_H) for i in range(NT)]
    for n in range(len(units) + 3):
        if n < len(units):
            jobs.add("att_s", n, 0)
            if units[n][0] == "d":
                jobs.add("att_s", n, 1)
        if n >= 3:
            jobs.add("att_o", n - 3)
        if 2 <= n < len(units) + 2:
            jobs.add("att_pT", n - 2)
    for k in range(KD):
        jobs.add("mT", k)
    for half in range(2):
        for t in range(NT):
            jobs.add("c_out", half, t)
    for k in range(KD):
        jobs.add("xT_d", k)
    for f in range(2 * PEER_H + 1):
        if f < 2 * PEER_H:
            jobs.add("pqT", f)
        if f >= 1:
            jobs.add("peer_s", f - 1)
        if f == 2 * PEER_H - 2:
            for i in range(GATHERED * 2):
                jobs.add("h2", i)
    for i in range(3):
        jobs.add("pairs", i)
    return jobs, units


def plan_headnorms():
    units = []
    for n in range(2):
        units += [(("b_in", n, t), 8, SWA_D) for t in range(NT)]
    swa = len(units)
    for n, (heads, width) in enumerate(((1, Q_LAT), (1, KV_LAT), (1, ROPE), (8, ROPE), (8, ROPE))):
        units += [(("c_in", n, t), heads, width) for t in range(NT)]
    proj = len(units)
    for t in range(NT):
        units += [(("q_nope", t), MLA_H, NOPE), (("q_rope", t), MLA_H, ROPE)]
    units += [(("k_nope", t), MLA_H, NOPE) for t in range(NT)]
    return units, swa, proj


def network(nc, ins, out):
    jobs, att_units = plan_jobs()
    hn_units, HN_SWA, HN_PROJ = plan_headnorms()
    HN_ALL = len(hn_units)

    Piece = namedtuple("Piece", "name src kt kind last")
    pieces = []

    def cut(name, src, width, kt, kind, last=None, count=None):
        n = src.shape[1] // (width * kt)
        return [Piece(name + (p,), src[:, p * kt * width:(p + 1) * kt * width], kt, kind,
                      last if kind == "plain" or p == n - 1 else None) for p in range(n)]

    def mixed(a, b):
        return [x for pair in zip(a, b) for x in pair]

    a_in = [cut(("a_in", n), ins["a_w_in"][n], BANK, 2, "split", ("a_in", n, 3)) for n in range(12)]
    ada_w = [cut(("ada", n), ins["ada_w"][n], BANK, 2, "ada") for n in range(12)]
    b_in = [cut(("b_in", n), ins["b_w_in"][n], BANK, 2, "split", ("b_in", n, NT - 1)) for n in range(4)]
    pieces += a_in[0]
    for n in range(1, 12):
        pieces += mixed(a_in[n], ada_w[n - 1]) if n <= ADA_IN_A else a_in[n]
    for n in range(4):
        pieces += cut(("a_out", n), ins["a_w_out"][n], BANK, 2, "split", ("a_out", n // 2, NT - 1) if n % 2 else None)
    pieces += cut(("kv", 0), ins["w_kv"], 256, 4, "plain", ("kv", NT - 1))
    pieces += b_in[0]
    for n in range(1, 4):
        pieces += mixed(b_in[n], ada_w[ADA_IN_A + n - 1])
    pieces += ada_w[ADA_IN_A + 3]
    for n in range(2):
        pieces += cut(("b_out", n), ins["b_w_out"][n], BANK, 2, "split", ("b_out", n, NT - 1))
    pieces += cut(("c_in", 0), ins["c_in0"], Q_LAT, 2, "split", ("c_in", 0, NT - 1))
    pieces += cut(("c_in", 1), ins["c_in1"], KV_LAT, 2, "split", ("c_in", 1, NT - 1))
    pieces += cut(("c_in", 2), ins["c_kpe"], ROPE, KD, "plain", ("c_in", 2, NT - 1))
    for n in range(3):
        pieces += cut(("c_in", 3 + n), ins["c_in2"][n], BANK, 2, "split", ("c_in", 3 + n, NT - 1))
    pieces += cut(("q_up", 0), ins["w_q_up"], 768, 1, "plain", ("q_rope", NT - 1))
    pieces += cut(("kv_up", 0), ins["w_kv_up"], 1024, 1, "plain", ("v_up", NT - 1))
    for n in range(2):
        pieces += cut(("c_out", n), ins["c_w_out"][n], BANK, 2, "split", ("c_out", n, NT - 1))
    for f in range(2 * PEER_H):
        pieces += cut(("pq", f), ins["peer_w_q"][f], P, KD, "split", ("pqT", f))
    place = {piece.name: c for c, piece in enumerate(pieces)}
    splits = [piece for piece in pieces if piece.kind == "split"]
    split_at = {piece.name: q for q, piece in enumerate(splits)}
    c_ahead = {n: max(q for q, x in enumerate(splits) if x.name[0:2] == ("c_in", n)) + NPIECE for n in (0, 1, 3, 4)}
    c_ahead[1] = split_at["c_in", 3, 0] + NPIECE - 1
    c_ahead[0] = min(c_ahead[0], c_ahead[1])
    counted = {piece.name: n + 1 for n, piece in enumerate([x for x in splits if x.last is None])}

    with ExitStack() as ctx:
        address = {}

        def sb(name, shape, dt=F32):
            address[name] = (nc.sbuf_base + 31) // 32 * 32
            return ctx.enter_context(nc.sbuf_tensor(name, shape, dt))

        def sem(name):
            return ctx.enter_context(nc.semaphore(name))

        xres = sb("xres", [P, NT, D])
        ring = sb("ring", [P, 3 * NPIECE * PIECE])
        hT = sb("hT", [P, KD, T])
        work = sb("work", [P, 24576])
        tables = sb("tables", [P, 4096])
        tmp = sb("tmp", [P, 2, BANK])
        ysum = sb("ysum", [P, BANK])
        spare = sb("spare", [P, BANK])
        cols = sb("cols", [P, NCOLS])
        iota = sb("iota", [P, NKEYS])
        consts = sb("consts", [P, NROWS + 2 * NT * HALF + P + 8 * 16])
        rows = consts[:, 0:NROWS]
        ident = sb("ident", [P, P])
        trig = consts[:, NROWS:NROWS + 2 * NT * HALF].rearrange("p (a t d) -> p a t d", a=2, d=HALF)
        ones = consts[:, NROWS + 2 * NT * HALF:NROWS + 2 * NT * HALF + P]
        minus_half = sb("minus_half", [P, 16])
        stat = sb("stat", [P, 4, NT])
        rstat = sb("rstat", [P, 3, 16])
        hstat = sb("hstat", [P, 4, 3, 8])
        modcol = sb("modcol", [P, 6, KD])
        csil = sb("csil", [P, KD])
        lam = sb("lam", [P, 8])
        astat = consts[:, NROWS + 2 * NT * HALF + P:].rearrange("p (a n) -> p a n", n=16)

        ps = ctx.enter_context(nc.psum_tensor("ps", [P, NB, BANK], F32))

        def parts(name, of, at, *dims):
            n = int(np.prod(dims))
            v = nc.alloc_sbuf_tensor_at(name, [P, n], F32R, offset=address[of] + 4 * at)
            return v[:].rearrange("p (a b) -> p a b", b=dims[-1]) if len(dims) == 2 else v[:]

        def W(at, *dims):
            n = int(np.prod(dims))
            v = work[:, at:at + n]
            if len(dims) == 2:
                v = v.rearrange("p (a b) -> p a b", b=dims[1])
            elif len(dims) == 3:
                v = v.rearrange("p (a b c) -> p a b c", b=dims[1], c=dims[2])
            elif len(dims) == 4:
                v = v.rearrange("p (a b c d) -> p a b c d", b=dims[1], c=dims[2], d=dims[3])
            return v

        def col(name, k=0, n=1):
            at = COLS[name][0] + k
            return cols[:, at:at + n]

        def row(name):
            at, n = ROWS[name]
            return rows[:, at:at + n]

        w_hi = [parts(f"w_hi{q}", "ring", (NPIECE + 2 * q) * PIECE, PIECE) for q in range(NPIECE)]
        w_lo = [parts(f"w_lo{q}", "ring", (NPIECE + 2 * q + 1) * PIECE, PIECE) for q in range(NPIECE)]
        x_hi = parts("x_hi", "hT", 0, KD, T)
        d_hi, d_lo = parts("x_hi_d", "work", 0, KD, T), parts("x_lo_d", "work", 18432, KD, T)
        x_lo = {"a": parts("x_lo_a", "xres", 0, KD, T), "b": parts("x_lo_b", "work", 4096, KD, T),
                "c": parts("x_lo_c", "work", 19968, KD, T)}
        o_hi = {"a_out": parts("o_hi_a", "work", 0, RET_K, T), "b_out": parts("o_hi_b", "work", 4096, KD, T),
                "c_out": parts("o_hi_c", "work", 4096, KD, T)}
        o_lo = {"a_out": parts("o_lo_a", "work", 8192, RET_K, T), "b_out": parts("o_lo_b", "work", 8192, KD, T),
                "c_out": parts("o_lo_c", "work", 10240, KD, T)}

        trigA = tables[:, 0:1024].rearrange("p (a t) -> p a t", a=2)
        decay = tables[:, 1024:3072].rearrange("p (h t) -> p h t", h=RET_H)
        causal = tables[:, 3072:3968]
        gates = tables[:, 0:2048].rearrange("p (a d) -> p a d", a=2)
        a_q, a_k = W(0, RET_H, 2, T), W(4096, RET_H, 2, T)
        a_v, a_z = W(8192, NT, 2048), W(16384, NT, 2048)
        a_sT = hT[:, :, :].rearrange("p (b j) t -> p b j t", b=2)
        a_xn = W(8192, NT, D)
        bias_in = W(7296, 784)
        bias_w, bias_hot, bias_mask = bias_in[0:32, 0:16], bias_in[0:32, 16:400], bias_in[0:SWA_H, 400:784]
        b_kvT, b_qT, b_xn, b_qn = W(0, KD, T), W(4096, KD, T), W(16384, NT, D), W(8192, NT, D)
        b_bias = W(12288, SWA_H, SWA_W)
        b_z = W(16384, NT, D)
        b_kv, b_kn, b_kT = W(20480, NT, 256), W(21504, NT, SWA_KV, 2, SWA_D), W(22528, SWA_KV, 2, T)
        b_s = [W(0, SWA_H, SWA_W), W(8192, SWA_H, SWA_W)]
        b_pT = hT[:, :, :].rearrange("p (a b) t -> p (a b t)", b=1)
        c_xn = W(0, NT, D)
        c_ql, c_kvl, c_kpe = W(4096, NT, Q_LAT), W(5632, NT, KV_LAT), W(6656, NT, ROPE)
        c_dq, c_dk, c_dv = W(8192, NT, 512), W(10240, NT, 512), W(12288, NT, 512)
        c_dqr, c_dkr, c_kper = W(0, NT, 512), W(2048, NT, 512), W(7168, NT, 2, ROPE)
        c_qlT, c_kvlT = W(14336, 3, T), W(15872, 2, T)
        c_kpeT, c_qdT, c_kdT = W(16896, 2, T), W(17920, DIFF_H, T), W(19968, DIFF_H, 2, T)
        c_qn, c_qr, c_kn, c_v = W(4096, NT, 512), W(6144, NT, 256), W(8192, NT, 512), W(10240, NT, 512)
        c_qnT, c_qrT, c_knT = W(1024, MLA_H, T), W(3072, 2, T), W(14336, MLA_H, T)
        c_qrr = [W(7680, 256), W(7936, 256), W(24064, 256), W(24320, 256)]
        c_s = W(4096, 8, BANK)
        c_pT = hT[:, :, :]
        c_om, c_od = W(8192, NT, 512), W(0, NT, 512)
        d_xn, d_qT, d_s = W(0, NT, D), W(4096, 2, T), W(5120, 4, NT, NKEYS)
        EK = NE * TOPK
        early = [Ranking(
            scr=W(7168, 2 * NE, NKEYS), cand=W(8192, NE, SUMS), cscr=W(9216, NE, SUMS), eq=None,
            v=W(11264, 2, NE, TOPK), idxf=W(11392 + b * 2 * EK, 2, NE, TOPK), idx=W(11584, 2, NE, TOPK).bitcast(U32),
            pos=W(11680, 3, EK).bitcast(U32), posf=W(11840 + b * 2 * EK, 2, EK),
            past=W(12032, EK)) for b in range(2)]
        eq_place = lambda v, at: v[:, at:at + EK * TOPK].rearrange("p (k a) -> p k a", a=TOPK)
        pick_eq = [[eq_place(work, 10240), eq_place(tables, 0)],
                   [eq_place(work, 22528), eq_place(work, 22528 + EK * TOPK)]]
        r_sel, r_g, r_sum = W(12288, 2, NE, PEER_H, TOPK), W(13312, NE, PEER_H, TOPK), W(13824, 2, NE * PEER_H)
        late_s = W(14336, 2 * PEER_H, NKEYS)
        keys = W(16384, 2 * PEER_H, NKEYS)
        kept = [hT[:, k, 0:GATHERED * P] for k in range(KD)]
        iT, jT = kept[0][:, 0:P].bitcast(BF16), kept[0][:, P:2 * P].bitcast(BF16)
        gT = [kept[1][:, 0:P].bitcast(BF16), kept[1][:, P:2 * P].bitcast(BF16), kept[2][:, 0:P].bitcast(BF16)]
        r_astage, r_cstage = kept[2][:, P:P + 8], kept[2][:, P + 8:P + 16]
        eidx = kept[3].bitcast(U32)
        late_sel = [kept[3][:, P:2 * P], ident[:]]
        g_kept = kept[4]
        r_a, r_coef = kept[5][:, 0:SLOTS], kept[5][:, SLOTS:2 * SLOTS]
        r_y = tables[:, 0:D]
        late_keep = ring[:, 10240:12288].rearrange("p (f n) -> p f n", n=NKEYS)

        LateRanking = namedtuple("LateRanking", "stage rank g out sum hold")

        def late_places(place):
            def Y(at, *dims):
                n = int(np.prod(dims))
                return place[:, at:at + n].rearrange("p (a b) -> p a b", b=dims[-1]) if len(dims) == 2 else \
                    place[:, at:at + n].rearrange("p (a b c) -> p a b c", b=dims[1], c=dims[2])

            return LateRanking(
                stage=Y(0, 2, NKEYS),
                rank=Ranking(
                    scr=Y(256, 2, NKEYS), cand=Y(512, 1, SUMS), cscr=Y(0, 1, SUMS), eq=Y(256, TOPK, TOPK),
                    v=Y(768, 2, 1, TOPK), idxf=Y(800, 2, 1, TOPK), idx=Y(832, 2, 1, TOPK).bitcast(U32),
                    pos=Y(864, 3, TOPK).bitcast(U32), posf=Y(912, 2, TOPK), past=place[:, 768:768 + TOPK]),
                g=Y(944, 1, TOPK), out=Y(960, 2, TOPK), sum=Y(992, 2, PEER_H), hold=place[:, 1008:1009])

        late = [late_places(r_y), late_places(ring[:, 10240:11264])]
        d_h2 = tables[:, 2048:4096].rearrange("p (t d) -> p t d", d=D)
        spread = [W(0, QKEYS, DT), W(QKEYS * DT, QKEYS, DT)]
        u_ring, v_ring = W(16384, 2, PAIR, KD, P), W(20480, 2, PAIR, D)
        wide_iota = consts[:, 0:NKEYS * BATCH // 2].bitcast(BF16).rearrange("p (i t) -> p i t", t=BATCH)
        hot_i = [ring[:, 8192 + b * 1024:8192 + (b + 1) * 1024].bitcast(BF16).rearrange("p (i t) -> p i t", t=BATCH)
                 for b in range(2)]
        hot_j = [[v.bitcast(BF16).rearrange("p (j t) -> p j t", t=BATCH) for v in vs]
                 for vs in ((ysum[:, 0:256], ysum[:, 256:512], kept[6]), (spare[:, 0:256], spare[:, 256:512], kept[7]))]
        g_rest = [tmp[:, 0, 0:DT], tmp[:, 1, 0:DT]]
        estage = sb("estage", [P, 2, GATHER], U32)
        absorb = sb("absorb", [P, 1])
        experts = ring[:, 0:2 * GATHER * D].rearrange("p (r d) -> p r d", d=D)

        bank_full = [sem(f"bank_full{b}") for b in range(NB)]
        bank_free = [sem(f"bank_free{b}") for b in range(NB)]
        piece_loaded = [sem(f"piece_loaded{s}") for s in range(NPIECE)]
        w_high = sem("w_high")
        w_split = sem("w_split")
        w_used = sem("w_used")
        x_high = sem("x_high")
        o_high = sem("o_high")
        d_high = sem("d_high")
        d_low = sem("d_low")
        x_low = sem("x_low")
        x_again = sem("x_again")
        x_loaded = [sem(f"x_loaded{t}") for t in range(NT)]
        const_loaded = sem("const_loaded")
        ret_loaded = sem("ret_loaded")
        row_loaded = sem("row_loaded")
        gate_bias = sem("gate_bias")
        bias_kept = sem("bias_kept")
        bias_loaded = sem("bias_loaded")
        made = sem("made")
        sq_done = sem("sq_done")
        ms_done = sem("ms_done")
        rr_done = sem("rr_done")
        xn_done = sem("xn_done")
        silu_c = sem("silu_c")
        ada_step = sem("ada_step")
        mod_done = sem("mod_done")
        qk_tmp = sem("qk_tmp")
        qk_done = sem("qk_done")
        z_sq = sem("z_sq")
        z_ms = sem("z_ms")
        z_r = sem("z_r")
        bias_done = sem("bias_done")
        k_sq = sem("k_sq")
        k_ss = sem("k_ss")
        k_ms = sem("k_ms")
        k_r = sem("k_r")
        k_n = sem("k_n")
        padded = sem("padded")
        hn_sq = sem("hn_sq")
        hn_ss = sem("hn_ss")
        hn_ms = sem("hn_ms")
        hn_r = sem("hn_r")
        sw_s = sem("sw_s")
        sw_m = sem("sw_m")
        sw_nm = sem("sw_nm")
        sw_e = sem("sw_e")
        sw_es = sem("sw_es")
        sw_l = sem("sw_l")
        sw_rl = sem("sw_rl")
        sw_zg = sem("sw_zg")
        rope_t = sem("rope_t")
        rope_done = sem("rope_done")
        lam_dve = sem("lam_dve")
        lam_act = sem("lam_act")
        at_nm = sem("at_nm")
        at_p = sem("at_p")
        at_rl = sem("at_rl")
        at_w = sem("at_w")
        od_clamped = sem("od_clamped")
        od_sq = sem("od_sq")
        od_ms = sem("od_ms")
        od_r = sem("od_r")
        od_rr = sem("od_rr")
        sub_done = sem("sub_done")
        out_tmp = sem("out_tmp")
        route = sem("route")
        route_e = sem("route_e")
        routed = sem("routed")
        placed = sem("placed")
        pick_step = sem("pick_step")
        picked = sem("picked")
        keys_loaded = sem("keys_loaded")
        late_kept = sem("late_kept")
        late_step = sem("late_step")
        late_done = sem("late_done")
        iota_ready = sem("iota_ready")
        gate_part = sem("gate_part")
        ranked = sem("ranked")
        u_loaded = [sem(f"u_loaded{b}") for b in range(2)]
        v_loaded = [sem(f"v_loaded{b}") for b in range(2)]
        hot_step = sem("hot_step")
        hot_ready = sem("hot_ready")
        spread_summed = sem("spread_summed")
        spread_kept = sem("spread_kept")
        u_done = sem("u_done")
        dense_gelu = sem("dense_gelu")
        dense_coef = sem("dense_coef")
        v_done = sem("v_done")
        g_staged = sem("g_staged")
        g_absorb = sem("g_absorb")
        g_loaded = [sem(f"g_loaded{r}") for r in range(2 * GATHER)]
        g_used = [sem(f"g_used{h}") for h in range(2)]
        g_dve = sem("g_dve")
        a_ready = sem("a_ready")
        gelu_done = sem("gelu_done")
        coef_done = sem("coef_done")
        y_step = sem("y_step")
        y_zero = sem("y_zero")
        out_ready = sem("out_ready")
        out_half = sem("out_half")
        gathering = sem("gathering")
        stored = sem("stored")

        def full(eng, *key):
            b, use = jobs(*key)
            eng.wait_ge(bank_full[b], use + 1)
            return ps[:, b, :]

        def taken(ins_, *key):
            ins_.then_inc(bank_free[jobs(*key)[0]], 1)

        def drained(eng, *key):
            b, use = jobs(*key)
            eng.wait_ge(bank_free[b], use + 1)

        def raw(*name):
            c = place[name]
            n = pieces[c].src.shape[1]
            at = c % NPIECE * PIECE
            return ring[:, at:at + n].rearrange("p (k c) -> p k c", k=pieces[c].kt)

        def arrived(eng, *name):
            c = place[name]
            eng.wait_ge(piece_loaded[c % NPIECE], 16 * (c // NPIECE + 1))

        def high_low(*name):
            q = split_at[name]
            n = splits[q].src.shape[1]
            return [v[q % NPIECE][:, 0:n].rearrange("p (k c) -> p k c", k=splits[q].kt) for v in (w_hi, w_lo)]

        def used(eng, piece):
            if piece.last is None:
                eng.wait_ge(w_used, counted[piece.name])
            else:
                full(eng, *piece.last)

        def sqbuf(n):
            return tmp[:, n % 2, :]

        block = ctx.enter_context(nc.Block())

        @block.sync
        def _(sp):
            for t in range(NT):
                sp.dma_start(xres[:, t, :], ins["x"][t * P:(t + 1) * P, :]).then_inc(x_loaded[t], 16)
                if t == 0:
                    sp.dma_start(ident[:], ins["ident"]).then_inc(const_loaded, 16)
                    sp.dma_start(cols[:], ins["cols"]).then_inc(const_loaded, 16)
            for c, piece in enumerate(pieces):
                name = piece.name
                if name == ("a_in", 1, 0):
                    sp.dma_start(trigA, ins["trig_a"]).then_inc(ret_loaded, 16)
                    sp.dma_start(decay, ins["decay"]).then_inc(ret_loaded, 16)
                if c >= NPIECE:
                    before = pieces[c - NPIECE]
                    if before.kind == "ada":
                        sp.wait_ge(ada_step, KD * before.name[1] + 2 * before.name[2] + 2)
                    elif before.kind == "split":
                        sp.wait_ge(w_split, split_at[before.name] + 1)
                    else:
                        full(sp, *before.last)
                at = c % NPIECE * PIECE
                sp.dma_start(ring[:, at:at + piece.src.shape[1]], piece.src).then_inc(piece_loaded[c % NPIECE], 16)
                if name == ("pq", 0, 0):
                    full(sp, "c_out", 1, NT - 1)
                    sp.dma_start(keys[:], ins["sub_keys"].rearrange("p (a n) -> p a n", n=NKEYS)).then_inc(keys_loaded, 16)
                if name == ("a_out", 0, 3):
                    drained(sp, "ret_s", RET_H - 1, NT - 1)
                    sp.dma_start(gates, ins["gate_b"]).then_inc(gate_bias, 16)
                    full(sp, "a_in", 11, 3)
                    for t in range(NT):
                        sp.dma_start(xres[:, t, :], ins["x"][t * P:(t + 1) * P, :]).then_inc(x_again, 16)
            full(sp, "peer_s", 2 * PEER_H - 1)
            u_rows = ins["u_steps"].rearrange("n p c -> p n c")
            v_rows = ins["peer_v"].rearrange("(i n) d -> i n d", i=NKEYS)

            def load_u(n, b):
                sp.dma_start(u_ring[:, b, :, :, :].rearrange("p j k i -> p (j k i)").unsqueeze(1),
                             u_rows[:, bass.ds(n, 1), :]).then_inc(u_loaded[b], 16)

            def load_v(n, b):
                sp.dma_start(v_ring[:, b, :, :], v_rows[:, bass.ds(n * PAIR, PAIR), :]).then_inc(v_loaded[b], 16)

            for n in range(2):
                load_u(n, n)
            sp.wait_ge(picked, 2 * PEER_H - 1)
            sp.wait_ge(routed, 1)
            for n in range(2):
                load_v(n, n)
            with sp.Fori(1, STEPS // 2) as turn:
                for b in range(2):
                    n = turn * 2 + b
                    sp.wait_ge(u_done, n - 1)
                    load_u(n, b)
                    sp.wait_ge(v_done, n + 1)
                    load_v(n, b)
            for t in range(NT):
                sp.wait_ge(out_ready, t + 1)
                sp.dma_start(out[t * P:(t + 1) * P, :], xres[:, t, :]).then_inc(stored, 16)
            sp.wait_ge(stored, 16 * NT)
            sp.wait_ge(row_loaded, 16 * 7)
            sp.wait_ge(gate_bias, 16)

        @block.tensor
        def _(pe):
            opened = [0]

            def start(*key):
                assert jobs.number[key] == opened[0], key
                opened[0] += 1
                b, use = jobs(*key)
                if use:
                    pe.wait_ge(bank_free[b], use)
                return ps[:, b, :]

            def end(mm, *key):
                mm.then_inc(bank_full[jobs(*key)[0]], 1)

            def transposes(key, src, ready=None):
                o = start(*key)
                for t in range(NT):
                    s = src(t)
                    if ready is not None:
                        ready(t)
                    mm = pe.transpose(o[0:s.shape[1], t * P:(t + 1) * P], s, ident[:])
                end(mm, *key)

            def stream_transposes(name, xn, n):
                def one(k, t):
                    mm = pe.transpose(ps[:, jobs(name, k)[0], t * P:(t + 1) * P], xn[:, t, k * P:(k + 1) * P], ident[:])
                    if t == NT - 1:
                        end(mm, name, k)

                for k in range(KD):
                    start(name, k)
                    for t in range(NT - 1):
                        if k == 0:
                            pe.wait_ge(xn_done, NT * n + t + 1)
                        one(k, t)
                pe.wait_ge(xn_done, NT * n + NT)
                for k in range(KD):
                    one(k, NT - 1)

            def project(keys_, names, x, tokens, width, tile_major=0, ready=None):
                os = [start(*key) for key in keys_]
                steps, k = [], 0
                for name in names:
                    steps.append((name, range(k, k + splits[split_at[name]].kt)))
                    k += len(steps[-1][1])
                major = len(steps) - tile_major

                def one(i, name, ks):
                    whi, wlo = high_low(*name)
                    for k in ks:
                        if ready is not None and i == 0:
                            pe.wait_ge(x_low, ready + k + 1)
                        kw = k - ks[0]
                        for n, (a, b) in enumerate(((0, 0), (0, 1), (1, 0))):
                            w = (whi, wlo)[b][:, kw, :]
                            v = x[a][:, k + x[2], :]
                            if tokens:
                                lhsT, rhs = v[:, i * P:(i + 1) * P], w
                            else:
                                lhsT, rhs = w[:, i * P:(i + 1) * P], v
                            mm = pe.matmul(os[i][:, 0:width], lhsT, rhs, start=(k == 0 and n == 0),
                                           stop=(name == names[-1] and k == ks[-1] and n == 2))
                    return mm

                for name, ks in steps[:major]:
                    pe.wait_ge(w_split, split_at[name] + 1)
                    for i in range(4):
                        mm = one(i, name, ks)
                        if name == names[-1]:
                            end(mm, *keys_[i])
                    if name in counted:
                        mm.then_inc(w_used, 1)
                for name, ks in steps[major:]:
                    pe.wait_ge(w_split, split_at[name] + 1)
                for i in range(4) if tile_major else ():
                    for name, ks in steps[major:]:
                        mm = one(i, name, ks)
                        if name == names[-1]:
                            end(mm, *keys_[i])
                        elif i == 3:
                            mm.then_inc(w_used, 1)

            def tokens_by_features(key, lhsT, w, kt, c0, width, t, ready=None):
                o = start(*key)
                for k in range(kt):
                    if ready is not None and t == 0:
                        drained(pe, ready, k)
                    mm = pe.matmul(o[:, 0:width], lhsT[:, k, t * P:(t + 1) * P], w(k)[:, c0:c0 + width],
                                   start=(k == 0), stop=(k == kt - 1))
                end(mm, *key)

            def output(name, transposed, chunks):
                for n in range(len(transposed)):
                    drained(pe, *transposed[n])
                for half in range(2):
                    names = [(name, half * chunks + c, p) for c in range(chunks) for p in range(4)]
                    project([(name, half, t) for t in range(NT)], names, (o_hi[name], o_lo[name], 0), True, BANK,
                            tile_major=4 if half == 1 else 0)

            def ada(n):
                part = ADA_ORDER[n] // 2
                o = start("ada", n)
                pe.wait_ge(ada_step, KD * (n + 1))
                if part in (2, 5):
                    mm = pe.matmul(o, ones[:], ysum[:], start=True, stop=True)
                else:
                    for i in range(4):
                        mm = pe.matmul(o[:, i:i + 1], ysum[:, i * P:(i + 1) * P], ones[:, 0:1],
                                       start=True, stop=True)
                end(mm, "ada", n)

            pe.wait_ge(const_loaded, 32)
            stream_transposes("xT_a", a_xn, 0)
            o = start("bias", 0)
            pe.wait_ge(row_loaded, 16 * 7)
            end(pe.matmul(o[0:SWA_H, 0:384], bias_w, bias_hot, start=True, stop=True), "bias", 0)
            pe.wait_ge(made, 1)
            for n in range(12):
                project([("a_in", n, i) for i in range(4)], [("a_in", n, p) for p in range(4)],
                        (x_hi, x_lo["a"], 0), n >= RET_H, BANK, ready=0 if n == 0 else None)
                if n < ADA_IN_A:
                    ada(n)
            for h in range(RET_H + 1):
                if h < RET_H:
                    pe.wait_ge(qk_done, 4 * (h + 1))
                    for j in range(NT):
                        o = start("ret_s", h, j)
                        for e in range(2):
                            mm = pe.matmul(o[:, 0:T - j * P], a_k[:, h, e, j * P:(j + 1) * P],
                                           a_q[:, h, e, j * P:T], start=(e == 0), stop=(e == 1))
                        end(mm, "ret_s", h, j)
                if h >= 1:
                    g = h - 1
                    for t in range(NT):
                        drained(pe, "a_in", RET_H + g, t)
                    for i in range(NT):
                        drained(pe, "ret_s", g, i)
                        o = start("ret_o", g, i)
                        for j in range(i + 1):
                            mm = pe.matmul(o, a_sT[:, g % 2, j, (i - j) * P:(i - j + 1) * P],
                                           a_v[:, j, g * BANK:(g + 1) * BANK], start=(j == 0), stop=(j == i))
                        end(mm, "ret_o", g, i)
            for f in range(RET_K):
                transposes(("zT_a", f), lambda t: a_z[:, t, f * P:(f + 1) * P],
                           lambda t: drained(pe, "ret_o", f // 4, t))
            output("a_out", [("zT_a", f) for f in range(RET_K)], 2)

            stream_transposes("xT_b", b_xn, 1)
            for p in range(2):
                arrived(pe, "kv", 0, p)
            for t in range(NT):
                tokens_by_features(("kv", t), b_kvT, lambda k: raw("kv", 0, k // 4)[:, k % 4, :], KD, 0, 256, t, "xT_b")
            for n in range(4):
                project([("b_in", n, t) for t in range(NT)], [("b_in", n, p) for p in range(4)],
                        (x_hi, x_lo["b"], 0), True, BANK, ready=KD if n == 0 else None)
                if n >= 1:
                    ada(ADA_IN_A + n - 1)
            pe.wait_ge(k_n, 2)
            for g in range(SWA_KV):
                transposes(("kT", g), lambda t: b_kn[:, t, g, :, :].rearrange("p a d -> p (a d)"))
            for i in range(KD):
                transposes(("qT", i), lambda t: b_qn[:, t, i * P:(i + 1) * P],
                           lambda t: drained(pe, "b_in", i // 4, t))
            ada(ADA_IN_A + 3)
            for n in range(NT + 1):
                if n < NT:
                    k0 = max(n - 1, 0) * P
                    w0 = P if n == 0 else 0
                    for i in range(8):
                        if n == 0:
                            drained(pe, "kT", i // 4)
                            drained(pe, "qT", 2 * (i // 2))
                            drained(pe, "qT", 2 * (i // 2) + 1)
                        o = start("swa_s", n, i)
                        for m in range(2):
                            mm = pe.matmul(o[:, m * SWA_W + w0:(m + 1) * SWA_W],
                                           b_qT[:, 2 * (i // 2) + m, n * P:(n + 1) * P],
                                           b_kT[:, i // 4, i % 2, k0:(n + 1) * P], start=True, stop=True)
                        end(mm, "swa_s", n, i)
                if n >= 1:
                    q = n - 1
                    for i in range(8):
                        pe.wait_ge(sw_e, SWA_H * q + 2 * i + 2)
                        o = start("swa_pT", q, i)
                        for m in range(2):
                            for kt in range(1 if q == 0 else 0, 2):
                                c = (2 * m + kt) * P
                                mm = pe.transpose(o[:, c:c + P], b_s[q % 2][:, 2 * i + m, kt * P:(kt + 1) * P],
                                                  ident[:])
                        end(mm, "swa_pT", q, i)
                    for g in range(SWA_KV):
                        o = start("swa_o", q, g)
                        for hh in range(8):
                            h = 8 * g + hh
                            drained(pe, "swa_pT", q, h // 2)
                            for kt in range(1 if q == 0 else 0, 2):
                                mm = pe.matmul(o[:, hh * SWA_D:(hh + 1) * SWA_D],
                                               b_pT[:, h * SWA_W + kt * P:h * SWA_W + (kt + 1) * P],
                                               b_kv[:, q - 1 + kt, P + g * SWA_D:P + (g + 1) * SWA_D],
                                               start=(kt == (1 if q == 0 else 0)), stop=(kt == 1))
                        end(mm, "swa_o", q, g)
            for k in range(KD):
                transposes(("zT_b", k), lambda t: b_z[:, t, k * P:(k + 1) * P],
                           lambda t: pe.wait_ge(sw_zg, SWA_KV * (t + 1)))
            output("b_out", [("zT_b", k) for k in range(KD)], 1)

            stream_transposes("xT_c", c_xn, 2)
            for n, width in enumerate((Q_LAT, KV_LAT, ROPE, BANK, BANK, BANK)):
                if n == 2:
                    arrived(pe, "c_in", 2, 0)
                    w = raw("c_in", 2, 0)
                    for t in range(NT):
                        o = start("c_in", 2, t)
                        for k in range(KD):
                            for x in (x_hi, x_lo["c"]):
                                mm = pe.matmul(o[:, 0:ROPE], x[:, k, t * P:(t + 1) * P].bitcast(F32), w[:, k, :],
                                               start=(k == 0 and x is x_hi), stop=(k == KD - 1 and x is not x_hi))
                        end(mm, "c_in", 2, t)
                    continue
                project([("c_in", n, t) for t in range(NT)], [x.name for x in splits if x.name[0:2] == ("c_in", n)],
                        (x_hi, x_lo["c"], 0), True, width, ready=2 * KD if n == 0 else None)
            for i in range(3):
                transposes(("qlT", i), lambda t: c_ql[:, t, i * P:(i + 1) * P],
                           lambda t: drained(pe, "c_in", 0, t))
            for i in range(2):
                transposes(("kvlT", i), lambda t: c_kvl[:, t, i * P:(i + 1) * P],
                           lambda t: drained(pe, "c_in", 1, t))
            for i in range(3):
                drained(pe, "qlT", i)
            for p in range(3):
                arrived(pe, "q_up", 0, p)
            w = lambda k: raw("q_up", 0, k)[:, 0, :]
            for t in range(NT):
                tokens_by_features(("q_nope", t), c_qlT, w, 3, 0, 512, t)
                tokens_by_features(("q_rope", t), c_qlT, w, 3, 512, 256, t)
            for i in range(2):
                drained(pe, "kvlT", i)
            for p in range(2):
                arrived(pe, "kv_up", 0, p)
            w = lambda k: raw("kv_up", 0, k)[:, 0, :]
            for t in range(NT):
                tokens_by_features(("k_nope", t), c_kvlT, w, 2, 0, 512, t)
                tokens_by_features(("v_up", t), c_kvlT, w, 2, 512, 512, t)
            pe.wait_ge(rope_done, 1)
            for h in range(DIFF_H):
                transposes(("qdT", h), lambda t: c_dqr[:, t, h * P:(h + 1) * P])
                transposes(("kdT", h), lambda t: c_dkr[:, t, h * P:(h + 1) * P])
            transposes(("kpeT", 0), lambda t: c_kper[:, t, :, :].rearrange("p a d -> p (a d)"))
            for h in range(MLA_H):
                transposes(("qnT", h), lambda t: c_qn[:, t, h * P:(h + 1) * P],
                           lambda t: drained(pe, "q_nope", t))
                transposes(("knT", h), lambda t: c_kn[:, t, h * P:(h + 1) * P],
                           lambda t: drained(pe, "k_nope", t))
            pe.wait_ge(rope_done, 2)
            for i in range(2):
                transposes(("qrT", i), lambda t: c_qrr[t][:, i * P:(i + 1) * P])
            for h in range(MLA_H):
                drained(pe, "qnT", h)
                drained(pe, "knT", h)
                drained(pe, "qdT", h)
                drained(pe, "kdT", h)
            drained(pe, "kpeT", 0)
            for i in range(2):
                drained(pe, "qrT", i)
            n_units = len(att_units)
            for n in range(n_units + 3):
                if n < n_units:
                    kind, h, i = att_units[n]
                    q, N = slice(i * P, (i + 1) * P), (i + 1) * P
                    o = start("att_s", n, 0)
                    if kind == "m":
                        pe.matmul(o[:, 0:N], c_qnT[:, h, q], c_knT[:, h, 0:N], start=True, stop=False)
                        mm = pe.matmul(o[:, 0:N], c_qrT[:, h // 2, q], c_kpeT[:, h % 2, 0:N], start=False, stop=True)
                        end(mm, "att_s", n, 0)
                    else:
                        mm = pe.matmul(o[:, 0:N], c_qdT[:, h, q], c_kdT[:, h, 0, 0:N], start=True, stop=True)
                        end(mm, "att_s", n, 0)
                        o = start("att_s", n, 1)
                        mm = pe.matmul(o[:, 0:N], c_qdT[:, h, q], c_kdT[:, h, 1, 0:N], start=True, stop=True)
                        end(mm, "att_s", n, 1)
                if n >= 3:
                    m = n - 3
                    kind, h, i = att_units[m]
                    drained(pe, "att_pT", m)
                    v = c_v if kind == "m" else c_dv
                    if m in (0, MLA_H * NT):
                        for t in range(NT):
                            drained(pe, *(("v_up", t) if kind == "m" else ("c_in", 5, t)))
                    o = start("att_o", m)
                    for kt in range(i + 1):
                        mm = pe.matmul(o[:, 0:P], c_pT[:, m % 8, kt * P:(kt + 1) * P], v[:, kt, h * P:(h + 1) * P],
                                       start=(kt == 0), stop=(kt == i))
                    end(mm, "att_o", m)
                if 2 <= n < n_units + 2:
                    m = n - 2
                    kind, h, i = att_units[m]
                    o = start("att_pT", m)
                    if kind == "m":
                        pe.wait_ge(at_p, m + 1)
                        sl = m % 8
                    else:
                        pe.wait_ge(at_w, 2 * (m - 16) + 2)
                        sl = (2 * m) % 8
                    for kt in range(i + 1):
                        mm = pe.transpose(o[:, kt * P:(kt + 1) * P], c_s[:, sl, kt * P:(kt + 1) * P], ident[:])
                    end(mm, "att_pT", m)
            for k in range(KD):
                src = c_om if k < 4 else c_od
                u0 = (k % 4) * NT + (0 if k < 4 else 16)
                transposes(("mT", k), lambda t: src[:, t, (k % 4) * P:(k % 4 + 1) * P],
                           lambda t: drained(pe, "att_o", u0 + t))
            output("c_out", [("mT", k) for k in range(KD)], 1)

            stream_transposes("xT_d", d_xn, 3)
            for f in range(2 * PEER_H + 1):
                if f < 2 * PEER_H:
                    pe.wait_ge(w_split, split_at["pq", f, 0] + 1)
                    w_parts = high_low("pq", f, 0)
                    o = start("pqT", f)
                    for k in range(KD):
                        if f == 0:
                            pe.wait_ge(d_low, k + 1)
                        for n, (w, v) in enumerate(((0, d_hi), (1, d_hi), (0, d_lo))):
                            mm = pe.matmul(o, w_parts[w][:, k, :], v[:, k, :], start=(k == 0 and n == 0),
                                           stop=(k == KD - 1 and n == 2))
                    end(mm, "pqT", f)
                if f >= 1:
                    g = f - 1
                    if g == 0:
                        pe.wait_ge(keys_loaded, 16)
                    drained(pe, "pqT", g)
                    o = start("peer_s", g)
                    for t in range(NT):
                        mm = pe.matmul(o[:, t * NKEYS:(t + 1) * NKEYS], d_qT[:, g % 2, t * P:(t + 1) * P],
                                       keys[:, g, :], start=True, stop=True)
                    end(mm, "peer_s", g)
                if f == 2 * PEER_H - 2:
                    for i in range(GATHERED * 2):
                        t, half = i // 2, i % 2
                        o = start("h2", i)
                        for k in range(4):
                            mm = pe.transpose(o[:, k * P:(k + 1) * P], hT[:, half * 4 + k, t * P:(t + 1) * P], ident[:])
                        end(mm, "h2", i)
            def spread_gates(m, s):
                pe.wait_ge(hot_ready, m + 1)
                pe.wait_ge(spread_kept, m + 1)
                for t in range(BATCH):
                    for part in range(PARTS):
                        mm = pe.matmul(ps[:, 6 + s, t * QKEYS:(t + 1) * QKEYS], hot_i[s][:, :, t],
                                       hot_j[s][part][:, :, t], start=(part == 0), stop=(part == PARTS - 1))
                mm.then_inc(spread_summed, 1)

            def dense_u(s, load):
                pe.wait_ge(u_loaded[s], load)
                for j in range(PAIR):
                    for k in range(KD):
                        mm = pe.matmul(ps[:, 4 + s, j * DT:(j + 1) * DT], u_ring[:, s, j, k, :],
                                       hT[:, k, GATHERED * P:T], start=(k == 0), stop=(k == KD - 1))
                mm.then_inc(u_done, 1)

            def dense_v(n, s, load, last=False):
                pe.wait_ge(v_loaded[s], load)
                pe.wait_ge(dense_coef, n + 1)
                for j in range(PAIR):
                    for t in range(DENSE):
                        for half in range(2):
                            mm = pe.matmul(ps[:, 2 * t + half, :],
                                           tmp[:, s, j * DT + t * P:j * DT + (t + 1) * P],
                                           v_ring[:, s, j, half * BANK:(half + 1) * BANK],
                                           start=False, stop=last and j == PAIR - 1, skip_group_check=True)
                mm.then_inc(v_done, 1)

            drained(pe, "pqT", 2 * PEER_H - 1)
            dense_u(0, 16)
            pe.wait_ge(routed, 2)
            for i in range(3):
                o = start("pairs", i)
                src = r_sel[:, i, :, :, :] if i < 2 else r_g
                for t in range(DENSE):
                    mm = pe.transpose(o[:, t * P:(t + 1) * P],
                                      src[:, EARLY.index(GATHERED + t), :, :].rearrange("p h k -> p (h k)"), ident[:])
                end(mm, "pairs", i)

            for b in range(NB):
                last = max(j for j in jobs.number.values() if j % NB == b)
                pe.wait_ge(bank_free[b], last // NB + 1)
            pe.wait_ge(y_zero, 1)
            for b in range(2 * DENSE):
                pe.matmul(ps[:, b, :], r_y[:, 0:P], r_y[:, 0:BANK], start=True, stop=True)

            pe.sem_inc(spread_summed, 2)
            pe.sem_inc(v_done, 2)
            with pe.Fori(0, QSTEPS // 2) as turn:
                for s in range(2):
                    spread_gates(turn * 2 + s, s)
            for q in range(QUARTERS):
                with pe.Fori(0, QSTEPS // 2 - (q == QUARTERS - 1)) as turn:
                    for s in range(2):
                        n = turn * 2 + (q * QSTEPS + s)
                        pe.wait_ge(dense_gelu, n + 1)
                        dense_u(1 - s, (turn + (q * QSTEPS // 2 + s)) * 16 + 16)
                        if q + 1 < QUARTERS:
                            spread_gates(n + QSTEPS, s)
                        dense_v(n, s, (turn + q * QSTEPS // 2) * 16 + 16)
            pe.wait_ge(dense_gelu, STEPS - 1)
            dense_u(1, STEPS // 2 * 16)
            for n in (STEPS - 2, STEPS - 1):
                dense_v(n, n % 2, STEPS // 2 * 16, n == STEPS - 1)

        @block.vector
        def _(dve):
            def stream_norm(n, xn, t):
                dve.wait_ge(rr_done, NT * n + t + 1)
                dve.tensor_scalar(xn[:, t, :], xres[:, t, :], stat[:, 2, t:t + 1], None, ALU.mult).then_inc(xn_done, 1)

            def add_residual(name, n, xn, gate=None):
                for half in range(2):
                    for t in range(NT):
                        if half == 1 and t >= 1:
                            stream_norm(n, xn, t - 1)
                        if name == "a_out" and half == 0 and t == 0:
                            dve.wait_ge(x_again, 16 * NT)
                        o = full(dve, name, half, t)
                        x = xres[:, t, half * BANK:(half + 1) * BANK]
                        if gate is None:
                            taken(dve.tensor_tensor(x, x, o, ALU.add), name, half, t)
                        else:
                            i = half * NT + t
                            dve.tensor_tensor(tmp[:, i % 2, :], o, gate[:, half * BANK:(half + 1) * BANK],
                                              ALU.mult).then_inc(out_tmp, 1)
                            dve.wait_ge(out_tmp, i + 1)
                            taken(dve.tensor_tensor(x, x, tmp[:, i % 2, :], ALU.add), name, half, t)
                stream_norm(n, xn, NT - 1)

            def ada(n):
                if n >= 1:
                    full(dve, "ada", n - 1)
                for k in range(KD):
                    if k % 2 == 0:
                        arrived(dve, "ada", n, k // 2)
                    w = raw("ada", n, k // 2)[:, k % 2, :]
                    if k == 0:
                        dve.tensor_scalar(ysum[:], w, csil[:, k:k + 1], None, ALU.mult).then_inc(ada_step, 1)
                    else:
                        dve.wait_ge(ada_step, KD * n + k)
                        dve.scalar_tensor_tensor(ysum[:], w, csil[:, k:k + 1], ysum[:],
                                                 ALU.mult, ALU.add).then_inc(ada_step, 1)

            def ada_out(n):
                part, half = ADA_ORDER[n] // 2, ADA_ORDER[n] % 2
                o = full(dve, "ada", n)
                if part in (2, 5):
                    g = gates[:, part // 3, half * BANK:(half + 1) * BANK]
                    taken(dve.tensor_tensor(g, o, g, ALU.add), "ada", n)
                else:
                    taken(dve.tensor_tensor(modcol[:, part, half * 4:half * 4 + 4], o[:, 0:4],
                                            col("ada_b", part * KD + half * 4, 4), ALU.add), "ada", n)

            for t in range(NT):
                stream_norm(0, a_xn, t)
            dve.wait_ge(const_loaded, 32)
            for k in range(KD):
                o = full(dve, "xT_a", k)
                dve.wait_ge(x_high, k + 1)
                taken(dve.scalar_tensor_tensor(x_lo["a"][:, k, :], o, col("a_g", k), x_hi[:, k, :], ALU.mult,
                                               ALU.subtract), "xT_a", k)
            for k in range(KD):
                drained(dve, "xT_a", k)
                dve.sem_inc(x_low, 1)
            o = full(dve, "bias", 0)
            dve.wait_ge(row_loaded, 16 * 7)
            dve.tensor_tensor(bias_mask, o[0:SWA_H, 0:384], bias_mask, ALU.add).then_inc(bias_done, 1)
            dve.wait_ge(bias_done, 1)
            taken(dve.tensor_scalar(bias_mask, bias_mask, float(SWA_D ** 0.5), None, ALU.mult), "bias", 0)
            dve.wait_ge(silu_c, 1)
            dve.wait_ge(ret_loaded, 32)
            for n in range(12):
                if n < ADA_IN_A:
                    ada(n)
                if n < RET_H:
                    for i, dst in enumerate((a_q, a_k)):
                        e, o = full(dve, "a_in", n, 2 * i), full(dve, "a_in", n, 2 * i + 1)
                        u = 2 * n + i
                        if n == RET_H - 1:
                            dve.wait_ge(bias_kept, 16)
                        if u >= 1:
                            dve.wait_ge(qk_done, 2 * u)
                        cos, sin = trigA[:, 0, :], trigA[:, 1, :]
                        dve.tensor_tensor(dst[:, n, 0, :], e, cos, ALU.mult).then_inc(qk_tmp, 1)
                        dve.tensor_tensor(tmp[:, 0, :], o, sin, ALU.mult).then_inc(qk_tmp, 1)
                        taken(dve.tensor_tensor(dst[:, n, 1, :], o, cos, ALU.mult), "a_in", n, 2 * i + 1)
                        taken(dve.tensor_tensor(tmp[:, 1, :], e, sin, ALU.mult), "a_in", n, 2 * i)
                        dve.wait_ge(qk_tmp, 2 * (u + 1))
                        dve.tensor_tensor(dst[:, n, 0, :], dst[:, n, 0, :], tmp[:, 0, :],
                                          ALU.subtract).then_inc(qk_done, 1)
                        drained(dve, "a_in", n, 2 * i + 1)
                        drained(dve, "a_in", n, 2 * i)
                        dve.tensor_tensor(dst[:, n, 1, :], dst[:, n, 1, :], tmp[:, 1, :],
                                          ALU.add).then_inc(qk_done, 1)
                if n < ADA_IN_A:
                    ada_out(n)
            for h in range(RET_H + 1):
                if h < RET_H:
                    for j in range(NT):
                        o = full(dve, "ret_s", h, j)
                        if h >= 2:
                            full(dve, "ret_o", h - 2, NT - 1)
                        taken(dve.tensor_tensor(a_sT[:, h % 2, j, 0:T - j * P], o[:, 0:T - j * P],
                                                decay[:, h, 0:T - j * P], ALU.mult), "ret_s", h, j)
                if h >= 1:
                    for i in range(NT):
                        u = (h - 1) * NT + i
                        dve.wait_ge(z_r, u + 1)
                        drained(dve, "a_in", 8 + h - 1, i)
                        o = full(dve, "ret_o", h - 1, i)
                        z = a_z[:, i, (h - 1) * BANK:h * BANK]
                        taken(dve.scalar_tensor_tensor(z, o, rstat[:, 2, u:u + 1], z, ALU.mult, ALU.mult),
                              "ret_o", h - 1, i)
            for f in range(RET_K):
                o = full(dve, "zT_a", f)
                dve.wait_ge(o_high, f + 1)
                taken(dve.tensor_tensor(o_lo["a_out"][:, f, :], o, o_hi["a_out"][:, f, :], ALU.subtract), "zT_a", f)
            add_residual("a_out", 1, b_xn)

            for k in range(KD):
                o = full(dve, "xT_b", k)
                dve.wait_ge(x_high, KD + k + 1)
                if k % 2 == 0:
                    dve.tensor_scalar(b_kvT[:, k, :], o, col("kv_g", k), None, ALU.mult)
                taken(dve.scalar_tensor_tensor(x_lo["b"][:, k, :], o, col("b_g", k), x_hi[:, k, :], ALU.mult,
                                               ALU.subtract), "xT_b", k)
            for k in range(KD):
                drained(dve, "xT_b", k)
                dve.sem_inc(x_low, 1)
            dve.memset(b_kT[:], 0.0).then_inc(padded, 1)
            for t in range(NT):
                drained(dve, "kv", t)
            kview = b_kv[:, :, 0:P].rearrange("p t (g d) -> p t g d", d=SWA_D)
            ksq = tmp[:, 0, :].rearrange("p (t g d) -> p t g d", g=SWA_KV, d=SWA_D)
            dve.tensor_tensor(ksq, kview, kview, ALU.mult).then_inc(k_sq, 1)
            dve.wait_ge(k_sq, 1)
            kss = astat[:, 0, 0:8].rearrange("p (t g) -> p t g", g=SWA_KV)
            dve.tensor_reduce(kss, ksq, AX.X, ALU.add).then_inc(k_ss, 1)
            dve.wait_ge(k_r, 1)
            kr = astat[:, 2, 0:8].rearrange("p (t g) -> p t g", g=SWA_KV)
            for dup in range(2):
                dve.tensor_tensor(b_kn[:, :, :, dup, :], kview,
                                  kr.unsqueeze(3).to_broadcast([P, NT, SWA_KV, SWA_D]), ALU.mult).then_inc(k_n, 1)

            def hn_reduce(n):
                key, heads, width = hn_units[n]
                b = n % 4
                sq = sqbuf(n)[:, 0:heads * width].rearrange("p (h d) -> p h d", d=width)
                dve.wait_ge(hn_sq, n + 1)
                if n >= 4:
                    dve.wait_ge(hn_r, n - 3)
                dve.tensor_reduce(hstat[:, b, 0, 0:heads], sq, AX.X, ALU.add).then_inc(hn_ss, 1)

            def hn_scale(n, dst):
                key, heads, width = hn_units[n]
                dve.wait_ge(hn_r, n + 1)
                o = full(dve, *key)
                r = hstat[:, n % 4, 2, 0:heads].unsqueeze(2).to_broadcast([P, heads, width])
                taken(dve.tensor_tensor(dst.rearrange("p (h d) -> p h d", d=width),
                                        o[:, 0:heads * width].rearrange("p (h d) -> p h d", d=width),
                                        r, ALU.mult), *key)

            def hn_run(n0, n1, dst, after=None):
                for n in range(n0, n1 + 2):
                    if n < n1:
                        hn_reduce(n)
                    if n >= n0 + 2:
                        hn_scale(n - 2, dst(n - 2))
                        if after is not None:
                            after(n - 2)

            def b_dst(n):
                key = hn_units[n][0]
                return b_qn[:, key[2], key[1] * BANK:(key[1] + 1) * BANK]

            hn_run(0, 4, b_dst)
            ada(ADA_IN_A)
            hn_run(4, 8, b_dst)
            dve.wait_ge(gate_bias, 16)
            for n in range(3):
                ada_out(ADA_IN_A + n)
                ada(ADA_IN_A + n + 1)
            for g in range(SWA_KV):
                o = full(dve, "kT", g)
                if g == 0:
                    dve.wait_ge(padded, 1)
                dve.tensor_scalar(b_kT[0:64, g, 0, :], o[0:64, :], col("k_g")[0:64], None, ALU.mult)
                taken(dve.tensor_scalar(b_kT[64:128, g, 1, :], o[64:128, :], col("k_g")[64:128], None,
                                        ALU.mult), "kT", g)
            for i in range(KD):
                o = full(dve, "qT", i)
                taken(dve.tensor_scalar(b_qT[:, i, :], o, col("q_g"), None, ALU.mult), "qT", i)
            ada_out(ADA_IN_A + 3)
            for i, (part, g) in enumerate(((1, "n1_g"), (4, "n2_g"))):
                for c in range(2):
                    drained(dve, "ada", (2 if i == 0 else 6) + c)
                dve.scalar_tensor_tensor(modcol[:, part, :], modcol[:, part, :], 1.0, col(g, 0, KD),
                                         ALU.add, ALU.mult).then_inc(mod_done, 1)
            dve.wait_ge(bias_loaded, 16)
            m_, nm_, d_, l_, es_, rl_ = (astat[:, i, :] for i in range(6))
            for n in range(NT + 1):
                if n < NT:
                    w0 = P if n == 0 else 0
                    s = b_s[n % 2]
                    for i in range(8):
                        o = full(dve, "swa_s", n, i)
                        if n >= 2:
                            full(dve, "swa_pT", n - 2, 7)
                        if n >= 1:
                            dve.wait_ge(sw_nm, 2 * n)
                        for m in range(2):
                            h = 2 * i + m
                            mm = dve.tensor_tensor_reduce(
                                out=s[:, h, w0:SWA_W], in0=o[:, m * SWA_W + w0:(m + 1) * SWA_W],
                                in1=b_bias[:, h, w0:SWA_W], scale=float(SWA_D ** -0.5), scalar=LOWEST,
                                op0=ALU.add, op1=ALU.max, accum_out=m_[:, h:h + 1])
                            if m == 0:
                                mm.then_inc(sw_s, 1)
                        mm.then_inc(bank_free[jobs("swa_s", n, i)[0]], 1)
                    for i in range(8):
                        drained(dve, "swa_s", n, i)
                    dve.wait_ge(sw_s, 8 * (n + 1))
                    dve.tensor_tensor(m_, m_, row("sinks"), ALU.max).then_inc(sw_m, 1)
                    dve.wait_ge(sw_m, n + 1)
                    if n >= 1:
                        dve.wait_ge(sw_e, SWA_H * n)
                        dve.wait_ge(sw_es, n)
                    dve.tensor_scalar(nm_, m_, -1.0, None, ALU.mult).then_inc(sw_nm, 1)
                    dve.tensor_tensor(d_, row("sinks"), m_, ALU.subtract).then_inc(sw_nm, 1)
                if n >= 1:
                    q = n - 1
                    dve.wait_ge(sw_e, SWA_H * n)
                    dve.wait_ge(sw_es, n)
                    dve.tensor_tensor(l_, l_, es_, ALU.add).then_inc(sw_l, 1)
                    dve.wait_ge(sw_l, n)
                    if q >= 1:
                        dve.wait_ge(sw_zg, SWA_KV * q)
                    dve.reciprocal(rl_, l_).then_inc(sw_rl, 1)
                    for i in range(0, 8, 2):
                        o = full(dve, "swa_pT", q, i)
                        c0 = P if q == 0 else 0
                        dst = b_pT[:, 2 * i * SWA_W:(2 * i + 2) * SWA_W].rearrange("p (m c) -> p m c", m=2)
                        src = o.rearrange("p (m c) -> p m c", m=2)
                        if q >= 1:
                            full(dve, "swa_o", q - 1, SWA_KV - 1)
                        taken(dve.tensor_copy(dst[:, :, c0:SWA_W], src[:, :, c0:SWA_W]), "swa_pT", q, i)
                    for g in range(SWA_KV):
                        o = full(dve, "swa_o", q, g)
                        u = SWA_KV * q + g
                        if u >= 2:
                            dve.wait_ge(sw_zg, u - 1)
                        dve.wait_ge(sw_rl, q + 1)
                        ov = o.rearrange("p (h d) -> p h d", d=SWA_D)
                        tv = tmp[:, u % 2, :].rearrange("p (h d) -> p h d", d=SWA_D)
                        rl = rl_[:, 8 * g:8 * g + 8].unsqueeze(2).to_broadcast([P, 8, SWA_D])
                        dve.tensor_tensor(tv, ov, rl, ALU.mult).then_inc(bank_free[jobs("swa_o", q, g)[0]], 1)
                        drained(dve, "swa_o", q, g)
                        drained(dve, "b_in", 2 + g, q)
                        z = b_z[:, q, g * BANK:(g + 1) * BANK]
                        dve.tensor_tensor(z, tmp[:, u % 2, :], z, ALU.mult).then_inc(sw_zg, 1)
            for k in range(KD):
                o = full(dve, "zT_b", k)
                dve.wait_ge(o_high, RET_K + k + 1)
                taken(dve.tensor_tensor(o_lo["b_out"][:, k, :], o, o_hi["b_out"][:, k, :], ALU.subtract), "zT_b", k)
            add_residual("b_out", 2, c_xn)

            dve.wait_ge(mod_done, 2)
            for k in range(KD):
                o = full(dve, "xT_c", k)
                dve.wait_ge(x_high, 2 * KD + k + 1)
                if k >= 2:
                    dve.wait_ge(x_low, 2 * KD + k - 1)
                taken(dve.scalar_tensor_tensor(tmp[:, k % 2, :], o, modcol[:, 1, k:k + 1], x_hi[:, k, :], ALU.mult,
                                               ALU.subtract), "xT_c", k)
                drained(dve, "xT_c", k)
                dve.tensor_scalar(x_lo["c"][:, k, :], tmp[:, k % 2, :], modcol[:, 0, k:k + 1], None,
                                  ALU.add).then_inc(x_low, 1)
            for i in range(2):
                dve.tensor_tensor_reduce(out=ysum[:, i * ROPE:(i + 1) * ROPE], in0=row(f"lq{i + 1}"),
                                         in1=row(f"lk{i + 1}"), scale=1.0, scalar=0.0, op0=ALU.mult,
                                         op1=ALU.add, accum_out=lam[:, i:i + 1]).then_inc(lam_dve, 1)
            dve.wait_ge(lam_act, 1)
            dve.tensor_tensor(lam[:, 4:5], lam[:, 2:3], lam[:, 3:4], ALU.subtract).then_inc(lam_dve, 1)
            dve.wait_ge(lam_dve, 3)
            dve.tensor_scalar(lam[:, 5:6], lam[:, 4:5], LAMBDA_INIT, -1.0, ALU.add, ALU.mult).then_inc(lam_dve, 1)
            dve.tensor_scalar(lam[:, 6:7], col("sub_g"), 1.0 - LAMBDA_INIT, None, ALU.mult).then_inc(sub_done, 1)

            def c_dst(n):
                key = hn_units[n][0]
                if key[0] == "c_in":
                    return [c_ql, c_kvl, c_kpe, c_dq, c_dk][key[1]][:, key[2], :]
                return {"q_nope": c_qn, "q_rope": c_qr, "k_nope": c_kn}[key[0]][:, key[1], :]

            rope_n = [0]

            def rope(src, dst, heads, gain, t):
                x = src[:, t, :].rearrange("p (h d) -> p h d", d=ROPE)
                y = dst(t).rearrange("p (h d) -> p h d", d=ROPE)
                g = gain.unsqueeze(1).to_broadcast([P, heads, ROPE])
                cos = trig[:, 0, t, :].unsqueeze(1).to_broadcast([P, heads, HALF])
                sin = trig[:, 1, t, :].unsqueeze(1).to_broadcast([P, heads, HALF])
                n = heads * HALF
                t0 = spare[:, 0:n].rearrange("p (h d) -> p h d", d=HALF)
                t1 = spare[:, 256:256 + n].rearrange("p (h d) -> p h d", d=HALF)
                r0 = rope_n[0]
                if r0:
                    dve.wait_ge(rope_t, r0)
                dve.tensor_tensor(x, x, g, ALU.mult).then_inc(rope_t, 1)
                dve.wait_ge(rope_t, r0 + 1)
                a, b = x[:, :, 0:HALF], x[:, :, HALF:ROPE]
                dve.tensor_tensor(y[:, :, 0:HALF], a, cos, ALU.mult).then_inc(rope_t, 1)
                dve.tensor_tensor(t0, b, sin, ALU.mult).then_inc(rope_t, 1)
                dve.tensor_tensor(y[:, :, HALF:ROPE], b, cos, ALU.mult).then_inc(rope_t, 1)
                dve.tensor_tensor(t1, a, sin, ALU.mult).then_inc(rope_t, 1)
                dve.wait_ge(rope_t, r0 + 5)
                dve.tensor_tensor(y[:, :, 0:HALF], y[:, :, 0:HALF], t0, ALU.subtract).then_inc(rope_t, 1)
                dve.tensor_tensor(y[:, :, HALF:ROPE], y[:, :, HALF:ROPE], t1, ALU.add).then_inc(rope_t, 1)
                rope_n[0] = r0 + 7

            def c_rope(n):
                key, heads, width = hn_units[n]
                if key[1] >= 2:
                    drained(dve, *key)
                    src, dst, gain = ((c_kpe, lambda t: c_kper[:, t, 0, :], "mk_g"),
                                      (c_dq, lambda t: c_dqr[:, t, :], "dq_g"),
                                      (c_dk, lambda t: c_dkr[:, t, :], "dk_g"))[key[1] - 2]
                    rope(src, dst, heads, row(gain), key[2])

            hn_run(HN_SWA, HN_PROJ, c_dst, c_rope)
            dve.memset(c_kpeT[:], 0.0).then_inc(padded, 1)
            for i in range(3):
                o = full(dve, "qlT", i)
                taken(dve.tensor_scalar(c_qlT[:, i, :], o, col("qlat_g", i), None, ALU.mult), "qlT", i)
            for i in range(2):
                o = full(dve, "kvlT", i)
                taken(dve.tensor_scalar(c_kvlT[:, i, :], o, col("kvlat_g", i), None, ALU.mult), "kvlT", i)
            full(dve, "c_in", 5, NT - 1)
            dve.memset(c_kdT[:], 0.0).then_inc(padded, 1)
            dve.wait_ge(rope_t, rope_n[0])
            dve.tensor_copy(c_kper[:, :, 1, :], c_kper[:, :, 0, :]).then_inc(rope_t, 1)
            rope_n[0] += 1
            dve.wait_ge(rope_t, rope_n[0])
            dve.sem_inc(rope_done, 1)

            def q_rope(n):
                key, heads, width = hn_units[n]
                if key[0] == "q_rope":
                    drained(dve, *key)
                    rope(c_qr, lambda t: c_qrr[t], heads, row("mq_g"), key[1])

            hn_run(HN_PROJ, HN_PROJ + 8, c_dst, q_rope)
            dve.wait_ge(rope_t, rope_n[0])
            dve.sem_inc(rope_done, 1)
            hn_run(HN_PROJ + 8, HN_ALL, c_dst)
            for h in range(DIFF_H):
                o = full(dve, "qdT", h)
                taken(dve.tensor_copy(c_qdT[:, h, :], o), "qdT", h)
            o = full(dve, "kpeT", 0)
            dve.wait_ge(padded, 3)
            dve.tensor_copy(c_kpeT[0:64, 0, :], o[0:64, :])
            taken(dve.tensor_copy(c_kpeT[64:128, 1, :], o[64:128, :]), "kpeT", 0)
            for h in range(MLA_H):
                o = full(dve, "qnT", h)
                taken(dve.tensor_scalar(c_qnT[:, h, :], o, col("mq_g"), None, ALU.mult), "qnT", h)
            for i in range(2):
                o = full(dve, "qrT", i)
                taken(dve.tensor_copy(c_qrT[:, i, :], o), "qrT", i)

            n_units = len(att_units)

            def att_scores(n):
                kind, h, i = att_units[n]
                N = (i + 1) * P
                mask = causal[:, 384 - i * P:384 - i * P + N]
                for c in range(1 if kind == "m" else 2):
                    sl = (n if kind == "m" else 2 * n + c) % 8
                    o = full(dve, "att_s", n, c)
                    prev = n - (8 if kind == "m" else 4)
                    if kind == "d" and n < 20:
                        prev = 9 + 2 * (n - 16)
                    if prev >= 0:
                        full(dve, "att_pT", prev)
                    taken(dve.tensor_tensor_reduce(
                        out=c_s[:, sl, 0:N], in0=o[:, 0:N], in1=mask,
                        scale=float((NOPE + ROPE) ** -0.5 if kind == "m" else ROPE ** -0.5), scalar=LOWEST,
                        op0=ALU.add, op1=ALU.max, accum_out=astat[:, c, n % 16:n % 16 + 1]), "att_s", n, c)
                    drained(dve, "att_s", n, c)
                    if n >= 16:
                        dve.wait_ge(at_rl, n - 15)
                    dve.tensor_scalar(astat[:, 2 + c, n % 16:n % 16 + 1], astat[:, c, n % 16:n % 16 + 1], -1.0, None,
                                      ALU.mult).then_inc(at_nm, 1)

            def att_norm(n):
                kind, h, i = att_units[n]
                N = (i + 1) * P
                at = slice(n % 16, n % 16 + 1)
                if kind == "m":
                    dve.wait_ge(at_p, n + 1)
                    dve.reciprocal(astat[:, 6, at], astat[:, 4, at]).then_inc(at_rl, 1)
                else:
                    m = n - 16
                    dve.wait_ge(at_p, 16 + 2 * m + 2)
                    dve.reciprocal(astat[:, 6:8, at], astat[:, 4:6, at]).then_inc(at_rl, 1)
                    dve.wait_ge(at_rl, n + 1)
                    dve.wait_ge(lam_dve, 4)
                    p0, p1 = c_s[:, (2 * n) % 8, 0:N], c_s[:, (2 * n + 1) % 8, 0:N]
                    dve.tensor_scalar(p1, p1, astat[:, 7, at], lam[:, 5:6], ALU.mult, ALU.mult).then_inc(at_w, 1)
                    dve.wait_ge(at_w, 2 * m + 1)
                    dve.scalar_tensor_tensor(p0, p0, astat[:, 6, at], p1, ALU.mult, ALU.add).then_inc(at_w, 1)

            def att_clamp(n):
                kind, h, i = att_units[n]
                if kind == "d":
                    u = n - 16
                    o = full(dve, "att_o", n)
                    if u >= 2:
                        dve.wait_ge(od_sq, u - 1)
                    dve.tensor_scalar(tmp[:, u % 2, 0:P], o[:, 0:P], BIG, -BIG, ALU.min, ALU.max).then_inc(od_clamped, 1)

            def att_out(n):
                kind, h, i = att_units[n]
                at = slice(n % 16, n % 16 + 1)
                if kind == "m":
                    dve.wait_ge(at_rl, n + 1)
                    o = full(dve, "att_o", n)
                    taken(dve.tensor_scalar(c_om[:, i, h * P:(h + 1) * P], o[:, 0:P], astat[:, 6, at], None,
                                            ALU.mult), "att_o", n)
                else:
                    m = n - 16
                    dve.wait_ge(od_r, m + 1)
                    dve.scalar_tensor_tensor(rstat[:, 2, m:m + 1], rstat[:, 0, m:m + 1], SUM_MAX, rstat[:, 2, m:m + 1],
                                             ALU.is_le, ALU.mult).then_inc(od_rr, 1)
                    dve.wait_ge(od_rr, m + 1)
                    o = full(dve, "att_o", n)
                    taken(dve.tensor_scalar(c_od[:, i, h * P:(h + 1) * P], o[:, 0:P], rstat[:, 2, m:m + 1], None,
                                            ALU.mult), "att_o", n)

            for n in range(n_units + 4):
                if n < n_units:
                    att_scores(n)
                if 1 <= n <= n_units:
                    att_norm(n - 1)
                if 3 <= n < n_units + 3:
                    att_clamp(n - 3)
                if n >= 4:
                    att_out(n - 4)
            for k in range(KD):
                o = full(dve, "mT", k)
                dve.wait_ge(o_high, RET_K + KD + k + 1)
                hi, lo = o_hi["c_out"][:, k, :], o_lo["c_out"][:, k, :]
                if k < 4:
                    taken(dve.tensor_tensor(lo, o, hi, ALU.subtract), "mT", k)
                else:
                    taken(dve.scalar_tensor_tensor(lo, o, lam[:, 6:7], hi, ALU.mult, ALU.subtract), "mT", k)
            for n in range(4):
                drained(dve, "ada", ADA_IN_A + n)
            add_residual("c_out", 3, d_xn, gates[:, 0, :])

            for k in range(KD):
                o = full(dve, "xT_d", k)
                taken(dve.tensor_scalar(hT[:, k, :], o, modcol[:, 4, k:k + 1], modcol[:, 3, k:k + 1],
                                        ALU.mult, ALU.add), "xT_d", k)
                if k >= 2:
                    dve.wait_ge(d_high, k - 1)
                    dve.tensor_tensor(d_lo[:, k - 2, :], hT[:, k - 2, :], d_hi[:, k - 2, :], ALU.subtract).then_inc(d_low, 1)
            for k in range(KD - 2, KD):
                dve.wait_ge(d_high, k + 1)
                dve.tensor_tensor(d_lo[:, k, :], hT[:, k, :], d_hi[:, k, :], ALU.subtract).then_inc(d_low, 1)

            class Steps:

                def __init__(self, semaphore, before=0, hold=None):
                    self.semaphore, self.before, self.done, self.hold = semaphore, before, 0, hold

                def __call__(self, ins_):
                    ins_.then_inc(self.semaphore, 1)
                    self.done += 1

                def settle(self):
                    dve.wait_ge(self.semaphore, self.before + self.done)
                    if self.hold is not None:
                        self(dve.tensor_copy(self.hold, iota[:, 0:1]))

            def top16(step, src, scr, values, index):
                n = len(src)
                for a in range(n):
                    step(dve.max(values[a][:, 0:8], src[a]))
                step.settle()
                for a in range(n):
                    step(dve.max_index(index[a][:, 0:8], values[a][:, 0:8], src[a]))
                    step(dve.match_replace(scr[a], values[a][:, 0:8], src[a], LOWEST))
                step.settle()
                for a in range(n):
                    step(dve.max(values[a][:, 8:16], scr[a]))
                step.settle()
                for a in range(n):
                    step(dve.max_index(index[a][:, 8:16], values[a][:, 8:16], scr[a]))
                step.settle()

            def rank_keys(step, r, n, src):
                both = [(p, t) for p in range(2) for t in range(n)]
                top16(step, src, [r.scr[:, a, :] for a in range(2 * n)], [r.v[:, p, t, :] for p, t in both],
                      [r.idx[:, p, t, :] for p, t in both])
                step(dve.tensor_copy(r.idxf[:], r.idx[:]))
                wide = [P, n, WHOLE, TOPK]
                step(dve.tensor_tensor(r.cand[:, :, 0:WHOLE * TOPK].rearrange("p t (a b) -> p t a b", b=TOPK),
                                       r.v[:, 0, :, 0:WHOLE].unsqueeze(3).to_broadcast(wide),
                                       r.v[:, 1].unsqueeze(2).to_broadcast(wide), ALU.add))
                step(dve.tensor_tensor(r.cand[:, :, WHOLE * TOPK:SUMS], r.v[:, 0, :, WHOLE:TOPK],
                                       r.v[:, 1, :, 0:1].to_broadcast([P, n, TOPK - WHOLE]), ALU.add))
                step.settle()

            def rank_pairs(step, r, n, sums):
                pos = r.pos[:, 0, :].rearrange("p (t k) -> p t k", k=TOPK)
                top16(step, [r.cand[:, t, :] for t in range(n)], [r.cscr[:, t, :] for t in range(n)],
                      [sums[:, t, :] for t in range(n)], [pos[:, t, :] for t in range(n)])
                step(dve.tensor_scalar(r.pos[:, 1, :], r.pos[:, 0, :], 4, None, ALU.logical_shift_right))
                step(dve.tensor_scalar(r.pos[:, 2, :], r.pos[:, 0, :], 15, None, ALU.bitwise_and))
                step.settle()
                step(dve.tensor_copy(r.posf[:], r.pos[:, 1:3, :]))
                step.settle()
                row, column, past = r.posf[:, 0, :], r.posf[:, 1, :], r.past
                step(dve.scalar_tensor_tensor(past, row, float(WHOLE), column, ALU.is_ge, ALU.mult))
                step.settle()
                step(dve.tensor_tensor(row, row, past, ALU.add))
                step(dve.tensor_tensor(column, column, past, ALU.subtract))
                step.settle()

            def one_hot_place(step, r, n, a, eq):
                step(dve.tensor_tensor(eq, r.posf[:, a, :].unsqueeze(2).to_broadcast([P, n * TOPK, TOPK]),
                                       iota[:, 0:TOPK].unsqueeze(1).to_broadcast([P, n * TOPK, TOPK]), ALU.is_equal))

            def pick(step, r, n, a, eq, numbers):
                eq = eq.rearrange("p (t k) a -> p t k a", k=TOPK)
                step(dve.tensor_tensor(eq, eq, r.idxf[:, a].unsqueeze(2).to_broadcast([P, n, TOPK, TOPK]), ALU.mult))
                step.settle()
                step(dve.tensor_reduce(numbers, eq, AX.X, ALU.add))
                step.settle()

            step = Steps(route)
            for h in range(PEER_H):
                r = early[h % 2]
                for p in range(2):
                    drained(dve, "peer_s", 2 * h + p)
                if h >= 2:
                    dve.wait_ge(picked, 2 * (h - 1))
                rank_keys(step, r, NE, [d_s[:, (2 * h + p) % 4, t, :] for p in range(2) for t in EARLY])
                dve.sem_inc(ranked, 1)
                rank_pairs(step, r, NE, r_g[:, :, h, :])
                for a in range(2):
                    one_hot_place(step, r, NE, a, pick_eq[h % 2][a])
                step.settle()
                dve.sem_inc(placed, 1)
            pick(step, r, NE, 1, pick_eq[h % 2][1], r_sel[:, 1, :, h, :])
            full(dve, "pqT", 2 * PEER_H - 1)
            by_head = [P, NE * PEER_H, TOPK]
            g_all = r_g[:].rearrange("p t h k -> p (t h) k")
            choices = lambda v: v[:, 0, :, :].rearrange("p h k -> p (h k)")
            step(dve.tensor_reduce(r_sum[:, 0, :], g_all, AX.X, ALU.max))
            dve.wait_ge(picked, 2 * PEER_H - 1)
            step(dve.scalar_tensor_tensor(eidx[:, 0:SLOTS], choices(r_sel[:, 0]), float(NKEYS), choices(r_sel[:, 1]),
                                          ALU.mult, ALU.add))
            step.settle()
            dve.sem_inc(gathering, 1)
            step(dve.tensor_tensor(g_all, g_all, r_sum[:, 0, :].unsqueeze(2).to_broadcast(by_head), ALU.subtract))
            step.settle()
            dve.sem_inc(routed, 1)
            dve.memset(r_y, 0.0).then_inc(y_zero, 1)
            dve.wait_ge(route_e, 1)
            step(dve.tensor_reduce(r_sum[:, 0, :], g_all, AX.X, ALU.add))
            step.settle()
            step(dve.reciprocal(r_sum[:, 1, :], r_sum[:, 0, :]))
            step.settle()
            step(dve.tensor_tensor(g_all, g_all, r_sum[:, 1, :].unsqueeze(2).to_broadcast(by_head), ALU.mult))
            step.settle()
            dve.sem_inc(routed, 1)
            step(dve.tensor_copy(g_kept[:, 0:SLOTS], choices(r_g)))
            for i, dst in enumerate((iT, jT)):
                o = full(dve, "pairs", i)
                taken(dve.tensor_copy(dst, o[:, 0:DT]), "pairs", i)
            o = full(dve, "pairs", 2)
            split = Steps(gate_part)
            split(dve.tensor_copy(gT[0], o[:, 0:DT]))
            split.settle()
            split(dve.tensor_tensor(g_rest[0], o[:, 0:DT], gT[0], ALU.subtract))
            split.settle()
            split(dve.tensor_copy(gT[1], g_rest[0]))
            split.settle()
            split(dve.tensor_tensor(g_rest[1], g_rest[0], gT[1], ALU.subtract))
            split.settle()
            taken(dve.tensor_copy(gT[2], g_rest[1]), "pairs", 2)
            for i in range(3):
                drained(dve, "pairs", i)
            step.settle()
            dve.wait_ge(iota_ready, 1)

            def one_hots(q, m, t0, s):
                of = lambda v, n: v[:, bass.ds(t0, BATCH)].unsqueeze(1).to_broadcast([P, n, BATCH])
                dve.wait_ge(spread_summed, m + 1)
                dve.tensor_tensor(hot_j[s][2], of(jT, QKEYS), wide_iota[:, q * QKEYS:(q + 1) * QKEYS, :],
                                  ALU.is_equal).then_inc(hot_step, 1)
                dve.tensor_tensor(hot_i[s], of(iT, NKEYS), wide_iota, ALU.is_equal)
                dve.wait_ge(hot_step, m + 1)
                for part in range(PARTS):
                    last = dve.tensor_tensor(hot_j[s][part], hot_j[s][2], of(gT[part], QKEYS), ALU.mult)
                last.then_inc(hot_ready, 1)

            with dve.Fori(0, QSTEPS // 2) as turn:
                for s in range(2):
                    one_hots(0, turn * 2 + s, turn * (2 * BATCH) + s * BATCH, s)

            def gather_u(u, block):
                turn = block + 2 * u * QSTEPS
                for r in range(2 * GATHER):
                    dve.wait_ge(g_loaded[r], turn * 16 + 16)
                    dve.tensor_tensor_reduce(out=experts[:, r, :], in0=experts[:, r, :], in1=d_h2[:, u, :],
                                             scale=1.0, scalar=0.0, op0=ALU.mult, op1=ALU.add,
                                             accum_out=r_astage[:, r:r + 1]).then_inc(g_used[r // GATHER], 1)
                for half in range(2):
                    dve.wait_ge(g_used[half], turn * GATHER + 2 * GATHER)
                dve.tensor_copy(r_a[:, bass.ds(block * 2 * GATHER, 2 * GATHER)], r_astage[:]).then_inc(g_dve, 1)
                dve.wait_ge(g_dve, block + (u * QSTEPS + 1))

            def gather_v(u, block):
                turn = block + (2 * u + 1) * QSTEPS
                dve.tensor_copy(r_cstage[:], r_coef[:, bass.ds(block * 2 * GATHER, 2 * GATHER)]).then_inc(y_step, 1)
                base = (block + u * QSTEPS) * (2 * GATHER + 1)
                for half in range(2):
                    for r in range(half * GATHER, (half + 1) * GATHER):
                        dve.wait_ge(y_step, base + r + 1)
                        dve.wait_ge(g_loaded[r], turn * 16 + 16)
                        dve.scalar_tensor_tensor(r_y, experts[:, r, :], r_cstage[:, r:r + 1], r_y,
                                                 ALU.mult, ALU.add).then_inc(y_step, 1)
                    dve.wait_ge(y_step, base + (half + 1) * GATHER + 1)
                    dve.sem_inc(g_used[half], GATHER)

            LATE_KEYS, LATE_PAIRS = 20, 35

            def late_keys(h, l):
                step = Steps(late_step, h * (LATE_KEYS + LATE_PAIRS), l.hold)
                step(dve.tensor_copy(l.stage[:], late_keep[:, bass.ds(h * 2, 2), :]))
                step.settle()
                rank_keys(step, l.rank, 1, [l.stage[:, p, :] for p in range(2)])
                assert step.done == LATE_KEYS, step.done

            def late_pairs(h, l):
                step = Steps(late_step, h * (LATE_KEYS + LATE_PAIRS) + LATE_KEYS, l.hold)
                rank_pairs(step, l.rank, 1, l.g)
                for a in range(2):
                    one_hot_place(step, l.rank, 1, a, l.rank.eq[:])
                    step.settle()
                    pick(step, l.rank, 1, a, l.rank.eq[:], l.out[:, a, :].unsqueeze(1))
                at = bass.ds(h * TOPK, TOPK)
                step(dve.tensor_copy(g_kept[:, SLOTS:2 * SLOTS][:, at], l.g[:, 0, :]))
                for a in range(2):
                    step(dve.tensor_copy(late_sel[a][:, at], l.out[:, a, :]))
                step.settle()
                assert step.done == LATE_PAIRS, step.done

            def late_softmax(late_sum):
                step = Steps(late_step, PEER_H * (LATE_KEYS + LATE_PAIRS))
                g = g_kept[:, SLOTS:2 * SLOTS].rearrange("p (h k) -> p h k", k=TOPK)
                by_head = [P, PEER_H, TOPK]
                step(dve.scalar_tensor_tensor(eidx[:, SLOTS:2 * SLOTS], late_sel[0], float(NKEYS), late_sel[1],
                                              ALU.mult, ALU.add))
                step(dve.tensor_reduce(late_sum[:, 0, :], g, AX.X, ALU.max))
                step.settle()
                dve.sem_inc(gathering, 1)
                step(dve.tensor_tensor(g, g, late_sum[:, 0, :].unsqueeze(2).to_broadcast(by_head), ALU.subtract))
                step.settle()
                dve.sem_inc(late_done, 1)
                dve.wait_ge(route_e, 2)
                step(dve.tensor_reduce(late_sum[:, 0, :], g, AX.X, ALU.add))
                step.settle()
                step(dve.reciprocal(late_sum[:, 1, :], late_sum[:, 0, :]))
                step.settle()
                step(dve.tensor_tensor(g, g, late_sum[:, 1, :].unsqueeze(2).to_broadcast(by_head), ALU.mult))
                step.settle()

            for q in range(QUARTERS):
                u, phase = q // 2, q % 2
                dve.wait_ge(spread_kept, (q + 1) * QSTEPS + 2)
                if q == 0:
                    dve.wait_ge(late_kept, 1)
                unrolled = 2 * QSTEPS // PEER_H if q < 2 else 2
                with dve.Fori(0, QSTEPS // unrolled) as turn:
                    for s in range(unrolled):
                        n = turn * unrolled + (q * QSTEPS + s)
                        dve.wait_ge(dense_gelu, n + 2)
                        gated = tmp[:, s % 2, :].rearrange("p (j t) -> p j t", t=DT)
                        at = bass.ds(turn * (unrolled * PAIR) + s * PAIR, PAIR)
                        dve.tensor_tensor(gated, gated, spread[q % 2][:, at, :], ALU.mult).then_inc(dense_coef, 1)
                        if q + 1 < QUARTERS:
                            one_hots(q + 1, n + QSTEPS, turn * (unrolled * BATCH) + s * BATCH, s % 2)
                        if q < 2 and s == 0:
                            late_keys(turn + q * (PEER_H // 2), late[q])
                        if q < 2 and s == unrolled // 2:
                            late_pairs(turn + q * (PEER_H // 2), late[q])
                        if phase == 0:
                            gather_u(u, turn * unrolled + s)
                        else:
                            gather_v(u, turn * unrolled + s)
                if q == 1:
                    late_softmax(late[1].sum)
                if phase == 0:
                    dve.sem_inc(a_ready, 1)
                    dve.wait_ge(gelu_done, u + 1)
                    dve.tensor_tensor(r_coef[:], r_coef[:], g_kept[:, u * SLOTS:(u + 1) * SLOTS],
                                      ALU.mult).then_inc(coef_done, 1)
                    dve.memset(r_y, 0.0).then_inc(y_zero, 1)
                    dve.wait_ge(y_zero, u + 2)
                    dve.wait_ge(coef_done, u + 1)
                else:
                    dve.tensor_tensor(r_y, r_y, gates[:, 1, :], ALU.mult).then_inc(out_tmp, 1)
                    dve.wait_ge(out_tmp, 8 + u + 1)
                    dve.tensor_tensor(xres[:, u, :], xres[:, u, :], r_y, ALU.add).then_inc(out_ready, 1)
                    dve.wait_ge(out_ready, u + 1)
            dve.wait_ge(v_done, STEPS + 2)
            for t in range(DENSE):
                for half in range(2):
                    i = 2 * t + half
                    at = slice(half * BANK, (half + 1) * BANK)
                    dve.tensor_tensor(tmp[:, i % 2, :], ps[:, i, :], gates[:, 1, at], ALU.mult).then_inc(out_tmp, 1)
                    dve.wait_ge(out_tmp, 8 + GATHERED + i + 1)
                    x = xres[:, GATHERED + t, at]
                    add = dve.tensor_tensor(x, x, tmp[:, i % 2, :], ALU.add)
                    add.then_inc(out_half, 1)
                    dve.wait_ge(out_half, i + 1)
                dve.sem_inc(out_ready, 1)

        @block.scalar
        def _(act):
            act.dma_start(rows[:], ins["rows"]).then_inc(row_loaded, 16)
            act.dma_start(iota[:], ins["iota"]).then_inc(row_loaded, 16)
            act.dma_start(causal, ins["causal"]).then_inc(row_loaded, 16)
            act.dma_start(trig[:], ins["trig"]).then_inc(row_loaded, 16)
            act.dma_start(bias_w, ins["rel_bias"]).then_inc(row_loaded, 16)
            act.dma_start(bias_hot, ins["bias_hot"]).then_inc(row_loaded, 16)
            act.dma_start(bias_mask, ins["bias_mask"]).then_inc(row_loaded, 16)

            split_n = [0]

            def high_parts(end):
                while split_n[0] < min(end, len(splits)):
                    q = split_n[0]
                    piece = splits[q]
                    if q >= NPIECE:
                        used(act, splits[q - NPIECE])
                    arrived(act, *piece.name)
                    n = piece.src.shape[1]
                    at = place[piece.name] % NPIECE * PIECE
                    act.activation(w_hi[q % NPIECE][:, 0:n], ring[:, at:at + n], ACT.Copy).then_inc(w_high, 1)
                    split_n[0] += 1

            def high_parts_for(*name):
                high_parts(split_at[name] + NPIECE)

            def stream_squares(n, xn, ready):
                for t in range(NT):
                    ready(t)
                    act.activation(xn[:, t, :], xres[:, t, :], ACT.Square,
                                   accum_out=stat[:, 0, t:t + 1]).then_inc(sq_done, 1)

            stream_squares(0, a_xn, lambda t: act.wait_ge(x_loaded[t], 16))
            act.wait_ge(const_loaded, 32)
            high_parts(NPIECE)
            for k in range(KD):
                o = full(act, "xT_a", k)
                act.activation(x_hi[:, k, :], o, ACT.Copy, scale=col("a_g", k)).then_inc(x_high, 1)
            act.activation(csil[:], col("c", 0, KD), ACT.Silu).then_inc(silu_c, 1)
            drained(act, "bias", 0)
            act.dma_start(ins["bias_rows"].rearrange("p h u -> h p u"),
                          bias_mask.unsqueeze(1).to_broadcast([SWA_H, P, 384])).then_inc(bias_kept, 16)
            for n in range(12):
                high_parts_for("a_in", n, 3)
                for t in range(NT) if n >= RET_H else ():
                    o = full(act, "a_in", n, t)
                    if n < 2 * RET_H:
                        taken(act.activation(a_v[:, t, (n - 4) * BANK:(n - 3) * BANK], o, ACT.Copy), "a_in", n, t)
                    else:
                        taken(act.activation(a_z[:, t, (n - 8) * BANK:(n - 7) * BANK], o, ACT.Silu), "a_in", n, t)
            high_parts(split_at["a_out", 0, 0] + NPIECE)
            for h in range(RET_H):
                for i in range(NT):
                    u = h * NT + i
                    o = full(act, "ret_o", h, i)
                    if u >= 2:
                        act.wait_ge(z_sq, u - 1)
                    elif u == 0:
                        act.wait_ge(qk_done, 16)
                    act.activation(tmp[:, u % 2, :], o, ACT.Square, accum_out=rstat[:, 0, u:u + 1]).then_inc(z_sq, 1)
            for f in range(RET_K):
                o = full(act, "zT_a", f)
                act.activation(o_hi["a_out"][:, f, :], o, ACT.Copy).then_inc(o_high, 1)
            high_parts(split_at["b_in", 0, 0])

            def from_out(name):
                def ready(t):
                    drained(act, name, 0, t)
                    drained(act, name, 1, t)
                return ready

            stream_squares(1, b_xn, from_out("a_out"))
            for k in range(KD):
                o = full(act, "xT_b", k)
                if k % 2:
                    act.activation(b_kvT[:, k, :], o, ACT.Copy, scale=col("kv_g", k))
                act.activation(x_hi[:, k, :], o, ACT.Copy, scale=col("b_g", k)).then_inc(x_high, 1)
            high_parts(split_at["b_in", 0, 0] + NPIECE)
            act.wait_ge(bias_kept, 16)
            for f in range(RET_K):
                drained(act, "zT_a", f)
            act.dma_start(b_bias, bass.AP(ins["bias_rows"].tensor, P - 1, [[SWA_H * 384 - 1, P], [384, SWA_H], [1, SWA_W]]))\
               .then_inc(bias_loaded, 16)
            for t in range(NT):
                o = full(act, "kv", t)
                taken(act.activation(b_kv[:, t, :], o[:, 0:256], ACT.Copy), "kv", t)

            def hn_square(n):
                key, heads, width = hn_units[n]
                o = full(act, *key)
                if n >= 2:
                    act.wait_ge(hn_ss, n - 1)
                act.activation(sqbuf(n)[:, 0:heads * width], o[:, 0:heads * width], ACT.Square).then_inc(hn_sq, 1)

            act.wait_ge(k_ss, 1)
            for n in range(4):
                high_parts_for("b_in", n, 3)
                for t in range(NT):
                    if n < 2:
                        hn_square(n * NT + t)
                        continue
                    o = full(act, "b_in", n, t)
                    taken(act.activation(b_z[:, t, (n - 2) * BANK:(n - 1) * BANK], o, ACT.Silu), "b_in", n, t)
            high_parts(split_at["b_out", 0, 0] + NPIECE)
            m_, nm_, d_, l_, es_, rl_ = (astat[:, i, :] for i in range(6))
            for n in range(NT + 1):
                if n >= 1:
                    q = n - 1
                    for i in range(1, 8, 2):
                        o = full(act, "swa_pT", q, i)
                        c0 = P if q == 0 else 0
                        dst = b_pT[:, 2 * i * SWA_W:(2 * i + 2) * SWA_W].rearrange("p (m c) -> p m c", m=2)
                        src = o.rearrange("p (m c) -> p m c", m=2)
                        if q >= 1:
                            full(act, "swa_o", q - 1, SWA_KV - 1)
                        taken(act.activation(dst[:, :, c0:SWA_W], src[:, :, c0:SWA_W], ACT.Copy), "swa_pT", q, i)
                if n < NT:
                    w0 = P if n == 0 else 0
                    act.wait_ge(sw_nm, 2 * (n + 1))
                    if n >= 1:
                        act.wait_ge(sw_rl, n)
                    for h in range(SWA_H):
                        s = b_s[n % 2][:, h, w0:SWA_W]
                        act.activation(s, s, ACT.Exp, bias=nm_[:, h:h + 1], accum_out=l_[:, h:h + 1]).then_inc(sw_e, 1)
                    act.activation(es_, d_, ACT.Exp).then_inc(sw_es, 1)
            for k in range(KD):
                o = full(act, "zT_b", k)
                act.activation(o_hi["b_out"][:, k, :], o, ACT.Copy).then_inc(o_high, 1)
            high_parts(split_at["c_in", 0, 0])

            stream_squares(2, c_xn, from_out("b_out"))
            high_parts(split_at["c_in", 0, 0] + NPIECE)
            act.wait_ge(mod_done, 2)
            for k in range(KD):
                o = full(act, "xT_c", k)
                act.activation(x_hi[:, k, :], o, ACT.Identity, scale=modcol[:, 1, k:k + 1],
                               bias=modcol[:, 0, k:k + 1]).then_inc(x_high, 1)
            act.wait_ge(lam_dve, 2)
            act.activation(lam[:, 2:4], lam[:, 0:2], ACT.Exp).then_inc(lam_act, 1)
            for n in range(5):
                if n != 2:
                    high_parts(c_ahead[n])
                for t in range(NT):
                    hn_square(HN_SWA + n * NT + t)
            high_parts(split_at["c_out", 0, 0])
            for t in range(NT):
                o = full(act, "c_in", 5, t)
                taken(act.activation(c_dv[:, t, :], o, ACT.Copy), "c_in", 5, t)
            for n in range(HN_PROJ, HN_PROJ + 8):
                hn_square(n)
            for t in range(NT):
                hn_square(HN_PROJ + 8 + t)
                o = full(act, "v_up", t)
                taken(act.activation(c_v[:, t, :], o, ACT.Copy), "v_up", t)
            high_parts(split_at["c_out", 0, 0] + NPIECE)
            act.wait_ge(padded, 3)
            for h in range(DIFF_H):
                o = full(act, "kdT", h)
                act.activation(c_kdT[0:64, h, 0, :], o[0:64, :], ACT.Copy)
                taken(act.activation(c_kdT[64:128, h, 1, :], o[64:128, :], ACT.Copy), "kdT", h)
            for h in range(MLA_H):
                o = full(act, "knT", h)
                taken(act.activation(c_knT[:, h, :], o, ACT.Copy, scale=col("mk_g")), "knT", h)
            n_units = len(att_units)
            for n in range(n_units + 3):
                if n < n_units:
                    kind, h, i = att_units[n]
                    N = (i + 1) * P
                    for c in range(1 if kind == "m" else 2):
                        sl = (n if kind == "m" else 2 * n + c) % 8
                        act.wait_ge(at_nm, (n if n < 16 else 16 + 2 * (n - 16)) + c + 1)
                        s = c_s[:, sl, 0:N]
                        at = slice(n % 16, n % 16 + 1)
                        act.activation(s, s, ACT.Exp, bias=astat[:, 2 + c, at],
                                       accum_out=astat[:, 4 + c, at]).then_inc(at_p, 1)
                if 2 <= n < n_units + 2:
                    m = n - 2
                    kind, h, i = att_units[m]
                    N = (i + 1) * P
                    o = full(act, "att_pT", m)
                    if m >= 8:
                        full(act, "att_o", m - 8)
                    taken(act.activation(c_pT[:, m % 8, 0:N], o[:, 0:N], ACT.Copy), "att_pT", m)
                if n >= 3:
                    kind, h, i = att_units[n - 3]
                    if kind == "d":
                        u = n - 3 - 16
                        act.wait_ge(od_clamped, u + 1)
                        act.activation(tmp[:, u % 2, 0:P], tmp[:, u % 2, 0:P], ACT.Square, scale=SQ_SCALE,
                                       accum_out=rstat[:, 0, u:u + 1]).then_inc(od_sq, 1)

            act.wait_ge(sub_done, 1)
            for k in range(KD):
                o = full(act, "mT", k)
                if k < 4:
                    act.activation(o_hi["c_out"][:, k, :], o, ACT.Copy).then_inc(o_high, 1)
                else:
                    act.activation(o_hi["c_out"][:, k, :], o, ACT.Copy, scale=lam[:, 6:7]).then_inc(o_high, 1)
            high_parts(split_at["pq", 0, 0])

            stream_squares(3, d_xn, from_out("c_out"))
            high_parts(split_at["pq", 2, 0])
            full(act, "xT_d", KD - 1)
            for k in range(KD):
                drained(act, "xT_d", k)
                act.activation(d_hi[:, k, :], hT[:, k, :], ACT.Copy).then_inc(d_high, 1)
            for f in range(2 * PEER_H + 1):
                if f < 2 * PEER_H:
                    high_parts(split_at["pq", f, 0] + NPIECE)
                    o = full(act, "pqT", f)
                    if f >= 2:
                        full(act, "peer_s", f - 2)
                    taken(act.activation(d_qT[:, f % 2, :], o, ACT.Copy), "pqT", f)
                if f >= 1:
                    g = f - 1
                    o = full(act, "peer_s", g)
                    if g >= 4:
                        act.wait_ge(ranked, g // 2 - 1)
                    act.activation(late_s[:, g, :], o[:, LATE * P:(LATE + 1) * P], ACT.Copy)
                    taken(act.activation(d_s[:, g % 4, :, :].rearrange("p t n -> p (t n)"), o, ACT.Copy), "peer_s", g)
                if f == 2 * PEER_H - 2:
                    for i in range(GATHERED * 2):
                        o = full(act, "h2", i)
                        taken(act.activation(d_h2[:, i // 2, (i % 2) * BANK:(i % 2 + 1) * BANK], o, ACT.Copy), "h2", i)
            for b in range(2):
                drained(act, "peer_s", 2 * PEER_H - 1 - b)
            full(act, "pqT", 2 * PEER_H - 1)
            act.activation(late_keep[:], late_s[:], ACT.Copy).then_inc(late_kept, 1)
            act.activation(wide_iota, iota[:].unsqueeze(2).to_broadcast([P, NKEYS, BATCH]), ACT.Copy)\
               .then_inc(iota_ready, 1)
            act.wait_ge(routed, 1)
            g_flat = r_g[:].rearrange("p t h k -> p (t h k)")
            act.activation(g_flat, g_flat, ACT.Exp).then_inc(route_e, 1)

            def keep_gates(q, m, t0, s):
                act.wait_ge(spread_summed, m + 3)
                act.activation(spread[q % 2][:, :, bass.ds(t0, BATCH)],
                               ps[:, 6 + s, :].rearrange("p (t j) -> p j t", j=QKEYS), ACT.Copy).then_inc(spread_kept, 1)

            act.sem_inc(spread_kept, 2)
            act.sem_inc(dense_gelu, 1)
            with act.Fori(0, QSTEPS // 2) as turn:
                for s in range(2):
                    keep_gates(0, turn * 2 + s, turn * (2 * BATCH) + s * BATCH, s)
            for q in range(QUARTERS):
                if q >= 1:
                    act.wait_ge(dense_coef, q * QSTEPS)
                with act.Fori(0, QSTEPS // 2) as turn:
                    for s in range(2):
                        n = turn * 2 + (q * QSTEPS + s)
                        act.wait_ge(u_done, n + 1)
                        act.wait_ge(v_done, n + 1)
                        act.activation(tmp[:, s, :], ps[:, 4 + s, :], ACT.Gelu).then_inc(dense_gelu, 1)
                        if q + 1 < QUARTERS:
                            keep_gates(q + 1, n + QSTEPS, turn * (2 * BATCH) + s * BATCH, s)
                if q == 1:
                    act.wait_ge(late_done, 1)
                    act.activation(g_kept[:, SLOTS:2 * SLOTS], g_kept[:, SLOTS:2 * SLOTS], ACT.Exp).then_inc(route_e, 1)
                if q % 2 == 0:
                    act.wait_ge(a_ready, q // 2 + 1)
                    if q >= 2:
                        act.wait_ge(out_ready, q // 2)
                    act.activation(r_coef[:], r_a[:], ACT.Gelu).then_inc(gelu_done, 1)

        @block.gpsimd
        def _(pool):
            pool.memset(ones[:], 1.0).then_inc(made, 1)
            pool.memset(minus_half[:], -0.5).then_inc(made, 1)
            pool.wait_ge(made, 2)

            def rsqrt(ss, ms, r, n, width, ms_sem, ms_at, r_sem):
                pool.tensor_scalar(ms, ss, 1.0 / width, EPS, ALU.mult, ALU.add).then_inc(ms_sem, 1)
                pool.wait_ge(ms_sem, ms_at)
                pool.tensor_tensor(r, ms, minus_half[:, 0:n], ALU.pow).then_inc(r_sem, 1)

            def stream_rsqrt(n):
                for t in range(NT):
                    pool.wait_ge(sq_done, NT * n + t + 1)
                    if n >= 1:
                        pool.wait_ge(xn_done, NT * (n - 1) + t + 1)
                    at = slice(t, t + 1)
                    rsqrt(stat[:, 0, at], stat[:, 1, at], stat[:, 2, at], 1, D, ms_done, NT * n + t + 1, rr_done)

            def hn_rsqrt(n):
                key, heads, width = hn_units[n]
                pool.wait_ge(hn_ss, n + 1)
                if n >= 4:
                    drained(pool, *hn_units[n - 4][0])
                s = hstat[:, n % 4, :, 0:heads]
                rsqrt(s[:, 0, :], s[:, 1, :], s[:, 2, :], heads, width, hn_ms, n + 1, hn_r)

            split_n = [0]

            def low_parts(end):
                while split_n[0] < min(end, len(splits)):
                    q = split_n[0]
                    piece = splits[q]
                    n = piece.src.shape[1]
                    at = place[piece.name] % NPIECE * PIECE
                    pool.wait_ge(w_high, q + 1)
                    pool.tensor_tensor(w_lo[q % NPIECE][:, 0:n], ring[:, at:at + n], w_hi[q % NPIECE][:, 0:n],
                                       ALU.subtract).then_inc(w_split, 1)
                    split_n[0] += 1

            stream_rsqrt(0)
            low_parts(split_at["a_out", 0, 0] + NPIECE)
            for u in range(RET_H * NT):
                pool.wait_ge(z_sq, u + 1)
                rsqrt(rstat[:, 0, u:u + 1], rstat[:, 1, u:u + 1], rstat[:, 2, u:u + 1], 1, BANK, z_ms, u + 1, z_r)
            low_parts(split_at["b_in", 0, 0])
            stream_rsqrt(1)
            low_parts(split_at["b_in", 0, 0] + NPIECE)
            pool.wait_ge(k_ss, 1)
            rsqrt(astat[:, 0, 0:8], astat[:, 1, 0:8], astat[:, 2, 0:8], 8, SWA_D, k_ms, 1, k_r)
            for n in range(2):
                low_parts(split_at["b_in", n, 3] + NPIECE)
                for t in range(NT):
                    hn_rsqrt(n * NT + t)
            low_parts(split_at["c_in", 0, 0])
            stream_rsqrt(2)
            for n in range(5):
                if n != 2:
                    low_parts(c_ahead[n])
                for t in range(NT):
                    hn_rsqrt(HN_SWA + n * NT + t)
            low_parts(split_at["c_out", 0, 0])
            for n in range(HN_PROJ, HN_ALL):
                hn_rsqrt(n)
            low_parts(split_at["c_out", 0, 0] + NPIECE)
            for u in range(DIFF_H * NT):
                pool.wait_ge(od_sq, u + 1)
                if u == 0:
                    drained(pool, "ret_o", RET_H - 1, NT - 1)
                pool.tensor_scalar(rstat[:, 1, u:u + 1], rstat[:, 0, u:u + 1], SUM_MAX, SQ_SCALE ** -2 / P,
                                   ALU.min, ALU.mult).then_inc(od_ms, 1)
                pool.wait_ge(od_ms, 2 * u + 1)
                pool.tensor_scalar(rstat[:, 1, u:u + 1], rstat[:, 1, u:u + 1], EPS, None, ALU.add).then_inc(od_ms, 1)
                pool.wait_ge(od_ms, 2 * u + 2)
                pool.tensor_tensor(rstat[:, 2, u:u + 1], rstat[:, 1, u:u + 1], minus_half[:, 0:1], ALU.pow).then_inc(od_r, 1)
            low_parts(split_at["pq", 0, 0])
            stream_rsqrt(3)

            low_parts(split_at["pq", 0, 0] + 6)
            steps_done = 0
            for h in range(PEER_H):
                halves = range(2) if h + 1 < PEER_H else range(1)
                eq = [v.rearrange("p (t k) a -> p t k a", k=TOPK) for v in pick_eq[h % 2]]
                pool.wait_ge(placed, h + 1)
                low_parts(split_at["pq", 2 * h, 0] + 8)
                for a in halves:
                    numbers = early[h % 2].idxf[:, a].unsqueeze(2).to_broadcast([P, NE, TOPK, TOPK])
                    pool.tensor_tensor(eq[a], eq[a], numbers, ALU.mult).then_inc(pick_step, 1)
                width = TOPK // 2
                while width:
                    steps_done += len(halves)
                    pool.wait_ge(pick_step, steps_done)
                    for a in halves:
                        if width > 1:
                            pool.tensor_tensor(eq[a][:, :, :, 0:width], eq[a][:, :, :, 0:width],
                                               eq[a][:, :, :, width:2 * width], ALU.add).then_inc(pick_step, 1)
                        else:
                            pool.tensor_tensor(r_sel[:, a, :, h, :], eq[a][:, :, :, 0], eq[a][:, :, :, 1],
                                               ALU.add).then_inc(picked, 1)
                    width //= 2

            pool.memset(absorb[:], 0.0).then_inc(g_absorb, 1)
            pool.wait_ge(g_absorb, 1)
            for half in range(2):
                pool.sem_inc(g_used[half], GATHER)
            blocks = SLOTS // (2 * GATHER)
            full(pool, "pqT", 2 * PEER_H - 1)
            for t in range(GATHERED):
                pool.wait_ge(gathering, t + 1)
                for phase, table in enumerate((ins["peer_u"], ins["peer_v"])):
                    with pool.Fori(0, blocks) as b:
                        turn = b + (2 * t + phase) * blocks
                        for half in range(2):
                            pool.wait_ge(g_used[half], turn * GATHER + GATHER)
                            at = b * 2 * GATHER + half * GATHER
                            pool.tensor_copy(estage[:, half, :], eidx[:, bass.ds(at + t * SLOTS, GATHER)]).then_inc(g_staged, 1)
                            pool.wait_ge(g_staged, turn * 2 + half + 1)
                            pool.tensor_tensor(absorb[:], absorb[:], absorb[:], ALU.mult).then_inc(g_absorb, 1)
                            for r in range(GATHER):
                                q = half * GATHER + r
                                pool.indirect_dma_start(
                                    experts[:, q, :], None, table,
                                    bass.IndirectOffsetOnAxis(ap=estage[:, half, r:r + 1], axis=0)).then_inc(g_loaded[q], 16)



def _chunks(w, width):
    k, n = w.shape
    return np.ascontiguousarray(
        w.reshape(k // P, P, n // width, width).transpose(2, 1, 0, 3)).reshape(n // width, P, (k // P) * width)


def _colvec(v):
    return np.ascontiguousarray(v.reshape(-1, P).T)


def shape_constants():
    f = np.float32
    c = {"ident": np.eye(P, dtype=f)}
    half = np.arange(P, dtype=f)
    lin = (half / f(P - 1)).astype(f)
    angle = (f(1.0) / np.power(f(10000.0), lin, dtype=f)).astype(f)
    arg = (np.arange(T, dtype=f)[None, :] * angle[:, None]).astype(f)
    c["trig_a"] = np.stack([np.cos(arg), np.sin(arg)], 1).astype(f)
    log_gamma = np.log((1.0 - 2.0 ** (-5.0 - np.arange(RET_H))).astype(f)).astype(f)
    diff = np.arange(T)[None, :] - np.arange(P)[:, None]
    dec = np.exp(np.maximum(diff, 0).astype(f)[:, None, :] * log_gamma[None, :, None]).astype(f)
    c["decay"] = (np.where(diff[:, None, :] >= 0, dec, 0) / 16).astype(f)
    col = np.arange(896)[None, :] - 384
    c["causal"] = np.where(col <= np.arange(P)[:, None], 0.0, NEG).astype(f)
    inv = (f(1.0) / np.power(f(10000.0), (np.arange(HALF, dtype=f) / f(HALF)), dtype=f)).astype(f)
    ang = (np.arange(T, dtype=f)[:, None] * inv[None, :]).astype(f).reshape(NT, P, HALF).transpose(1, 0, 2)
    c["trig"] = np.stack([np.cos(ang), np.sin(ang)], 1).astype(f)
    dist = 255 - np.arange(384)
    inside = (dist >= 0) & (dist < P)
    d = np.clip(dist, 0, P - 1)
    large = 16 + (np.log(np.maximum(d, 1).astype(f) / f(16)) / f(np.log(8.0)) * f(16)).astype(np.int32)
    bucket = np.where(d < 16, d, np.minimum(large, 31))
    c["bias_hot"] = ((np.arange(32)[:, None] == bucket[None, :]) & inside[None, :]).astype(f)
    c["bias_mask"] = np.broadcast_to(np.where(inside, 0.0, NEG).astype(f), (SWA_H, 384)).copy()
    return c


def lay_out(i):
    a = shape_constants()
    a["x"] = np.ascontiguousarray(i["x"].reshape(T, D))
    w = i["a_w_in"][0]
    qk = np.stack([w[:, :D].reshape(D, RET_H, P, 2), w[:, D:2 * D].reshape(D, RET_H, P, 2)], 2)
    qk = qk.transpose(0, 1, 2, 4, 3).reshape(D, 2 * D)
    a["a_w_in"] = _chunks(np.concatenate([qk, w[:, 2 * D:]], 1), BANK)
    wo = i["a_w_out"][0].reshape(2, KD, P, 2, BANK).transpose(3, 0, 2, 1, 4)
    a["a_w_out"] = np.ascontiguousarray(wo).reshape(4, P, KD * BANK)
    a["w_kv"] = _chunks(i["w_kv"], 256)[0]
    wb = i["b_w_in"][0]
    order = [4 * (t // 2) + 2 * half + t % 2 for t in range(8) for half in range(2)]
    q = wb[:, :D].reshape(D, SWA_H, SWA_D)[:, order, :].reshape(D, D)
    a["b_w_in"] = _chunks(np.concatenate([q, wb[:, D:]], 1), BANK)
    a["b_w_out"] = _chunks(i["b_w_out"][0], BANK)
    a["rel_bias"] = np.ascontiguousarray(i["rel_bias"])
    wc = i["w_in_2"][0]
    a["c_in0"] = _chunks(wc[:, :Q_LAT], Q_LAT)[0]
    a["c_in1"] = _chunks(wc[:, Q_LAT:Q_LAT + KV_LAT], KV_LAT)[0]
    a["c_kpe"] = _chunks(wc[:, Q_LAT + KV_LAT:Q_LAT + KV_LAT + ROPE], ROPE)[0]
    a["c_in2"] = _chunks(wc[:, Q_LAT + KV_LAT + ROPE:], BANK)
    wq = i["mla_w_q_up_2"][0].reshape(Q_LAT, MLA_H, NOPE + ROPE)
    a["w_q_up"] = _chunks(np.concatenate([wq[:, :, :NOPE].reshape(Q_LAT, -1), wq[:, :, NOPE:].reshape(Q_LAT, -1)], 1), 768)[0]
    wk = i["mla_w_kv_up_2"][0].reshape(KV_LAT, MLA_H, 2, NOPE)
    a["w_kv_up"] = _chunks(np.ascontiguousarray(wk.transpose(0, 2, 1, 3)).reshape(KV_LAT, 1024), 1024)[0]
    a["c_w_out"] = _chunks(i["w_out_2"][0], BANK)
    wa = i["ada_w_2"][0]
    a["ada_w"] = _chunks(wa, BANK)[ADA_ORDER]
    a["peer_w_q"] = _chunks(i["peer_w_q_2"][0], P)
    a["sub_keys"] = np.ascontiguousarray(i["peer_sub_keys_2"][0].transpose(3, 0, 1, 2)).reshape(P, 2 * PEER_H * NKEYS)
    a["peer_u"] = np.ascontiguousarray(i["peer_u_2"][0])
    u = a["peer_u"].reshape(NKEYS, STEPS, PAIR, KD, P)
    a["u_steps"] = np.ascontiguousarray(u.transpose(1, 4, 2, 3, 0)).reshape(STEPS, P, PAIR * D)
    a["peer_v"] = np.ascontiguousarray(i["peer_v_2"][0])
    two = lambda v: np.concatenate([v.reshape(-1), v.reshape(-1)])
    col = {"a_g": i["a_norm_g"], "kv_g": i["kv_norm_g"], "b_g": i["b_norm_g"], "n1_g": i["norm1_g_2"],
           "n2_g": i["norm2_g_2"], "c": i["c_2"], "ada_b": i["ada_b_2"], "k_g": two(i["k_norm_g"]),
           "q_g": two(i["b_q_norm_g"]), "qlat_g": i["mla_q_lat_g_2"], "kvlat_g": i["mla_kv_lat_g_2"],
           "mq_g": i["mla_q_g_2"][0, :NOPE], "mk_g": i["mla_k_g_2"][0, :NOPE], "sub_g": i["diff_subln_g_2"]}
    a["cols"] = np.ascontiguousarray(np.concatenate([_colvec(np.asarray(col[n])) for n in COLS], 1))
    row = {"sinks": i["b_sinks"], "mq_g": i["mla_q_g_2"][0, NOPE:], "mk_g": i["mla_k_g_2"][0, NOPE:],
           "dq_g": i["diff_q_g_2"], "dk_g": i["diff_k_g_2"], "lq1": i["diff_lq1_2"], "lk1": i["diff_lk1_2"],
           "lq2": i["diff_lq2_2"], "lk2": i["diff_lk2_2"]}
    every = lambda v: np.broadcast_to(v, (P, v.size)).copy()
    a["rows"] = every(np.concatenate([np.asarray(row[n]).reshape(-1) for n in ROWS]))
    a["iota"] = every(np.arange(NKEYS, dtype=np.float32))
    ab = i["ada_b_2"].reshape(6, D)
    a["gate_b"] = every(np.concatenate([ab[2], ab[5]]))
    return {k: np.ascontiguousarray(v) for k, v in a.items()}


def build(nc, arrays):
    ins = {n: nc.dram_tensor(f"in_{n}", v.shape, F32, kind="ExternalInput").ap() for n, v in arrays.items()}
    ins["bias_rows"] = nc.dram_tensor("bias_rows", [P, SWA_H, 384], F32, kind="Internal").ap()
    out = nc.dram_tensor("out", [T, D], F32, kind="ExternalOutput").ap()
    network(nc, ins, out)


def kernel(**inputs):
    import concourse.bacc as bacc
    from concourse.bass_utils import run_bass_kernel_spmd

    inputs = {n: np.asarray(v) for n, v in inputs.items()}
    arrays = lay_out(inputs)
    nc = bacc.Bacc("TRN2", target_bir_lowering=False, num_devices=1)
    build(nc, arrays)
    r = run_bass_kernel_spmd(nc, [{f"in_{n}": v for n, v in arrays.items()}], core_ids=[0])
    return r.results[0]["out"].reshape(1, T, D)
```
